# Optimizing a Trainium2 kernel written in Bass

```python
import functools
import jax, jax.numpy as jnp
from jax import lax
import numpy as np

D_MODEL = 1024
BATCH = 1
SEQ = 1024
DEPTH = 1
DEC_BATCH = 8
DEC_SEQ = 8
PAST_LEN = 1024
PAGE_SIZE = 128

MIX_WIDTH = D_MODEL
LRU_WIDTH = MIX_WIDTH // 2
LRU_BLOCKS = 8
LRU_BLOCK = LRU_WIDTH // LRU_BLOCKS
CONV_WIDTH = 4
LRU_C = 8.0
ATTN_HEADS = 8
HEAD_DIM = (MIX_WIDTH - LRU_WIDTH) // ATTN_HEADS
KV_HEADS = 2
GROUP = ATTN_HEADS // KV_HEADS
WINDOW = 128
ROPE_THETA = 10000.0
N_MEM = 256
X_HEADS = 4
X_HEAD_DIM = D_MODEL // X_HEADS
D_FF = 2816
EPS = 1e-6
Q_WIDTH = ATTN_HEADS * HEAD_DIM
KV_WIDTH = KV_HEADS * HEAD_DIM
IN_COLS = 2 * LRU_WIDTH + Q_WIDTH + 2 * KV_WIDTH

kernel_name = 'hymba_rglru_swa_macaron_memxattn_step'

def rmsnorm(x, g):
    xf = x.astype(jnp.float32)
    y = xf * lax.rsqrt(jnp.mean(xf * xf, axis=-1, keepdims=True) + EPS)
    return (y * g.astype(jnp.float32)).astype(x.dtype)

def swiglu(x, w_gate, w_up, w_down):
    return (jax.nn.silu(x @ w_gate) * (x @ w_up)) @ w_down

def rope(z, pos):
    half = HEAD_DIM // 2
    inv = ROPE_THETA ** (-jnp.arange(half, dtype=jnp.float32) / half)
    ang = pos.astype(jnp.float32)[:, None] * inv[None, :]
    cos = jnp.cos(ang)[:, None, :]
    sin = jnp.sin(ang)[:, None, :]
    z1 = z[..., :half].astype(jnp.float32)
    z2 = z[..., half:].astype(jnp.float32)
    return jnp.concatenate([z1 * cos - z2 * sin, z2 * cos + z1 * sin], axis=-1).astype(z.dtype)

def sink_softmax(s, mask, sink):
    s = jnp.where(mask, s, -jnp.inf)
    sk = jnp.broadcast_to(sink.astype(jnp.float32), s.shape[:-1] + (1,))
    p = jax.nn.softmax(jnp.concatenate([s, sk], axis=-1), axis=-1)
    return p[..., :-1]

def lru_combine(left, right):
    a1, b1 = left
    a2, b2 = right
    return a1 * a2, a2 * b1 + b2

def rg_lru(u, conv_buf, h0, conv_w, conv_b, w_a, b_a, w_i, b_i, lam):
    n, t = u.shape[:2]
    xc = jnp.concatenate([conv_buf.astype(u.dtype), u], axis=1)
    conv = conv_b
    for j in range(CONV_WIDTH):
        conv = conv + xc[:, j:j + t] * conv_w[j]
    new_buf = xc[:, -(CONV_WIDTH - 1):]
    xb = conv.reshape(n, t, LRU_BLOCKS, LRU_BLOCK)
    r = jax.nn.sigmoid(jnp.einsum('ntgi,gij->ntgj', xb, w_a).reshape(n, t, LRU_WIDTH) + b_a)
    gi = jax.nn.sigmoid(jnp.einsum('ntgi,gij->ntgj', xb, w_i).reshape(n, t, LRU_WIDTH) + b_i)
    log_a = -LRU_C * r.astype(jnp.float32) * jax.nn.softplus(-lam.astype(jnp.float32))
    a = jnp.exp(log_a)
    b = jnp.sqrt(-jnp.expm1(2.0 * log_a)) * (gi * conv).astype(jnp.float32)
    b = b.at[:, 0].add(a[:, 0] * h0.astype(jnp.float32))
    _, h = lax.associative_scan(lru_combine, (a, b), axis=1)
    return h, h[:, -1], new_buf

def swa_prompt(q, k, v, sink):
    n, t = q.shape[:2]
    nb = t // WINDOW
    qb = q.reshape(n, nb, WINDOW, KV_HEADS, GROUP, HEAD_DIM)

    def band(z):
        zb = z.reshape(n, nb, WINDOW, KV_HEADS, HEAD_DIM)
        prev = jnp.concatenate([jnp.zeros_like(zb[:, :1]), zb[:, :-1]], axis=1)
        return jnp.concatenate([prev, zb], axis=2)

    kk, vv = band(k), band(v)
    s = jnp.einsum('nbqkgd,nbskd->nbkgqs', qb, kk, preferred_element_type=jnp.float32) * (HEAD_DIM ** -0.5)
    i = jnp.arange(WINDOW)[:, None]
    j = jnp.arange(2 * WINDOW)[None, :]
    dist = i + WINDOW - j
    within = (dist >= 0) & (dist < WINDOW)
    blk = jnp.arange(nb)[:, None, None]
    mask = within[None] & ((blk > 0) | (j[None] >= WINDOW))
    p = sink_softmax(s, mask[None, :, None, None], sink.reshape(KV_HEADS, GROUP)[None, None, :, :, None, None])
    o = jnp.einsum('nbkgqs,nbskd->nbqkgd', p.astype(vv.dtype), vv).reshape(n, t, Q_WIDTH)
    return o, k[:, -WINDOW:], v[:, -WINDOW:]

def swa_sample(q, k, v, sink, buf_k, buf_v):
    n, s_len = q.shape[:2]
    kk = jnp.concatenate([buf_k.astype(k.dtype), k], axis=1)
    vv = jnp.concatenate([buf_v.astype(v.dtype), v], axis=1)
    qp = PAST_LEN + jnp.arange(s_len, dtype=jnp.int32)
    kp = jnp.concatenate([PAST_LEN - WINDOW + jnp.arange(WINDOW, dtype=jnp.int32), qp])
    dist = qp[:, None] - kp[None, :]
    mask = (dist >= 0) & (dist < WINDOW) & (kp[None, :] >= 0)
    qg = q.reshape(n, s_len, KV_HEADS, GROUP, HEAD_DIM)
    s = jnp.einsum('nqkgd,nskd->nkgqs', qg, kk, preferred_element_type=jnp.float32) * (HEAD_DIM ** -0.5)
    p = sink_softmax(s, mask, sink.reshape(KV_HEADS, GROUP)[None, :, :, None, None])
    o = jnp.einsum('nkgqs,nskd->nqkgd', p.astype(vv.dtype), vv).reshape(n, s_len, Q_WIDTH)
    return o, kk[:, -WINDOW:], vv[:, -WINDOW:]

def memory_kv(mem, g_mem, w_ck, w_cv):
    n, m = mem.shape[:2]
    mm = rmsnorm(mem, g_mem)
    mk = (mm @ w_ck).reshape(n, m, X_HEADS, X_HEAD_DIM)
    mv = (mm @ w_cv).reshape(n, m, X_HEADS, X_HEAD_DIM)
    return mk, mv

def cross_attend(h, mk, mv, w_cq, w_co):
    n, t = h.shape[:2]
    q = (h @ w_cq).reshape(n, t, X_HEADS, X_HEAD_DIM)
    s = jnp.einsum('nthd,nmhd->nhtm', q, mk.astype(q.dtype), preferred_element_type=jnp.float32) * (X_HEAD_DIM ** -0.5)
    p = jax.nn.softmax(s, axis=-1).astype(mv.dtype)
    o = jnp.einsum('nhtm,nmhd->nthd', p, mv).reshape(n, t, D_MODEL).astype(h.dtype)
    return o @ w_co

def trunk_layer(x, pos, mk, mv, conv_buf, h0, attend, p):
    x = x + 0.5 * swiglu(rmsnorm(x, p['g_ffn1']), p['w1_gate'], p['w1_up'], p['w1_down'])
    h = rmsnorm(x, p['g_mix'])
    n, t = h.shape[:2]
    proj = h @ p['w_in']
    o1 = LRU_WIDTH
    o2 = 2 * LRU_WIDTH
    o3 = o2 + Q_WIDTH
    o4 = o3 + KV_WIDTH
    u, gate = proj[..., :o1], proj[..., o1:o2]
    q = rope(proj[..., o2:o3].reshape(n, t, ATTN_HEADS, HEAD_DIM), pos)
    k = rope(proj[..., o3:o4].reshape(n, t, KV_HEADS, HEAD_DIM), pos)
    v = proj[..., o4:].reshape(n, t, KV_HEADS, HEAD_DIM)
    hl, h_last, new_conv = rg_lru(u, conv_buf, h0, p['conv_w'], p['conv_b'], p['w_a'], p['b_a'], p['w_i'], p['b_i'], p['lam'])
    lru_out = rmsnorm(hl.astype(x.dtype) * jax.nn.gelu(gate), p['g_lru_out'])
    attn_o, new_k, new_v = attend(q, k, v, p['sink'])
    attn_out = rmsnorm(attn_o.astype(x.dtype), p['g_attn_out'])
    x = x + jnp.concatenate([lru_out, attn_out], axis=-1) @ p['w_out']
    x = x + cross_attend(rmsnorm(x, p['g_xattn']), mk, mv, p['w_cq'], p['w_co'])
    x = x + 0.5 * swiglu(rmsnorm(x, p['g_ffn2']), p['w2_gate'], p['w2_up'], p['w2_down'])
    return x, new_k, new_v, new_conv, h_last.astype(x.dtype)

def setup_inputs(seed: int = 0) -> dict:
    key = jax.random.key(seed)
    ks = iter(list(jax.random.split(key, 48)))

    def nrm(shape, scale):
        return jax.random.normal(next(ks), shape, jnp.float32) * scale

    def gain(shape):
        return 1.0 + nrm(shape, 0.05)

    L = DEPTH
    D = D_MODEL
    u = jax.random.uniform(next(ks), (L, LRU_WIDTH), jnp.float32, minval=0.9, maxval=0.999)
    a0 = u ** (1.0 / LRU_C)
    lam = jnp.log(a0) - jnp.log1p(-a0)
    return {
        'x_prompt': nrm((BATCH, SEQ, D), 1.0),
        'x_sample': nrm((DEC_BATCH, DEC_SEQ, D), 1.0),
        'mem_prompt': nrm((BATCH, N_MEM, D), 1.0),
        'cache_mem_k': nrm((L, DEC_BATCH, N_MEM, X_HEADS, X_HEAD_DIM), 1.0),
        'cache_mem_v': nrm((L, DEC_BATCH, N_MEM, X_HEADS, X_HEAD_DIM), 1.0),
        'cache_swa_k': nrm((L, DEC_BATCH, WINDOW, KV_HEADS, HEAD_DIM), 1.0),
        'cache_swa_v': nrm((L, DEC_BATCH, WINDOW, KV_HEADS, HEAD_DIM), 1.0),
        'state_conv': nrm((L, DEC_BATCH, CONV_WIDTH - 1, LRU_WIDTH), 1.0),
        'state_lru_h': nrm((L, DEC_BATCH, LRU_WIDTH), 0.5),
        'g_ffn1': gain((L, D)),
        'w1_gate': nrm((L, D, D_FF), D ** -0.5),
        'w1_up': nrm((L, D, D_FF), D ** -0.5),
        'w1_down': nrm((L, D_FF, D), D_FF ** -0.5),
        'g_mix': gain((L, D)),
        'w_in': nrm((L, D, IN_COLS), D ** -0.5),
        'conv_w': nrm((L, CONV_WIDTH, LRU_WIDTH), CONV_WIDTH ** -0.5),
        'conv_b': nrm((L, LRU_WIDTH), 0.02),
        'w_a': nrm((L, LRU_BLOCKS, LRU_BLOCK, LRU_BLOCK), LRU_BLOCK ** -0.5),
        'b_a': nrm((L, LRU_WIDTH), 0.02),
        'w_i': nrm((L, LRU_BLOCKS, LRU_BLOCK, LRU_BLOCK), LRU_BLOCK ** -0.5),
        'b_i': nrm((L, LRU_WIDTH), 0.02),
        'lam': lam,
        'sink': nrm((L, ATTN_HEADS), 0.5),
        'g_lru_out': gain((L, LRU_WIDTH)),
        'g_attn_out': gain((L, Q_WIDTH)),
        'w_out': nrm((L, MIX_WIDTH, D), MIX_WIDTH ** -0.5),
        'g_xattn': gain((L, D)),
        'g_mem': gain((L, D)),
        'w_cq': nrm((L, D, D), D ** -0.5),
        'w_ck': nrm((L, D, D), D ** -0.5),
        'w_cv': nrm((L, D, D), D ** -0.5),
        'w_co': nrm((L, D, D), D ** -0.5),
        'g_ffn2': gain((L, D)),
        'w2_gate': nrm((L, D, D_FF), D ** -0.5),
        'w2_up': nrm((L, D, D_FF), D ** -0.5),
        'w2_down': nrm((L, D_FF, D), D_FF ** -0.5),
        'g_final': gain((D,)),
    }

def reference(x_prompt, x_sample, mem_prompt, cache_mem_k, cache_mem_v, cache_swa_k, cache_swa_v, state_conv, state_lru_h,
              g_ffn1, w1_gate, w1_up, w1_down, g_mix, w_in, conv_w, conv_b, w_a, b_a, w_i, b_i, lam, sink,
              g_lru_out, g_attn_out, w_out, g_xattn, g_mem, w_cq, w_ck, w_cv, w_co, g_ffn2, w2_gate, w2_up, w2_down, g_final):
    pos_p = jnp.arange(x_prompt.shape[1], dtype=jnp.int32)
    pos_s = PAST_LEN + jnp.arange(x_sample.shape[1], dtype=jnp.int32)
    xp, xs = x_prompt, x_sample
    nbp = x_prompt.shape[0]
    mkp_l, mvp_l, kp_l, vp_l, cp_l, hp_l = [], [], [], [], [], []
    ks_l, vs_l, cs_l, hs_l = [], [], [], []
    for l in range(DEPTH):
        p = {
            'g_ffn1': g_ffn1[l], 'w1_gate': w1_gate[l], 'w1_up': w1_up[l], 'w1_down': w1_down[l],
            'g_mix': g_mix[l], 'w_in': w_in[l], 'conv_w': conv_w[l], 'conv_b': conv_b[l],
            'w_a': w_a[l], 'b_a': b_a[l], 'w_i': w_i[l], 'b_i': b_i[l], 'lam': lam[l], 'sink': sink[l],
            'g_lru_out': g_lru_out[l], 'g_attn_out': g_attn_out[l], 'w_out': w_out[l],
            'g_xattn': g_xattn[l], 'w_cq': w_cq[l], 'w_co': w_co[l],
            'g_ffn2': g_ffn2[l], 'w2_gate': w2_gate[l], 'w2_up': w2_up[l], 'w2_down': w2_down[l],
        }
        mk_p, mv_p = memory_kv(mem_prompt, g_mem[l], w_ck[l], w_cv[l])
        conv0 = jnp.zeros((nbp, CONV_WIDTH - 1, LRU_WIDTH), xp.dtype)
        h0 = jnp.zeros((nbp, LRU_WIDTH), jnp.float32)
        xp, kp_, vp_, cp_, hp_ = trunk_layer(xp, pos_p, mk_p, mv_p, conv0, h0, swa_prompt, p)
        attend_s = functools.partial(swa_sample, buf_k=cache_swa_k[l], buf_v=cache_swa_v[l])
        xs, ks_, vs_, cs_, hs_ = trunk_layer(xs, pos_s, cache_mem_k[l], cache_mem_v[l], state_conv[l], state_lru_h[l], attend_s, p)
        mkp_l.append(mk_p)
        mvp_l.append(mv_p)
        kp_l.append(kp_)
        vp_l.append(vp_)
        cp_l.append(cp_)
        hp_l.append(hp_)
        ks_l.append(ks_)
        vs_l.append(vs_)
        cs_l.append(cs_)
        hs_l.append(hs_)
    y_prompt = rmsnorm(xp, g_final)
    y_sample = rmsnorm(xs, g_final)
    return (y_prompt, y_sample,
            jnp.stack(mkp_l), jnp.stack(mvp_l),
            jnp.stack(kp_l), jnp.stack(vp_l), jnp.stack(cp_l), jnp.stack(hp_l),
            jnp.stack(ks_l), jnp.stack(vs_l), jnp.stack(cs_l), jnp.stack(hs_l))


_drawn_inputs = setup_inputs


def setup_inputs(seed=0):
    import zlib

    import numpy as np

    out = dict(_drawn_inputs(seed))
    spreads = {}
    factors = {'b_a': 8.0, 'b_i': 8.0, 'sink': 7.212, 'g_xattn': 8.0, 'g_ffn2': 3.756}
    for name, (base, spread) in spreads.items():
        noise = np.random.default_rng([zlib.crc32(name.encode()), seed]).standard_normal(out[name].shape)
        drawn = base * np.exp(spread * noise) if base else spread * noise
        out[name] = __import__('jax').numpy.asarray(drawn.astype(out[name].dtype))
    for name, factor in factors.items():
        out[name] = (out[name] * factor).astype(out[name].dtype)
    return out
```

```python
from contextlib import ExitStack

import numpy as np
import concourse.bass as bass
from concourse import mybir

F32 = mybir.dt.float32
F32R = mybir.dt.float32r
ALU = mybir.AluOpType
ACT = mybir.ActivationFunctionType
AX_X = mybir.AxisListType.X

P = 128
D = 1024
KT = D // P
SEQ = 1024
NS, LS = 8, 8
TS = NS * LS
T = TS + SEQ
FF = 2816
FT = FF // P
FI = FT // 2
LRU = 512
LT = LRU // P
HD = 64
NH = 8
WIN = 128
NB = SEQ // WIN
KVH = 2
GRP = NH // KVH
NM = 256
XH = 4
XD = D // XH
EPS = 1e-6
IN_T = (2 * LRU + NH * HD + 2 * KVH * HD) // P
NEG = -1.0e30
CH = [(0, 364), (364, 362), (726, 362)]
NC = len(CH)
M_U, M_G, M_Q, M_K, M_V = 0, 4, 8, 12, 13

DOWN_BANKS = (6, 7, 0, 3, 1, 4, 2, 5)

COLS = {}
_n = 0
for _name, _w in [("g_ffn1", KT), ("g_mix", KT), ("g_xattn", KT), ("g_ffn2", KT), ("g_mem", KT), ("g_final", KT),
                  ("g_lru_out", LT), ("g_attn_out", LT), ("conv_w", 4 * LT), ("conv_b", LT), ("b_a", LT),
                  ("b_i", LT), ("lam", LT), ("sink", NH), ("sink_s", 4), ("h0", LT * NS), ("hist", LT * NS * 3)]:
    COLS[_name] = (_n, _w)
    _n += _w
NCST = _n
SM_CP, SM_CS, SM_HP, SM_HS = 0, LT * 3, LT * 3 + LT * NS * 3, LT * 3 + LT * NS * 3 + LT
NSM = SM_HS + LT * NS
PAIR_IN, PAIR_KV, PAIR_OUT, PAIR_CQ, PAIR_CO, PAIRS = 0, 7, 15, 19, 23, 27
GROUPS = [(PAIR_IN, PAIR_KV, 0, NC), (PAIR_KV, PAIR_OUT, 7 * NC, 1), (PAIR_OUT, PAIRS, 7 * NC + 8, NC)]
NORMS = ("ffn1", "mix", "lru", "mem", "attn", "xattn", "ffn2", "final")
_TILES = {"lru": LT, "mem": 1, "attn": LT}
SQ0 = {k: sum(_TILES.get(j, KT) for j in NORMS[:n]) for n, k in enumerate(NORMS)}
SUM0 = {k: sum(1 if j == "mem" else NC for j in NORMS[:n]) for n, k in enumerate(NORMS)}
SPLIT0 = {k: n * NC * KT for n, k in enumerate(("ffn1", "mix", "cat", "xattn", "co", "ffn2"))}


def groups_before(pair):
    return max(base + (min(pair, b) - a) * each for a, b, base, each in GROUPS if pair > a) if pair else 0


class Steps:

    def __init__(self, eng, sem, base=0):
        self.eng, self.sem, self.base, self.n = eng, sem, base, 0

    def mark(self, ins):
        self.n += 1
        ins.then_inc(self.sem, 1)
        return self.base + self.n

    def done(self, ins):
        self.eng.wait_ge(self.sem, self.mark(ins))


def build(nc, t_in, t_out):
    ctx = ExitStack()
    with ctx:
        def sem(name):
            return ctx.enter_context(nc.semaphore(name))

        START = 16512
        LIMIT = 229344

        def at(name, shape, off, dt=F32):
            size = 4 * int(np.prod(shape[1:]))
            assert off % 32 == 0 and off + size <= LIMIT, (name, off, size)
            return nc.alloc_sbuf_tensor_at(name, shape, dt, offset=off)

        ROW = 4 * T
        X0 = START
        A0 = X0 + KT * ROW
        RS0 = A0 + 2 * KT * ROW
        W0 = RS0 + ROW
        C0 = W0 + 6 * 4096
        P0 = C0 + 928 + 512 + 576
        x = at("x", [P, KT, T], X0)
        act_hi = at("act_hi", [P, KT, T], A0, F32R)
        act_lo = at("act_lo", [P, KT, T], A0 + KT * ROW, F32R)
        rstd = at("rstd", [P, T], RS0)
        w_raw = [at(f"w_raw{s}", [P, KT, P], W0 + s * 4096) for s in range(2)]
        w_hi = [at(f"w_hi{s}", [P, KT, P], W0 + 8192 + s * 4096, F32R) for s in range(2)]
        w_lo = [at(f"w_lo{s}", [P, KT, P], W0 + 16384 + s * 4096, F32R) for s in range(2)]
        assert NCST * 4 <= 928 and NSM * 4 <= 576
        cst = at("cst", [P, NCST], C0)
        ones = at("ones", [P, P], C0 + 928)
        small = at("small", [P, NSM], C0 + 1440)
        ACC0 = P0 + 68608
        lrup = at("lrup", [P, 8, LT], ACC0 + 2 * ROW)
        acc = at("acc", [P, T], ACC0)
        sq = at("sq", [P, T], ACC0 + ROW)
        ff_raw_up = at("ff_raw_up", [P, KT, P], P0)
        ff_raw_down = at("ff_raw_down", [P, KT, P], P0 + 4096)
        up_hi = [at(f"up_hi{s}", [P, KT, P], P0 + 8192 + s * 4096, F32R) for s in range(2)]
        up_lo = [at(f"up_lo{s}", [P, KT, P], P0 + 16384 + s * 4096, F32R) for s in range(2)]
        dn_hi = [at(f"dn_hi{s}", [P, KT, P], P0 + 24576 + s * 4096, F32R) for s in range(2)]
        dn_lo = [at(f"dn_lo{s}", [P, KT, P], P0 + 32768 + s * 4096, F32R) for s in range(2)]
        hid_hi = [at(f"hid_hi{s}", [P, T], P0 + 40960 + s * ROW, F32R) for s in range(2)]
        hid_lo = [at(f"hid_lo{s}", [P, T], P0 + 40960 + (2 + s) * ROW, F32R) for s in range(2)]
        gate_t = at("gate_t", [P, T], P0 + 40960 + 4 * ROW)
        hid_t = at("hid_t", [P, T], P0 + 40960 + 5 * ROW)
        mix = at("mix", [P, IN_T, T], P0)
        t_conv = at("t_conv", [P, T], P0 + IN_T * ROW)
        t_a = at("t_a", [P, T], P0 + (IN_T + 1) * ROW)
        t_b = at("t_b", [P, T], P0 + (IN_T + 2) * ROW)
        bd = at("bd", [P, LT, 2, P], P0 + M_V * ROW)
        mem_kT = at("mem_kT", [P, KT, NM], P0 + M_G * ROW)
        mem_v = at("mem_v", [P, 2, D], P0 + M_G * ROW + 8192)
        mem_raw = at("mem_raw", [P, KT, NM], P0 + M_G * ROW + 8192)

        cur = [A0]

        def here(name, shape, dt=F32):
            tns = at(name, shape, cur[0], dt)
            cur[0] += -(-4 * int(np.prod(shape[1:])) // 32) * 32
            assert cur[0] <= RS0, name
            return tns

        rope_cos = here("rope_cos", [P, T])
        rope_sin = here("rope_sin", [P, T])
        masks = here("masks", [P, 2, 2 * WIN])
        ident = here("ident", [P, P])
        rotm = here("rotm", [P, P])
        s_m = [here(f"s_m{s}", [P, NH, 2 * WIN]) for s in range(2)]
        p_T = here("p_T", [P, 2, NH, WIN])
        q_r = here("q_r", [P, GRP, WIN])
        k_r = [here(f"k_r{s}", [P, WIN]) for s in range(2)]
        v_b = here("v_b", [P, WIN])
        v_n = [here(f"v_n{s}", [P, KVH * HD]) for s in range(2)]
        rot_q = here("rot_q", [P, GRP, WIN])
        rot_k = here("rot_k", [P, WIN])
        st8 = here("st8", [P, 8, NH])
        memn_hi = here("memn_hi", [P, KT, NM], F32R)
        memn_lo = here("memn_lo", [P, KT, NM], F32R)
        SA0 = P0 + IN_T * ROW
        kc_T = at("kc_T", [P, NS, WIN], SA0)
        v_c = at("v_c", [P, NS, KVH * HD], SA0 + 4096)
        qs_r = at("qs_r", [P, NS, GRP, LS], SA0 + 8192)
        ks_r = at("ks_r", [P, TS], SA0 + 9216)
        mask_s = at("mask_s", [P, WIN + LS], SA0 + 9472)
        SM0 = A0 + 2 * ROW + 2048 + 1024
        ss_m = at("ss_m", [P, 4, WIN + LS], SM0)
        pcs_T = at("pcs_T", [P, 4, P], SM0 + 2208)
        pns_T = at("pns_T", [LS, 4, P], SM0 + 2208 + 2048)
        vs_n = at("vs_n", [LS, NS, KVH * HD], SM0 + 8192)

        xq = at("xq", [P, KT, T], P0 + 33792)
        cur[0] = A0
        x_id = here("x_id", [P, P])
        xq_b = here("xq_b", [P, KT, P])
        xs_m = [here(f"xs_m{s}", [P, XH, NM]) for s in range(2)]
        xp_T = here("xp_T", [P, 2, XH, P])
        xst = here("xst", [P, 2, 4, XH])
        qs_b = here("qs_b", [P, KT, 32])
        ys_m = [here(f"ys_m{s}", [P, NM]) for s in range(2)]
        yp_T = here("yp_T", [P, 2, P])
        yst = here("yst", [P, 8])
        ck_T = [here(f"ck_T{s}", [P, KT, NM]) for s in range(2)]
        cv_n = [here(f"cv_n{s}", [P, 2, D]) for s in range(2)]

        y = at("y", [P, KT, T], P0)
        ps = ctx.enter_context(nc.psum_tensor("ps", [P, 8, 512], F32))

        def c_(name, j=0, n=1):
            o, w = COLS[name]
            return cst[:, o + j:o + j + n]

        def cd(name, j):
            return cst[:, bass.ds(j + COLS[name][0], 1)]

        cst_in = sem("cst_in")
        bd_in = sem("bd_in")
        x_in = [sem(f"x_in{c}") for c in range(NC)]
        ones_set = sem("ones_set")
        dve_own = sem("dve_own")
        act_own = sem("act_own")
        act_hi_done, act_lo_done = sem("act_hi_done"), sem("act_lo_done")
        memn_hi_done, memn_lo_done = sem("memn_hi_done"), sem("memn_lo_done")
        sq_done, sq_used = sem("sq_done"), sem("sq_used")
        ssq_mm, ssq_ev = sem("ssq_mm"), sem("ssq_ev")
        rms_done, rstd_done = sem("rms_done"), sem("rstd_done")

        def ffn_sems(tag):
            names = ("gu_in", "dn_in", "gu_split", "dn_split", "pool_own", "pool_dn", "gate_mm", "up_mm",
                     "gate_ev", "up_ev", "silu", "hid_f", "hid_hi", "hid_lo", "dn_mm", "dn_ev")
            return {n: sem(f"{tag}_{n}") for n in names}

        ffn = {"ffn1": ffn_sems("ffn1"), "ffn2": ffn_sems("ffn2")}
        w_in = [sem(f"w_in{s}") for s in range(2)]
        w_split = [sem(f"w_split{s}") for s in range(2)]
        w_mm = [sem(f"w_mm{s}") for s in range(2)]
        w_pool = sem("w_pool")
        STAGES = ("in", "out", "cq", "co")
        g_ev = {k: sem(f"{k}_ev") for k in STAGES}
        conv_done = sem("conv_done")
        conv_back = sem("conv_back")
        gate_gelu = sem("gate_gelu")
        lru_sp = sem("lru_sp")
        lru_mm = sem("lru_mm")
        lru_ev = sem("lru_ev")
        lru_r = sem("lru_r")
        lru_th = sem("lru_th")
        lru_a = sem("lru_a")
        lru_q = sem("lru_q")
        lru_s = sem("lru_s")
        lru_y = sem("lru_y")
        lru_normed = sem("lru_normed")
        swa_tab = sem("swa_tab")
        rope_tab = sem("rope_tab")
        rot_mm, rope_done = sem("rot_mm"), sem("rope_done")
        sc_mm, sc_taken, nmax_done, exp_done, p_done = (
            sem("sc_mm"), sem("sc_taken"), sem("nmax_done"), sem("exp_done"), sem("p_done"))
        pt_mm, pt_ev = sem("pt_mm"), sem("pt_ev")
        vt_mm, vt_ev = sem("vt_mm"), sem("vt_ev")
        pv_mm, o_ev = sem("pv_mm"), sem("o_ev")
        kv_ev = sem("kv_ev")
        swa_own = sem("swa_own")
        mem_in = sem("mem_in")
        kvc_in = sem("kvc_in")
        s_rot_mm, s_rope, s_sc_mm, s_nmax, s_exp, s_p = (
            sem("s_rot_mm"), sem("s_rope"), sem("s_sc_mm"), sem("s_nmax"), sem("s_exp"), sem("s_p"))
        s_pt_mm, s_pt_ev, s_pv_mm, s_o_ev = sem("s_pt_mm"), sem("s_pt_ev"), sem("s_pv_mm"), sem("s_o_ev")
        x_tab = sem("x_tab")
        ckv_in = [sem(f"ckv_in{s}") for s in range(2)]
        xq_st, x_sc_mm, x_nmax, x_exp, x_p = sem("xq_st"), sem("x_sc_mm"), sem("x_nmax"), sem("x_exp"), sem("x_p")
        x_pt_mm, x_pt_ev, x_pv_mm, x_o_ev, x_own = (
            sem("x_pt_mm"), sem("x_pt_ev"), sem("x_pv_mm"), sem("x_o_ev"), sem("x_own"))
        y_done = sem("y_done")
        stored = sem("stored")

        block = ctx.enter_context(nc.Block())

        def pair_src(s, p):
            return t_in["w_plain"][s, p, :, :, :]


        @block.sync
        def _(sp):
            def load_gu(f, w, t, first=False):
                if not first:
                    sp.wait_ge(f["gu_split"], t)
                sp.dma_start(w_raw[0][:, :, :], w[t, 0, :, :, :]).then_inc(f["gu_in"], 16)
                sp.dma_start(ff_raw_up[:, :, :], w[t, 1, :, :, :]).then_inc(f["gu_in"], 16)

            def load_down(f, w, j, first=False):
                if not first:
                    sp.wait_ge(f["dn_split"], j)
                sp.dma_start(w_raw[1][:, :, :], w[j * 2, 2, :, :, :]).then_inc(f["dn_in"], 16)
                sp.dma_start(ff_raw_down[:, :, :], w[j * 2 + 1, 2, :, :, :]).then_inc(f["dn_in"], 16)

            def load_ffn(f, w):
                load_gu(f, w, 1)
                load_down(f, w, 0, first=True)
                load_gu(f, w, 2)
                load_gu(f, w, 3)
                with sp.Fori(1, FI - 1) as i:
                    load_gu(f, w, i * 2 + 2)
                    load_down(f, w, i)
                    load_gu(f, w, i * 2 + 3)
                load_down(f, w, FI - 1)

            def load_pairs(a, b):
                with sp.Fori(a, b) as p:
                    for s in range(2):
                        sp.wait_ge(w_split[s], p)
                        sp.dma_start(w_raw[s][:, :, :], pair_src(s, p)).then_inc(w_in[s], 16)

            f = ffn["ffn1"]
            sp.dma_start(cst[:, :], t_in["cst"]).then_inc(cst_in, 16)
            for c, (o, n) in enumerate(CH):
                sp.dma_start(x[:, :, o:o + n], t_in["x"][:, :, o:o + n]).then_inc(x_in[c], 16)
                if c == 0:
                    load_gu(f, t_in["w_ffn1"], 0, first=True)
            load_ffn(f, t_in["w_ffn1"])

            sp.wait_ge(f["gu_split"], FT)
            sp.dma_start(w_raw[0][:, :, :], pair_src(0, 0)).then_inc(w_in[0], 16)
            sp.wait_ge(f["dn_split"], FI)
            sp.dma_start(w_raw[1][:, :, :], pair_src(1, 0)).then_inc(w_in[1], 16)
            sp.wait_ge(g_ev["in"], 6 + 3)
            sp.dma_start(bd[:, :, :, :], t_in["bd"]).then_inc(bd_in, 16)
            load_pairs(1, PAIR_KV + 1)
            sp.wait_ge(w_mm[1], groups_before(PAIR_KV))
            for dst, src in ((rotm, "rotm"), (rope_cos, "cos"), (rope_sin, "sin"), (ident, "ident")):
                sp.dma_start(dst[:, :], t_in[src]).then_inc(rope_tab, 16)
            sp.dma_start(masks[:, :, :], t_in["masks"]).then_inc(swa_tab, 16)
            sp.wait_ge(lru_y, LT)
            sp.dma_start(mem_raw[:, :, :], t_in["mem"]).then_inc(mem_in, 16)
            sp.wait_ge(ssq_mm, SUM0["mem"] + 1)
            sp.dma_start(kc_T[:, :, :], t_in["kc"]).then_inc(kvc_in, 16)
            sp.dma_start(v_c[:, :, :], t_in["vc"]).then_inc(kvc_in, 16)
            sp.dma_start(mask_s[:, :], t_in["mask_s"]).then_inc(kvc_in, 16)
            load_pairs(PAIR_KV + 1, PAIR_CO)
            sp.wait_ge(w_mm[1], groups_before(PAIR_CO))
            sp.dma_start(x_id[:, :], t_in["ident"]).then_inc(x_tab, 16)

            def load_cache(b, s):
                sp.dma_start(ck_T[s][:, :, :], t_in["ck"][b, :, :, :]).then_inc(ckv_in[s], 16)
                sp.dma_start(cv_n[s][:, :, :], t_in["cv"][b, :, :, :]).then_inc(ckv_in[s], 16)

            for s in range(2):
                load_cache(s, s)
            load_pairs(PAIR_CO, PAIR_CO + 1)
            with sp.Fori(1, NS // 2) as i:
                for s in range(2):
                    sp.wait_ge(x_pv_mm, i * 2 + (s - 1))
                    load_cache(i * 2 + s, s)
            load_pairs(PAIR_CO + 1, PAIRS)

            f = ffn["ffn2"]
            sp.wait_ge(act_lo_done, SPLIT0["co"] + NC * KT)
            sp.wait_ge(w_split[0], PAIRS)
            sp.wait_ge(w_split[1], PAIRS)
            load_gu(f, t_in["w_ffn2"], 0, first=True)
            load_ffn(f, t_in["w_ffn2"])

        @block.gpsimd
        def _(pool):
            def split(raw, hi, lo, steps, last=None):
                one = ones[:, :].unsqueeze(1).to_broadcast([P, KT, P])
                steps.done(pool.tensor_tensor(hi[:, :, :], raw[:, :, :], one, ALU.mult))
                ins = pool.tensor_tensor(lo[:, :, :], raw[:, :, :], hi[:, :, :].bitcast(F32), ALU.subtract)
                steps.done(ins) if last is None else ins.then_inc(last, 1)

            def split_gu(f, t, s):
                pool.wait_ge(f["gu_in"], (t + 1) * 32)
                steps = Steps(pool, f["pool_own"], t * 3)
                split(w_raw[0], w_hi[s], w_lo[s], steps)
                split(ff_raw_up, up_hi[s], up_lo[s], steps, f["gu_split"])

            def split_down(f, j):
                pool.wait_ge(f["dn_in"], (j + 1) * 32)
                steps = Steps(pool, f["pool_dn"], j * 3)
                split(w_raw[1], dn_hi[0], dn_lo[0], steps)
                split(ff_raw_down, dn_hi[1], dn_lo[1], steps, f["dn_split"])

            def split_ffn(f):
                split_gu(f, 1, 1)
                split_down(f, 0)
                for t in (2, 3):
                    pool.wait_ge(f["up_mm"], (t - 1) * NC)
                    split_gu(f, t, t % 2)
                with pool.Fori(1, FI - 1) as i:
                    pool.wait_ge(f["up_mm"], i * (2 * NC) + NC)
                    split_gu(f, i * 2 + 2, 0)
                    pool.wait_ge(f["dn_mm"], i * (NC * KT))
                    split_down(f, i)
                    pool.wait_ge(f["up_mm"], i * (2 * NC) + 2 * NC)
                    split_gu(f, i * 2 + 3, 1)
                pool.wait_ge(f["dn_mm"], (FI - 1) * (NC * KT))
                split_down(f, FI - 1)

            def split_plain(s, p):
                pool.wait_ge(w_in[s], (p + 1) * 16)
                split(w_raw[s], w_hi[s], w_lo[s], Steps(pool, w_pool, p * 2 + s), w_split[s])

            f = ffn["ffn1"]
            pool.wait_ge(ones_set, 1)
            split_gu(f, 0, 0)
            split_ffn(f)
            for s in range(2):
                pool.wait_ge(f["up_mm"], (FT - 1 + s) * NC)
                split_plain(s, 0)
            for pair0, pair1, base, each in GROUPS:
                with pool.Fori(max(pair0, 1), pair1) as p:
                    for s in range(2):
                        pool.wait_ge(w_mm[s], p * each + (base - pair0 * each))
                        split_plain(s, p)
            f = ffn["ffn2"]
            pool.wait_ge(w_mm[0], groups_before(PAIRS))
            pool.wait_ge(stored, 16 * 9)
            split_gu(f, 0, 0)
            pool.wait_ge(w_mm[1], groups_before(PAIRS))
            split_ffn(f)

        @block.tensor
        def _(pe):
            def three(out, pairs, first, last):
                ins = None
                for n, (wh, wl, ah, al) in enumerate(pairs):
                    end = last and n == len(pairs) - 1
                    pe.matmul(out, wh, ah, start=(first and n == 0), stop=False)
                    pe.matmul(out, wh, al, start=False, stop=False)
                    ins = pe.matmul(out, wl, ah, start=False, stop=end)
                return ins

            def product(out, wh, wl, c, feed):
                o, n = CH[c]
                for k in range(KT):
                    if feed:
                        pe.wait_ge(act_lo_done, SPLIT0[feed] + c * KT + k + 1)
                    ins = three(out, [(wh[:, k, :], wl[:, k, :], act_hi[:, k, o:o + n], act_lo[:, k, o:o + n])],
                                k == 0, k == KT - 1)
                return ins

            def sum_squares(key, chunks, adds):
                pe.wait_ge(sq_used, SQ0[key] + adds)
                for c, (o, n) in enumerate(chunks):
                    if c >= 2:
                        pe.wait_ge(ssq_ev, SUM0[key] + c - 1)
                    pe.matmul(ps[:, 6 + c % 2, 0:n], ones[:, :], acc[:, o:o + n], start=True, stop=True)\
                      .then_inc(ssq_mm, 1)

            def gu(f, t, s, feed=None, taken=None, norm=None):
                pe.wait_ge(f["gu_split"], t + 1)
                for c, (o, n) in enumerate(CH):
                    if taken:
                        taken(c)
                    product(ps[:, c, 0:n], w_hi[s], w_lo[s], c, feed).then_inc(f["gate_mm"], 1)
                    product(ps[:, 3 + c, 0:n], up_hi[s], up_lo[s], c, None).then_inc(f["up_mm"], 1)
                    if norm and c == 0:
                        sum_squares(norm, CH, KT)

            def down(f, j, t_before):
                pe.wait_ge(f["dn_split"], j + 1)
                for n_ in range(KT * NC):
                    m, c = divmod(n_, NC)
                    bank = DOWN_BANKS[n_ % 8]
                    o, n = CH[c]
                    if m == 0:
                        pe.wait_ge(f["hid_lo"], j * (2 * NC) + NC + c + 1)
                    pe.wait_ge(f["dn_ev"], j * (NC * KT) + n_ + 1)
                    if n_ < 8 and bank < 6:
                        pe.wait_ge(f["gate_ev" if bank < 3 else "up_ev"], t_before * NC + bank % 3 + 1)
                    three(ps[:, bank, 0:n], [(dn_hi[s][:, m, :], dn_lo[s][:, m, :], hid_hi[s][:, o:o + n],
                                              hid_lo[s][:, o:o + n]) for s in range(2)], True, True)\
                        .then_inc(f["dn_mm"], 1)

            def ffn_layer(f, key, before):
                def after_gu(t):
                    def taken(c):
                        pe.wait_ge(f["gate_ev"], t * NC + c + 1)
                        pe.wait_ge(f["up_ev"], t * NC + c + 1)
                    return taken

                def after_down(j):
                    def taken(c):
                        at_ = max(DOWN_BANKS.index(c), DOWN_BANKS.index(3 + c))
                        pe.wait_ge(f["dn_ev"], j * (NC * KT) + (NC * KT - 8) + at_ + 1 + 8)
                    return taken

                before()
                gu(f, 0, 0, feed=key, norm=key)
                gu(f, 1, 1, taken=after_gu(0))
                with pe.Fori(1, FI) as i:
                    gu(f, i * 2, 0, taken=after_gu(i * 2 - 1))
                    down(f, i - 1, i * 2)
                    gu(f, i * 2 + 1, 1, taken=after_down(i - 1))
                down(f, FI - 1, FT - 1)

            def tile(stage, p, s, n0, feed=None, norm=None):
                pe.wait_ge(w_split[s], p + 1)
                for c, (o, n) in enumerate(CH):
                    pe.wait_ge(g_ev[stage], n0 + c + 1)
                    ins = product(ps[:, 3 * s + c, 0:n], w_hi[s], w_lo[s], c, feed)
                    ins.then_inc(w_mm[s], 1)
                    if norm and c == 1:
                        sum_squares(norm, CH, KT)

            def plain(stage, pair0, pairs, feed, norm=None):
                tile(stage, pair0, 0, 0, feed=feed, norm=norm)
                tile(stage, pair0, 1, NC)
                with pe.Fori(1, pairs) as i:
                    for s in range(2):
                        tile(stage, i + pair0, s, i * (2 * NC) + s * NC)

            pe.wait_ge(ones_set, 1)
            ffn_layer(ffn["ffn1"], "ffn1", lambda: None)

            def lru_gates(ct):
                pe.wait_ge(conv_back, ct + 1)
                if ct == 0:
                    pe.wait_ge(bd_in, 16)
                    pe.wait_ge(ssq_ev, SUM0["mix"] + NC)
                for j in range(2 * NC):
                    n_ = ct * 2 * NC + j
                    o, n = CH[j % NC]
                    if n_ >= 2:
                        pe.wait_ge(lru_ev, n_ - 1)
                    pe.matmul(ps[:, 6 + n_ % 2, 0:n], bd[:, ct, j // NC, :], mix[:, M_U + ct, o:o + n],
                              start=True, stop=True).then_inc(lru_mm, 1)

            plain("in", PAIR_IN, 4, "mix", norm="mix")
            for m in range(8, IN_T):
                if m < 8 + LT:
                    lru_gates(m - 8)
                tile("in", m // 2, m % 2, m * NC)

            pe.wait_ge(lru_ev, LT * 2 * NC)
            sum_squares("lru", CH, LT)
            pe.wait_ge(ssq_ev, SUM0["lru"] + NC)
            sum_squares("mem", [(0, NM)], 1)
            pe.wait_ge(ssq_ev, SUM0["mem"] + 1)
            pe.wait_ge(g_ev["in"], 6 + 3 * IN_T)
            pe.wait_ge(rope_tab, 64)

            def blk(b):
                return bass.ds(b * WIN + TS, WIN)

            def rotate(b):
                if not isinstance(b, int) or b > 0:
                    pe.wait_ge(o_ev, b)
                pe.matmul(ps[:, 6, :], rotm[:, :], mix[:, M_Q:M_Q + GRP, blk(b)], start=True, stop=True)
                if not isinstance(b, int) or b > 0:
                    pe.wait_ge(vt_ev, b)
                    pe.wait_ge(kv_ev, b * 2 - 1)
                pe.matmul(ps[:, 7, 0:WIN], rotm[:, :], mix[:, M_K, blk(b)], start=True, stop=True)\
                  .then_inc(rot_mm, 1)

            def scores(b, s):
                pe.wait_ge(rope_done, b + 1)
                pe.wait_ge(sc_taken, b + 1)
                for h in range(NH):
                    kv, g = divmod(h, GRP)
                    r = slice(kv * HD, kv * HD + HD)
                    for half in range(2):
                        k = k_r[1 - s] if half == 0 else k_r[s]
                        ins = pe.matmul(ps[:, h // 2, (h % 2) * 256 + half * WIN:(h % 2) * 256 + half * WIN + WIN],
                                        q_r[r, g, :], k[r, :], start=True, stop=True)
                ins.then_inc(sc_mm, 1)

            def turn_v(b):
                pe.wait_ge(rope_done, b + 1)
                pe.wait_ge(kv_ev, b * 2 + 1)
                pe.transpose(ps[:, 7, WIN:2 * WIN], v_b[:, :], ident[:, :]).then_inc(vt_mm, 1)

            def turn_p(b, s, kv):
                pe.wait_ge(pt_ev, b * 2 + kv + 1)
                for g in range(GRP):
                    for half in range(2):
                        ins = pe.transpose(ps[:, 4 + half, g * WIN:(g + 1) * WIN],
                                           s_m[s][:, kv * GRP + g, half * WIN:(half + 1) * WIN], ident[:, :])
                ins.then_inc(pt_mm, 1)

            def weigh(b, s, kv):
                for half in range(2):
                    v = v_n[1 - s] if half == 0 else v_n[s]
                    ins = pe.matmul(ps[kv * HD:(kv + 1) * HD, 6, :], v[:, kv * HD:(kv + 1) * HD],
                                    p_T[:, half, kv * GRP:(kv + 1) * GRP, :], start=(half == 0), stop=(half == 1))
                return ins

            def memory_tile(b, s):
                pe.wait_ge(w_split[s], b + (PAIR_KV + 1))
                pe.wait_ge(kv_ev, b * 2 + s + 1)
                if s == 0:
                    pe.wait_ge(vt_ev, b + 1)
                for mt in range(1 if s == 0 else 2):
                    for k in range(KT):
                        if s == 0:
                            out = ps[:, 7, 256:512]
                            ins = three(out, [(w_hi[0][:, k, :], w_lo[0][:, k, :], memn_hi[:, k, :],
                                               memn_lo[:, k, :])], k == 0, k == KT - 1)
                        else:
                            r = slice(mt * P, (mt + 1) * P)
                            out = ps[:, 7, 256 + mt * P:256 + (mt + 1) * P]
                            ins = three(out, [(memn_hi[:, k, r], memn_lo[:, k, r], w_hi[1][:, k, :],
                                               w_lo[1][:, k, :])], k == 0, k == KT - 1)
                ins.then_inc(w_mm[s], 1)

            def block_step(b, s, more=True):
                if more:
                    rotate(b + 1)
                pe.wait_ge(p_done, b + 1)
                turn_p(b, s, 0)
                if more:
                    pe.wait_ge(rope_done, b + 2)
                memory_tile(b, 0)
                turn_p(b, s, 1)
                if more:
                    scores(b + 1, 1 - s)
                if not more:
                    pe.wait_ge(o_ev, b + 1)
                pe.wait_ge(pt_ev, b * 2 + 2)
                weigh(b, s, 0)
                memory_tile(b, 1)
                pe.wait_ge(pt_ev, b * 2 + 3)
                weigh(b, s, 1).then_inc(pv_mm, 1)
                if more:
                    turn_v(b + 1)

            rotate(0)
            scores(0, 0)
            turn_v(0)
            pe.wait_ge(memn_lo_done, 1)
            with pe.Fori(0, NB // 2 - 1) as i:
                block_step(i * 2, 0)
                block_step(i * 2 + 1, 1)
            block_step(NB - 2, 0)
            block_step(NB - 1, 1, more=False)

            pe.wait_ge(kvc_in, 48)
            pe.wait_ge(o_ev, NB + 1)
            pe.matmul(ps[:, 6, 0:GRP * TS], rotm[:, :], mix[:, M_Q:M_Q + GRP, 0:TS], start=True, stop=True)
            pe.matmul(ps[:, 6, 256:256 + TS], rotm[:, :], mix[:, M_K, 0:TS], start=True, stop=True)\
              .then_inc(s_rot_mm, 1)
            pe.wait_ge(pt_ev, NB * 2 + 1)
            for b in range(NS):
                pe.transpose(ps[0:LS, 4 + b // 4, (b % 4) * P:(b % 4 + 1) * P], mix[:, M_V, b * LS:(b + 1) * LS],
                             ident[:, :]).then_inc(s_rot_mm, 1)
            pe.wait_ge(s_rope, 1)
            pe.wait_ge(sc_taken, NB + 1)
            for b in range(NS):
                for kv in range(KVH):
                    r = slice(kv * HD, kv * HD + HD)
                    q = qs_r[r, b, :, :]
                    out = ps[32 * (b % 4):32 * (b % 4) + 32, (b // 4) * 2 + kv, 0:WIN + LS]
                    pe.matmul(out[:, 0:WIN], q, kc_T[r, b, :], start=True, stop=True)
                    ins = pe.matmul(out[:, WIN:WIN + LS], q, ks_r[r, b * LS:(b + 1) * LS], start=True, stop=True)
            ins.then_inc(s_sc_mm, 1)
            pe.wait_ge(s_p, 1)
            for t in range(4):
                pe.transpose(ps[:, 2, t * P:(t + 1) * P], ss_m[:, t, 0:WIN], ident[:, :])
                ins = pe.transpose(ps[0:LS, 3, t * P:(t + 1) * P], ss_m[:, t, WIN:WIN + LS], ident[:, :])
            ins.then_inc(s_pt_mm, 1)
            pe.wait_ge(s_pt_ev, 3)
            for b in range(NS):
                for kv in range(KVH):
                    t, j = (b // 4) * 2 + kv, b % 4
                    r = slice(kv * HD, kv * HD + HD)
                    out = ps[r, 6, b * 32:(b + 1) * 32]
                    pe.matmul(out, v_c[:, b, r], pcs_T[:, t, 32 * j:32 * j + 32], start=True, stop=False)
                    ins = pe.matmul(out, vs_n[:, b, r], pns_T[:, t, 32 * j:32 * j + 32], start=False, stop=True)
            ins.then_inc(s_pv_mm, 1)
            sum_squares("attn", CH, LT)

            plain("out", PAIR_OUT, 4, "cat")
            plain("cq", PAIR_CQ, 4, "xattn", norm="xattn")

            pe.wait_ge(x_tab, 16)
            pe.wait_ge(g_ev["cq"], 6 + NC * KT)

            def x_scores(b, half, s):
                pe.wait_ge(xq_st, b + 1)
                pe.wait_ge(x_exp, b + 1)
                for h in range(XH):
                    for d in range(2):
                        pe.matmul(ps[:, h // 2, (h % 2) * NM:(h % 2 + 1) * NM], xq_b[:, 2 * h + d, :],
                                  mem_kT[:, 2 * h + d, :], start=(d == 0), stop=(d == 1))
                pe.wait_ge(ckv_in[s], half * 32 + 32)
                for h in range(XH):
                    for d in range(2):
                        ins = pe.matmul(ps[32 * h:32 * h + 32, 2, 0:NM], qs_b[:, 2 * h + d, :],
                                        ck_T[s][:, 2 * h + d, :], start=(d == 0), stop=(d == 1))
                ins.then_inc(x_sc_mm, 1)

            def x_turn(b, s):
                pe.wait_ge(x_p, b + 1)
                pe.wait_ge(x_pt_ev, b + 1)
                pe.wait_ge(x_o_ev, b + 1)
                for h in range(XH):
                    for mt in range(2):
                        pe.transpose(ps[:, 3 + mt, h * P:(h + 1) * P], xs_m[s][:, h, mt * P:(mt + 1) * P],
                                     x_id[:, :])
                for mt in range(2):
                    ins = pe.transpose(ps[:, 5, mt * P:(mt + 1) * P], ys_m[s][:, mt * P:(mt + 1) * P], x_id[:, :])
                ins.then_inc(x_pt_mm, 1)

            def x_weigh(b, s):
                pe.wait_ge(x_pt_ev, b + 2)
                for kt in range(KT):
                    for mt in range(2):
                        pe.matmul(ps[:, 6 + kt // 4, (kt % 4) * P:(kt % 4 + 1) * P],
                                  mem_v[:, mt, kt * P:(kt + 1) * P], xp_T[:, mt, kt // 2, :],
                                  start=(mt == 0), stop=(mt == 1))
                for kt in range(KT):
                    for mt in range(2):
                        h = kt // 2
                        ins = pe.matmul(ps[:, 5, 256 + kt * LS:256 + (kt + 1) * LS],
                                        cv_n[s][:, mt, kt * P:(kt + 1) * P], yp_T[:, mt, 32 * h:32 * h + LS],
                                        start=(mt == 0), stop=(mt == 1))
                ins.then_inc(x_pv_mm, 1)

            def x_step(b, half, s, more=True):
                if more:
                    x_scores(b + 1, half + s, 1 - s)
                x_turn(b, s)
                x_weigh(b, s)

            x_scores(0, 0, 0)
            with pe.Fori(0, NB // 2 - 1) as i:
                x_step(i * 2, i, 0)
                x_step(i * 2 + 1, i, 1)
            x_step(NB - 2, NB // 2 - 1, 0)
            x_step(NB - 1, NB // 2 - 1, 1, more=False)

            plain("co", PAIR_CO, 4, "co")
            ffn_layer(ffn["ffn2"], "ffn2", lambda: pe.wait_ge(g_ev["co"], 6 + NC * KT))
            sum_squares("final", CH, KT)

        @block.scalar
        def _(act):
            def squares(key, tiles, src, ready):
                for m in range(tiles):
                    square(key, m, src(m), ready)

            def square(key, m, src, ready):
                ready(m)
                if not (isinstance(m, int) and m == 0):
                    act.wait_ge(sq_used, m + SQ0[key])
                act.activation(sq[:, :], src, ACT.Square).then_inc(sq_done, 1)

            def rms(key, n, chunks=NC):
                act.wait_ge(ssq_ev, SUM0[key] + chunks)
                act.activation(rstd[:, 0:n], rstd[:, 0:n], ACT.Sqrt).then_inc(rms_done, 1)

            def hi_parts(key, src, gain=None, ready=None):
                for c, (o, n) in enumerate(CH):
                    if ready:
                        ready(c)
                    for k in range(KT):
                        act.activation(act_hi[:, k, o:o + n], src(k)[:, o:o + n], ACT.Copy,
                                       scale=c_(gain, k) if gain else 1.0).then_inc(act_hi_done, 1)

            def ffn_tile(f, t, s, down_done):
                for c, (o, n) in enumerate(CH):
                    act.wait_ge(f["gate_ev"], t * NC + c + 1)
                    act.activation(gate_t[:, o:o + n], gate_t[:, o:o + n], ACT.Silu).then_inc(f["silu"], 1)
                if down_done is not None:
                    act.wait_ge(f["dn_mm"], down_done)
                for c, (o, n) in enumerate(CH):
                    act.wait_ge(f["hid_f"], t * NC + c + 1)
                    act.activation(hid_hi[s][:, o:o + n], hid_t[:, o:o + n], ACT.Copy).then_inc(f["hid_hi"], 1)

            def ffn_layer(f, after):
                ffn_tile(f, 0, 0, None)
                ffn_tile(f, 1, 1, None)
                with act.Fori(1, FI) as i:
                    ffn_tile(f, i * 2, 0, i * (NC * KT))
                    ffn_tile(f, i * 2 + 1, 1, i * (NC * KT))
                squares(after, KT, lambda m: x[:, m, :],
                        lambda m: act.wait_ge(f["dn_ev"], 8 + (FI - 1) * NC * KT + NC * (m + 1)))

            def x_tile(k):
                return x[:, k, :]

            act.wait_ge(cst_in, 16)
            hi_parts("ffn1", x_tile, "g_ffn1", ready=lambda c: act.wait_ge(x_in[c], 16))
            squares("ffn1", KT, x_tile, lambda m: None)
            act.wait_ge(lru_sp, 1)
            act.activation(lrup[:, 2, :], lrup[:, 2, :], ACT.Exp, scale=-1.0).then_inc(lru_sp, 1)
            rms("ffn1", T)
            ffn_layer(ffn["ffn1"], "mix")
            hi_parts("mix", x_tile, "g_mix")
            rms("mix", T)

            for ct in range(LT):
                act.wait_ge(conv_done, ct + 1)
                act.activation(mix[:, M_U + ct, :], t_conv[:, :], ACT.Copy).then_inc(conv_back, 1)
            act.wait_ge(g_ev["in"], 6 + 8 * NC)
            act.activation(mix[:, M_G:M_G + LT, :], mix[:, M_G:M_G + LT, :], ACT.Gelu_apprx_tanh)\
               .then_inc(gate_gelu, 1)
            for ct in range(LT):
                if ct:
                    act.wait_ge(lru_y, ct)
                for j in range(2 * NC):
                    n_ = ct * 2 * NC + j
                    o, n = CH[j % NC]
                    act.wait_ge(lru_mm, n_ + 1)
                    if j < NC:
                        act.activation(t_a[:, o:o + n], ps[:, 6 + n_ % 2, 0:n], ACT.Exp,
                                       bias=lrup[:, 4, ct:ct + 1], scale=-1.0).then_inc(lru_ev, 1)
                    else:
                        act.activation(t_b[:, o:o + n], ps[:, 6 + n_ % 2, 0:n], ACT.Tanh,
                                       bias=lrup[:, 5, ct:ct + 1], scale=0.5).then_inc(lru_ev, 1)
                act.wait_ge(lru_r, ct + 1)
                act.activation(t_conv[:, :], t_a[:, :], ACT.Tanh, scale=lrup[:, 6, ct:ct + 1]).then_inc(lru_th, 1)
                act.activation(t_a[:, :], t_a[:, :], ACT.Exp, scale=lrup[:, 7, ct:ct + 1]).then_inc(lru_a, 1)
                act.wait_ge(lru_q, ct + 1)
                act.activation(t_conv[:, :], t_conv[:, :], ACT.Sqrt, scale=0.5).then_inc(lru_s, 1)
            act.wait_ge(lru_y, LT)
            act.dma_start(t_out["small"], small[:, :]).then_inc(stored, 16)
            squares("lru", LT, lambda m: mix[:, M_U + m, :], lambda m: None)
            rms("lru", T)
            act.wait_ge(mem_in, 16)
            act.activation(s_m[0][:, :, :], mem_raw[:, :, :], ACT.Square).then_inc(sq_done, 1)
            rms("mem", NM, 1)
            act.wait_ge(lru_normed, LT + KT)
            act.activation(memn_hi[:, :, :], mem_raw[:, :, :], ACT.Copy).then_inc(memn_hi_done, 1)

            def exps(b, s):
                act.wait_ge(nmax_done, b + 1)
                for h in range(NH):
                    act.activation(s_m[s][:, h, :], s_m[s][:, h, :], ACT.Exp, bias=st8[:, 1, h:h + 1],
                                   scale=HD ** -0.5, accum_out=st8[:, 4, h:h + 1])
                act.activation(st8[:, 3, :], st8[:, 2, :], ACT.Exp).then_inc(exp_done, 1)

            def take_v(b, s):
                act.wait_ge(vt_mm, b + 1)
                act.activation(v_n[s][:, :], ps[:, 7, WIN:2 * WIN], ACT.Copy).then_inc(vt_ev, 1)

            def block_step(b, s, more=True):
                for kv in range(KVH):
                    act.wait_ge(pt_mm, b * 2 + kv + 1)
                    act.activation(p_T[:, :, kv * GRP:(kv + 1) * GRP, :], ps[:, 4:6, :], ACT.Copy)\
                       .then_inc(pt_ev, 1)
                if more:
                    exps(b + 1, 1 - s)
                    take_v(b + 1, 1 - s)

            act.sem_inc(pt_ev, 1)
            exps(0, 0)
            take_v(0, 0)
            with act.Fori(0, NB // 2 - 1) as i:
                block_step(i * 2, 0)
                block_step(i * 2 + 1, 1)
            block_step(NB - 2, 0)
            act.wait_ge(rope_done, NB)
            act.wait_ge(vt_ev, NB)
            act.dma_start(t_out["k_prompt"], k_r[1][:, :]).then_inc(stored, 16)
            act.dma_start(t_out["v_prompt"], v_n[1][:, :]).then_inc(stored, 16)
            block_step(NB - 1, 1, more=False)
            act.wait_ge(s_rot_mm, 1 + NS)
            act.activation(vs_n[:, :, :], ps[0:LS, 4:6, :], ACT.Copy).then_inc(s_pt_ev, 1)
            act.wait_ge(s_rope, 1)
            act.dma_start(t_out["k_sample"][:, :, 0:WIN - LS], kc_T[:, :, LS:WIN]).then_inc(stored, 16)
            act.dma_start(t_out["k_sample"][:, :, WIN - LS:WIN], ks_r[:, :].rearrange("p (b t) -> p b t", b=NS))\
               .then_inc(stored, 16)
            act.dma_start(t_out["v_sample"][0:WIN - LS, :, :], v_c[LS:WIN, :, :]).then_inc(stored, 16)
            act.wait_ge(s_pt_ev, 1)
            act.dma_start(t_out["v_sample"][WIN - LS:WIN, :, :], vs_n[:, :, :]).then_inc(stored, 16)
            act.wait_ge(s_nmax, 1)
            for t in range(4):
                act.activation(ss_m[:, t, :], ss_m[:, t, :], ACT.Exp, bias=st8[:, 1, t:t + 1], scale=HD ** -0.5,
                               accum_out=st8[:, 4, t:t + 1])
            act.activation(st8[:, 3, 0:4], st8[:, 2, 0:4], ACT.Exp).then_inc(s_exp, 1)
            act.wait_ge(s_pt_mm, 1)
            act.activation(pcs_T[:, :, :], ps[:, 2, :], ACT.Copy).then_inc(s_pt_ev, 1)
            act.activation(pns_T[:, :, :], ps[0:LS, 3, :], ACT.Copy).then_inc(s_pt_ev, 1)

            def cat_tile(k):
                return mix[:, M_U + k, :] if k < LT else mix[:, M_Q + k - LT, :]

            act.wait_ge(s_o_ev, 1)
            act.wait_ge(stored, 16 * 7)
            squares("attn", LT, lambda m: mix[:, M_Q + m, :], lambda m: None)
            rms("attn", T)
            act.wait_ge(lru_normed, 2 * LT + KT)
            hi_parts("cat", cat_tile)
            act.dma_start(t_out["mem_k"], mem_kT[:, :, :]).then_inc(stored, 16)
            act.dma_start(t_out["mem_v"], mem_v[:, :, :]).then_inc(stored, 16)

            def plain_squares(stage, key):
                def ready(m):
                    act.wait_ge(g_ev[stage], m * NC + (6 + NC))
                for m in range(2):
                    square(key, m, x[:, m, :], ready)
                with act.Fori(2, KT) as m:
                    square(key, m, x[:, m, :], ready)

            plain_squares("out", "xattn")
            act.wait_ge(w_mm[1], groups_before(PAIR_CQ))
            hi_parts("xattn", x_tile, "g_xattn")
            rms("xattn", T)

            def x_exps(b, s):
                act.wait_ge(x_nmax, b + 1)
                for h in range(XH):
                    act.activation(xs_m[s][:, h, :], ps[:, h // 2, (h % 2) * NM:(h % 2 + 1) * NM], ACT.Exp,
                                   bias=xst[:, s, 1, h:h + 1], scale=XD ** -0.5, accum_out=xst[:, s, 2, h:h + 1])
                act.activation(ys_m[s][:, :], ps[:, 2, 0:NM], ACT.Exp, bias=yst[:, s * 4 + 1:s * 4 + 2],
                               scale=XD ** -0.5, accum_out=yst[:, s * 4 + 2:s * 4 + 3]).then_inc(x_exp, 1)

            def x_step(b, s, more=True):
                if more:
                    x_exps(b + 1, 1 - s)
                act.wait_ge(x_pt_mm, b + 1)
                act.activation(xp_T[:, :, :, :], ps[:, 3:5, :], ACT.Copy)
                act.activation(yp_T[:, :, :], ps[:, 5, 0:2 * P], ACT.Copy).then_inc(x_pt_ev, 1)

            act.sem_inc(x_exp, 1)
            act.sem_inc(x_pt_ev, 1)
            x_exps(0, 0)
            with act.Fori(0, NB // 2 - 1) as i:
                x_step(i * 2, 0)
                x_step(i * 2 + 1, 1)
            x_step(NB - 2, 0)
            x_step(NB - 1, 1, more=False)

            act.wait_ge(x_pv_mm, NB)
            act.wait_ge(x_o_ev, 1 + NB)
            hi_parts("co", lambda k: xq[:, k, :])
            plain_squares("co", "ffn2")
            act.wait_ge(w_mm[1], groups_before(PAIRS))
            hi_parts("ffn2", x_tile, "g_ffn2")
            rms("ffn2", T)
            act.wait_ge(stored, 16 * 9)
            ffn_layer(ffn["ffn2"], "final")
            rms("final", T)
            for m in range(KT):
                act.wait_ge(y_done, m + 1)
                act.dma_start(t_out["y"][:, m, :], y[:, m, :]).then_inc(stored, 16)
            act.wait_ge(stored, 16 * (9 + KT))

        @block.vector
        def _(dve):
            own = Steps(dve, dve_own)

            def take_out(out, src):
                return dve.tensor_scalar(out, src, 1.0, None, ALU.mult)

            def add_square(key, m):
                dve.wait_ge(sq_done, m + (SQ0[key] + 1))
                if isinstance(m, int) and m == 0:
                    dve.tensor_copy(acc[:, :], sq[:, :]).then_inc(sq_used, 1)
                else:
                    dve.wait_ge(sq_used, m + SQ0[key])
                    dve.tensor_tensor(acc[:, :], acc[:, :], sq[:, :], ALU.add).then_inc(sq_used, 1)

            def inverse_rms(key, width, chunks=CH):
                for c, (o, n) in enumerate(chunks):
                    dve.wait_ge(ssq_mm, SUM0[key] + c + 1)
                    dve.tensor_scalar(rstd[:, o:o + n], ps[:, 6 + c % 2, 0:n], 1.0 / width, EPS, ALU.mult, ALU.add)\
                       .then_inc(ssq_ev, 1)
                end = chunks[-1][0] + chunks[-1][1]
                dve.wait_ge(rms_done, NORMS.index(key) + 1)
                dve.reciprocal(rstd[:, 0:end], rstd[:, 0:end]).then_inc(rstd_done, 1)
                dve.wait_ge(rstd_done, NORMS.index(key) + 1)

            def lo_parts(key, src, gain=None):
                for c, (o, n) in enumerate(CH):
                    for k in range(KT):
                        dve.wait_ge(act_hi_done, SPLIT0[key] + c * KT + k + 1)
                        hi = act_hi[:, k, o:o + n].bitcast(F32)
                        if gain:
                            ins = dve.scalar_tensor_tensor(out=act_lo[:, k, o:o + n], in0=src(k)[:, o:o + n],
                                                           scalar=c_(gain, k), in1=hi, op0=ALU.mult,
                                                           op1=ALU.subtract)
                        else:
                            ins = dve.tensor_tensor(act_lo[:, k, o:o + n], src(k)[:, o:o + n], hi, ALU.subtract)
                        ins.then_inc(act_lo_done, 1)

            def ffn_hidden(f, t):
                def gate(c):
                    o, n = CH[c]
                    dve.wait_ge(f["gate_mm"], t * NC + c + 1)
                    dve.tensor_tensor(gate_t[:, o:o + n], ps[:, c, 0:n], rstd[:, o:o + n], ALU.mult)\
                       .then_inc(f["gate_ev"], 1)

                def up(c):
                    o, n = CH[c]
                    dve.wait_ge(f["up_mm"], t * NC + c + 1)
                    dve.wait_ge(f["silu"], t * NC + c + 1)
                    dve.tensor_tensor(hid_t[:, o:o + n], ps[:, 3 + c, 0:n], gate_t[:, o:o + n], ALU.mult)\
                       .then_inc(f["up_ev"], 1)
                    dve.wait_ge(f["up_ev"], t * NC + c + 1)
                    dve.tensor_tensor(hid_t[:, o:o + n], hid_t[:, o:o + n], rstd[:, o:o + n], ALU.mult)\
                       .then_inc(f["hid_f"], 1)

                gate(0)
                gate(1)
                up(0)
                gate(2)
                up(1)
                up(2)

            def ffn_lo(f, t, s):
                for c, (o, n) in enumerate(CH):
                    dve.wait_ge(f["hid_hi"], t * NC + c + 1)
                    dve.tensor_tensor(hid_lo[s][:, o:o + n], hid_t[:, o:o + n],
                                      hid_hi[s][:, o:o + n].bitcast(F32), ALU.subtract).then_inc(f["hid_lo"], 1)

            def ffn_take(f, j, m):
                for c, (o, n) in enumerate(CH):
                    dve.wait_ge(f["dn_mm"], j * (NC * KT) + m * NC + c + 1)
                    dve.scalar_tensor_tensor(out=x[:, m, o:o + n], in0=ps[:, DOWN_BANKS[(m * NC + c) % 8], 0:n],
                                             scalar=0.5, in1=x[:, m, o:o + n], op0=ALU.mult, op1=ALU.add)\
                       .then_inc(f["dn_ev"], 1)

            def ffn_layer(f, key, after):
                inverse_rms(key, D)
                dve.sem_inc(f["dn_ev"], 8)
                for t in range(2):
                    ffn_hidden(f, t)
                    ffn_lo(f, t, t)
                with dve.Fori(1, FI) as i:
                    ffn_hidden(f, i * 2)
                    dve.wait_ge(f["dn_ev"], i * (NC * KT) + (8 - NC * KT))
                    for m in range(KT):
                        ffn_take(f, i - 1, m)
                    ffn_lo(f, i * 2, 0)
                    ffn_hidden(f, i * 2 + 1)
                    ffn_lo(f, i * 2 + 1, 1)
                dve.wait_ge(f["dn_ev"], (FI - 1) * NC * KT + 8)
                for m in range(KT):
                    ffn_take(f, FI - 1, m)
                    if m:
                        add_square(after, m - 1)
                add_square(after, KT - 1)
                dve.wait_ge(f["dn_ev"], FI * NC * KT + 8)

            def x_tile(k):
                return x[:, k, :]

            def scaled_take(stage, s, p, dst):
                for c, (o, n) in enumerate(CH):
                    dve.wait_ge(w_mm[s], slot_groups(stage, p, c))
                    dve.tensor_tensor(dst[:, o:o + n], ps[:, 3 * s + c, 0:n], rstd[:, o:o + n], ALU.mult)\
                       .then_inc(g_ev[stage], 1)

            def slot_groups(stage, p, c):
                a, _, base, each = GROUPS[0] if stage == "in" else GROUPS[2]
                return p * each + (base - a * each + c + 1)

            dve.memset(ones[:, :], 1.0).then_inc(ones_set, 1)
            dve.wait_ge(cst_in, 16)
            lo_parts("ffn1", x_tile, "g_ffn1")
            for m in range(KT):
                add_square("ffn1", m)

            lam, neg, e, den, z, z2, ser = (c_("lam", 0, LT), lrup[:, 1, :], lrup[:, 2, :], lrup[:, 3, :],
                                            lrup[:, 0, :], lrup[:, 4, :], lrup[:, 5, :])
            own.done(dve.tensor_scalar(neg, lam, -1.0, None, ALU.mult))
            dve.tensor_tensor(e, lam, neg, ALU.max).then_inc(lru_sp, 1)
            dve.wait_ge(lru_sp, 2)
            own.done(dve.tensor_scalar(den, e, 2.0, None, ALU.add))
            own.done(dve.reciprocal(den, den))
            own.done(dve.tensor_tensor(z, e, den, ALU.mult))
            own.done(dve.tensor_tensor(z2, z, z, ALU.mult))
            own.done(dve.tensor_scalar(ser, z2, 1.0 / 17, 1.0 / 15, ALU.mult, ALU.add))
            for k in (13, 11, 9, 7, 5, 3, 1):
                own.done(dve.tensor_tensor(ser, ser, z2, ALU.mult))
                own.done(dve.tensor_scalar(ser, ser, 1.0 / k, None, ALU.add))
            own.done(dve.tensor_tensor(ser, ser, z, ALU.mult))
            own.done(dve.tensor_scalar(ser, ser, 16.0, None, ALU.mult))
            own.done(dve.tensor_scalar(neg, neg, 0.0, 8.0, ALU.max, ALU.mult))
            own.done(dve.tensor_tensor(lrup[:, 6, :], ser, neg, ALU.add))
            own.done(dve.tensor_scalar(lrup[:, 7, :], lrup[:, 6, :], -1.0, None, ALU.mult))
            own.done(dve.tensor_scalar(lrup[:, 4, :], c_("b_a", 0, LT), -1.0, None, ALU.mult))
            own.done(dve.tensor_scalar(lrup[:, 5, :], c_("b_i", 0, LT), 0.5, None, ALU.mult))

            ffn_layer(ffn["ffn1"], "ffn1", "mix")
            lo_parts("mix", x_tile, "g_mix")
            dve.sem_inc(g_ev["in"], 6)
            inverse_rms("mix", D)

            def take_in(a, b):
                with dve.Fori(a, b) as p:
                    for s in range(2):
                        scaled_take("in", s, p, mix[:, bass.ds(p * 2 + s, 1), :].squeeze(1))

            take_in(0, 2)

            own.base, own.n = own.base + own.n, 0
            dve.wait_ge(g_ev["in"], 6 + 4 * NC)
            for ct in range(LT):
                u = mix[:, M_U + ct, :]
                us = u[:, 0:TS].rearrange("p (b t) -> p b t", b=NS)
                cs = t_conv[:, 0:TS].rearrange("p (b t) -> p b t", b=NS)
                o, _ = COLS["hist"]
                hist = cst[:, o + ct * NS * 3:o + (ct + 1) * NS * 3].rearrange("p (b t) -> p b t", b=NS)
                if ct:
                    dve.wait_ge(conv_back, ct)
                dve.tensor_copy(small[:, SM_CP + ct * 3:SM_CP + ct * 3 + 3], u[:, T - 3:T])
                dve.tensor_copy(small[:, SM_CS + ct * NS * 3:SM_CS + (ct + 1) * NS * 3]
                                .rearrange("p (b t) -> p b t", b=NS), us[:, :, LS - 3:LS])
                own.done(dve.tensor_scalar(t_conv[:, :], u, c_("conv_w", 3 * LT + ct), c_("conv_b", ct), ALU.mult,
                                           ALU.add))
                for d in (1, 2, 3):
                    w = c_("conv_w", (3 - d) * LT + ct)
                    parts = [(t_conv[:, TS + d:T], u[:, TS:T - d]), (cs[:, :, d:LS], us[:, :, 0:LS - d]),
                             (cs[:, :, 0:d], hist[:, :, 3 - d:3])]
                    for n_, (to, src) in enumerate(parts):
                        ins = dve.scalar_tensor_tensor(out=to, in0=src, scalar=w, in1=to, op0=ALU.mult, op1=ALU.add)
                        if d == 3 and n_ == 2:
                            ins.then_inc(conv_done, 1)
                        else:
                            own.done(ins)
            take_in(2, 4)

            def lru_tile(ct):
                u, g = mix[:, M_U + ct, :], mix[:, M_G + ct, :]
                h0 = c_("h0", ct * NS, NS)
                tmp = small[:, SM_HS + ct * NS:SM_HS + (ct + 1) * NS]
                dve.wait_ge(lru_ev, ct * 2 * NC + NC)
                own.done(dve.tensor_scalar(t_a[:, :], t_a[:, :], 1.0, None, ALU.add))
                dve.reciprocal(t_a[:, :], t_a[:, :]).then_inc(lru_r, 1)
                dve.wait_ge(lru_ev, (ct + 1) * 2 * NC)
                own.done(dve.scalar_tensor_tensor(out=t_b[:, :], in0=t_b[:, :], scalar=1.0, in1=u, op0=ALU.add,
                                                  op1=ALU.mult))
                dve.wait_ge(lru_th, ct + 1)
                own.done(dve.tensor_scalar(u, t_conv[:, :], 1.0, None, ALU.add))
                own.done(dve.reciprocal(u, u))
                dve.tensor_tensor(t_conv[:, :], t_conv[:, :], u, ALU.mult).then_inc(lru_q, 1)
                dve.wait_ge(lru_a, ct + 1)
                own.done(dve.tensor_tensor(tmp, t_a[:, 0:TS:LS], h0, ALU.mult))
                dve.wait_ge(lru_s, ct + 1)
                own.done(dve.tensor_tensor(t_b[:, :], t_conv[:, :], t_b[:, :], ALU.mult))
                own.done(dve.tensor_tensor(t_b[:, 0:TS:LS], t_b[:, 0:TS:LS], tmp, ALU.add))
                own.done(dve.memset(t_a[:, 0:TS + 1:LS], 0.0))
                own.done(dve.tensor_tensor_scan(u, t_a[:, :], t_b[:, :], 0.0, ALU.mult, ALU.add))
                own.done(dve.tensor_copy(tmp, u[:, LS - 1:TS:LS]))
                own.done(dve.tensor_copy(small[:, SM_HP + ct:SM_HP + ct + 1], u[:, T - 1:T]))
                if ct == 0:
                    dve.wait_ge(gate_gelu, 1)
                dve.tensor_tensor(u, u, g, ALU.mult).then_inc(lru_y, 1)

            for m in range(8, IN_T):
                if m < 8 + LT:
                    lru_tile(m - 8)
                scaled_take("in", m % 2, m // 2, mix[:, m, :])

            def norm_tiles(first, gain, before):
                for ct in range(LT):
                    tile_ = mix[:, first + ct, :]
                    dve.scalar_tensor_tensor(out=tile_, in0=tile_, scalar=c_(gain, ct), in1=rstd[:, :], op0=ALU.mult,
                                             op1=ALU.mult).then_inc(lru_normed, 1)
                dve.wait_ge(lru_normed, before + LT)

            for ct in range(LT):
                add_square("lru", ct)
            inverse_rms("lru", LRU)
            norm_tiles(M_U, "g_lru_out", 0)

            dve.wait_ge(sq_done, SQ0["mem"] + 1)
            dve.tensor_reduce(acc[:, 0:NM], s_m[0][:, :, :].rearrange("p k t -> p t k"), AX_X, ALU.add)\
               .then_inc(sq_used, 1)
            inverse_rms("mem", D, [(0, NM)])
            for k in range(KT):
                dve.scalar_tensor_tensor(out=mem_raw[:, k, :], in0=mem_raw[:, k, :], scalar=c_("g_mem", k),
                                         in1=rstd[:, 0:NM], op0=ALU.mult, op1=ALU.mult).then_inc(lru_normed, 1)
            dve.wait_ge(memn_hi_done, 1)
            dve.tensor_tensor(memn_lo[:, :, :], mem_raw[:, :, :], memn_hi[:, :, :].bitcast(F32), ALU.subtract)\
               .then_inc(memn_lo_done, 1)

            dve.memset(k_r[1][:, :], 0.0)
            own.done(dve.memset(v_n[1][:, :], 0.0))
            own.done(dve.tensor_scalar(st8[:, 7, :], c_("sink", 0, NH), HD ** 0.5, None, ALU.mult))
            dve.sem_inc(sc_taken, 1)
            dve.sem_inc(o_ev, 1)
            dve.sem_inc(kv_ev, 1)
            dve.wait_ge(rope_tab, 64)

            def blk(b):
                return bass.ds(b * WIN + TS, WIN)

            def over(ap, n, w):
                return ap.unsqueeze(1).to_broadcast([P, n, w])

            SWA_STEPS = 13

            def rope(b, s, steps):
                cos, sin = rope_cos[:, blk(b)], rope_sin[:, blk(b)]
                dve.wait_ge(rot_mm, b + 1)
                if not (isinstance(b, int) and b == 0):
                    dve.wait_ge(sc_mm, b)
                    dve.wait_ge(vt_mm, b)
                dve.tensor_tensor(rot_q[:, :, :], ps[:, 6, :].rearrange("p (g w) -> p g w", g=GRP),
                                  over(sin, GRP, WIN), ALU.mult)
                steps.mark(dve.tensor_tensor(rot_k[:, :], ps[:, 7, 0:WIN], sin, ALU.mult))
                dve.tensor_tensor(q_r[:, :, :], mix[:, M_Q:M_Q + GRP, blk(b)], over(cos, GRP, WIN), ALU.mult)
                dve.tensor_copy(v_b[:, :], mix[:, M_V, blk(b)])
                steps.done(dve.tensor_tensor(k_r[s][:, :], mix[:, M_K, blk(b)], cos, ALU.mult))
                dve.tensor_tensor(q_r[:, :, :], q_r[:, :, :], rot_q[:, :, :], ALU.add)
                dve.tensor_tensor(k_r[s][:, :], k_r[s][:, :], rot_k[:, :], ALU.add).then_inc(rope_done, 1)

            def softmax(b, s, steps, mask):
                dve.wait_ge(sc_mm, b + 1)
                dve.tensor_tensor(s_m[s][:, :, :], ps[:, 0:4, :].rearrange("p a (h w) -> p (a h) w", w=2 * WIN),
                                  over(mask, NH, 2 * WIN), ALU.add).then_inc(sc_taken, 1)
                dve.wait_ge(sc_taken, b + 2)
                steps.done(dve.tensor_reduce(st8[:, 0, :], s_m[s][:, :, :], AX_X, ALU.max))
                steps.done(dve.tensor_tensor(st8[:, 0, :], st8[:, 0, :], st8[:, 7, :], ALU.max))
                steps.done(dve.tensor_scalar(st8[:, 1, :], st8[:, 0, :], -(HD ** -0.5), None, ALU.mult))
                dve.tensor_tensor(st8[:, 2, :], st8[:, 1, :], c_("sink", 0, NH), ALU.add).then_inc(nmax_done, 1)
                dve.wait_ge(exp_done, b + 1)
                steps.done(dve.tensor_tensor(st8[:, 5, :], st8[:, 3, :], st8[:, 4, :], ALU.add))
                steps.done(dve.reciprocal(st8[:, 6, :], st8[:, 5, :]))
                dve.tensor_tensor(s_m[s][:, :, :], s_m[s][:, :, :],
                                  st8[:, 6, :].unsqueeze(2).to_broadcast([P, NH, 2 * WIN]), ALU.mult)\
                   .then_inc(p_done, 1)

            STEPS_A_BLOCK = 7

            def block_step(b, s, mask, more=True):
                steps = Steps(dve, swa_own, (b + 1) * STEPS_A_BLOCK)
                if more:
                    rope(b + 1, 1 - s, steps)
                dve.wait_ge(w_mm[0], b + (groups_before(PAIR_KV) + 1))
                take_out(mem_kT[:, bass.ds(b, 1), :].squeeze(1), ps[:, 7, 256:512]).then_inc(kv_ev, 1)
                if more:
                    softmax(b + 1, 1 - s, steps, mask)
                    assert steps.n == STEPS_A_BLOCK
                dve.wait_ge(w_mm[1], b + (groups_before(PAIR_KV) + 1))
                take_out(mem_v[:, :, bass.ds(b * P, P)], ps[:, 7, 256:512].rearrange("p (m d) -> p m d", m=2))\
                   .then_inc(kv_ev, 1)
                dve.wait_ge(pv_mm, b + 1)
                take_out(mix[:, M_Q:M_Q + GRP, blk(b)], ps[:, 6, :].rearrange("p (g w) -> p g w", g=GRP))\
                   .then_inc(o_ev, 1)

            first = Steps(dve, swa_own, 0)
            rope(0, 0, first)
            dve.wait_ge(swa_tab, 16)
            softmax(0, 0, first, masks[:, 0, :])
            band = masks[:, 1, :]
            with dve.Fori(0, NB // 2 - 1) as i:
                block_step(i * 2, 0, band)
                block_step(i * 2 + 1, 1, band)
            block_step(NB - 2, 0, band)
            block_step(NB - 1, 1, None, more=False)

            own.base, own.n = own.base + own.n, 0
            dve.wait_ge(s_rot_mm, 1)
            cos, sin = rope_cos[:, 0:TS], rope_sin[:, 0:TS]
            dve.tensor_tensor(rot_q[:, :, 0:TS], ps[:, 6, 0:256].rearrange("p (g w) -> p g w", g=GRP),
                              over(sin, GRP, TS), ALU.mult)
            dve.tensor_tensor(rot_k[:, 0:TS], ps[:, 6, 256:256 + TS], sin, ALU.mult)
            dve.tensor_tensor(q_r[:, :, 0:TS], mix[:, M_Q:M_Q + GRP, 0:TS], over(cos, GRP, TS), ALU.mult)
            own.done(dve.tensor_tensor(ks_r[:, :], mix[:, M_K, 0:TS], cos, ALU.mult))
            dve.tensor_tensor(qs_r[:, :, :, :].rearrange("p b g t -> p g b t"),
                              q_r[:, :, 0:TS].rearrange("p g (b t) -> p g b t", b=NS),
                              rot_q[:, :, 0:TS].rearrange("p g (b t) -> p g b t", b=NS), ALU.add)
            dve.tensor_tensor(ks_r[:, :], ks_r[:, :], rot_k[:, 0:TS], ALU.add).then_inc(s_rope, 1)
            own.done(dve.tensor_scalar(st8[:, 7, 0:4], c_("sink_s", 0, 4), HD ** 0.5, None, ALU.mult))
            dve.wait_ge(kvc_in, 48)
            dve.wait_ge(s_sc_mm, 1)
            own.done(dve.tensor_tensor(ss_m[:, :, :], ps[:, 0:4, 0:WIN + LS], over(mask_s[:, :], 4, WIN + LS), ALU.add))
            own.done(dve.tensor_reduce(st8[:, 0, 0:4], ss_m[:, :, :], AX_X, ALU.max))
            own.done(dve.tensor_tensor(st8[:, 0, 0:4], st8[:, 0, 0:4], st8[:, 7, 0:4], ALU.max))
            own.done(dve.tensor_scalar(st8[:, 1, 0:4], st8[:, 0, 0:4], -(HD ** -0.5), None, ALU.mult))
            dve.tensor_tensor(st8[:, 2, 0:4], st8[:, 1, 0:4], c_("sink_s", 0, 4), ALU.add).then_inc(s_nmax, 1)
            dve.wait_ge(s_exp, 1)
            own.done(dve.tensor_tensor(st8[:, 5, 0:4], st8[:, 3, 0:4], st8[:, 4, 0:4], ALU.add))
            own.done(dve.reciprocal(st8[:, 6, 0:4], st8[:, 5, 0:4]))
            dve.tensor_tensor(ss_m[:, :, :], ss_m[:, :, :],
                              st8[:, 6, 0:4].unsqueeze(2).to_broadcast([P, 4, WIN + LS]), ALU.mult).then_inc(s_p, 1)
            dve.wait_ge(s_pv_mm, 1)
            dve.tensor_copy(mix[:, M_Q:M_Q + GRP, 0:TS].rearrange("p g (b t) -> p g b t", b=NS),
                            ps[:, 6, 0:256].rearrange("p (b g t) -> p g b t", b=NS, g=GRP)).then_inc(s_o_ev, 1)

            dve.wait_ge(stored, 16 * 7)
            for ct in range(LT):
                add_square("attn", ct)
            inverse_rms("attn", LRU)
            norm_tiles(M_Q, "g_attn_out", LT + KT)

            def cat_tile(k):
                return mix[:, M_U + k, :] if k < LT else mix[:, M_Q + k - LT, :]

            lo_parts("cat", cat_tile)

            def plain_residual(stage, pair0, key):
                def take(m, p, s):
                    to = x[:, m, :] if isinstance(m, int) else x[:, bass.ds(m, 1), :].squeeze(1)
                    for c, (o, n) in enumerate(CH):
                        dve.wait_ge(w_mm[s], slot_groups(stage, p, c))
                        dve.tensor_tensor(to[:, o:o + n], ps[:, 3 * s + c, 0:n], to[:, o:o + n], ALU.add)\
                           .then_inc(g_ev[stage], 1)
                    add_square(key, m)

                dve.sem_inc(g_ev[stage], 6)
                for s in range(2):
                    take(s, pair0, s)
                with dve.Fori(1, KT // 2) as i:
                    for s in range(2):
                        take(i * 2 + s, i + pair0, s)
                dve.wait_ge(g_ev[stage], 6 + NC * KT)

            plain_residual("out", PAIR_OUT, "xattn")
            lo_parts("xattn", x_tile, "g_xattn")
            dve.sem_inc(g_ev["cq"], 6)
            inverse_rms("xattn", D)
            with dve.Fori(0, KT // 2) as i:
                for s in range(2):
                    scaled_take("cq", s, i + PAIR_CQ, xq[:, bass.ds(i * 2 + s, 1), :].squeeze(1))
            dve.wait_ge(g_ev["cq"], 6 + NC * KT)

            def xcol(b):
                return bass.ds(b * P + TS, P)

            def x_stage(b):
                dve.tensor_copy(qs_b[:, :, :], xq[:, :, bass.ds(b * LS, 32)])
                dve.tensor_copy(xq_b[:, :, :], xq[:, :, xcol(b)]).then_inc(xq_st, 1)

            def x_soft(b, s, steps):
                dve.wait_ge(x_sc_mm, b + 1)
                steps.mark(dve.tensor_reduce(xst[:, s, 0, :], ps[:, 0:2, :].rearrange("p a (h w) -> p (a h) w", w=NM),
                                             AX_X, ALU.max))
                steps.done(dve.tensor_reduce(yst[:, 4 * s:4 * s + 1], ps[:, 2, 0:NM], AX_X, ALU.max))
                dve.tensor_scalar(xst[:, s, 1, :], xst[:, s, 0, :], -(XD ** -0.5), None, ALU.mult)
                dve.tensor_scalar(yst[:, 4 * s + 1:4 * s + 2], yst[:, 4 * s:4 * s + 1], -(XD ** -0.5), None,
                                  ALU.mult).then_inc(x_nmax, 1)

            def x_norm(b, s, steps):
                dve.wait_ge(x_exp, b + 2)
                steps.mark(dve.reciprocal(xst[:, s, 3, :], xst[:, s, 2, :]))
                steps.done(dve.reciprocal(yst[:, 4 * s + 3:4 * s + 4], yst[:, 4 * s + 2:4 * s + 3]))
                dve.tensor_tensor(xs_m[s][:, :, :], xs_m[s][:, :, :],
                                  xst[:, s, 3, :].unsqueeze(2).to_broadcast([P, XH, NM]), ALU.mult)
                dve.tensor_scalar(ys_m[s][:, :], ys_m[s][:, :], yst[:, 4 * s + 3:4 * s + 4], None, ALU.mult)\
                   .then_inc(x_p, 1)

            X_STEPS = 4

            def x_take(b):
                dve.wait_ge(x_pv_mm, b + 1)
                take_out(xq[:, :, xcol(b)], ps[:, 6:8, :].rearrange("p a (k w) -> p (a k) w", w=P))
                dve.tensor_copy(xq[:, :, bass.ds(b * LS, LS)],
                                ps[:, 5, 256:256 + TS].rearrange("p (k w) -> p k w", w=LS)).then_inc(x_o_ev, 1)

            def x_step(b, s, more=True, stage=True):
                if more:
                    steps = Steps(dve, x_own, (b + 1) * X_STEPS)
                    x_soft(b + 1, 1 - s, steps)
                    if stage:
                        x_stage(b + 2)
                    x_norm(b + 1, 1 - s, steps)
                x_take(b)

            dve.sem_inc(x_o_ev, 1)
            x_stage(0)
            first = Steps(dve, x_own, 0)
            x_soft(0, 0, first)
            x_stage(1)
            x_norm(0, 0, first)
            with dve.Fori(0, NB // 2 - 1) as i:
                x_step(i * 2, 0)
                x_step(i * 2 + 1, 1)
            x_step(NB - 2, 0, stage=False)
            x_step(NB - 1, 1, more=False)
            dve.wait_ge(x_o_ev, 1 + NB)

            lo_parts("co", lambda k: xq[:, k, :])
            plain_residual("co", PAIR_CO, "ffn2")
            lo_parts("ffn2", x_tile, "g_ffn2")
            ffn_layer(ffn["ffn2"], "ffn2", "final")
            inverse_rms("final", D)
            for m in range(KT):
                dve.scalar_tensor_tensor(out=y[:, m, :], in0=x[:, m, :], scalar=c_("g_final", m), in1=rstd[:, :],
                                         op0=ALU.mult, op1=ALU.mult).then_inc(y_done, 1)


_OUTS = {
    "y": (P, KT, T), "mem_k": (P, KT, NM), "mem_v": (P, 2, D), "k_prompt": (P, WIN), "v_prompt": (P, KVH * HD),
    "k_sample": (P, NS, WIN), "v_sample": (WIN, NS, KVH * HD), "small": (P, NSM),
}


def tables():
    half = HD // 2
    inv = (10000.0 ** (-np.arange(half) / half)).astype(np.float32)
    pos = np.concatenate([np.tile(1024 + np.arange(LS), NS), np.arange(SEQ)]).astype(np.float32)
    ang = np.tile(inv, P // half)[:, None] * pos[None, :]
    rot = np.zeros((P, P), np.float32)
    for m in range(P):
        if m % HD < half:
            rot[m + half, m] = -1.0
        else:
            rot[m - half, m] = 1.0
    i, j = np.arange(WIN)[:, None], np.arange(2 * WIN)[None, :]
    band = np.where((j > i) & (j <= i + WIN), 0.0, NEG).astype(np.float32)
    start = np.where(j >= WIN, band, np.float32(NEG))
    masks = np.stack([start, band], axis=1)
    tok, key = (np.arange(P) % LS)[:, None], np.arange(WIN + LS)[None, :]
    mask_s = np.where((key > tok) & (key <= tok + WIN), 0.0, NEG).astype(np.float32)
    return {"cos": np.cos(ang).astype(np.float32), "sin": np.sin(ang).astype(np.float32), "rotm": rot,
            "ident": np.eye(P, dtype=np.float32), "masks": np.ascontiguousarray(masks), "mask_s": mask_s}


def kernel(**inputs):
    import concourse.bacc as bacc
    from concourse.bass_utils import run_bass_kernel_spmd

    a = {k: np.asarray(v) for k, v in inputs.items()}

    def per_tile(v):
        return v.reshape(-1, P).T

    def lhs_tiles(w):
        k, m = w.shape
        return w.reshape(k // P, P, m // P, P).transpose(2, 1, 0, 3)

    heads = [kv * GRP + g for g in range(GRP) for kv in range(KVH)]
    perm = np.concatenate([np.arange(h * HD, (h + 1) * HD) for h in heads])
    w_in = a["w_in"][0]
    q0 = 2 * LRU
    w_in = np.concatenate([w_in[:, :q0], w_in[:, q0:q0 + NH * HD][:, perm], w_in[:, q0 + NH * HD:]], axis=1)
    w_out = np.concatenate([a["w_out"][0][:LRU], a["w_out"][0][LRU:][perm]], axis=0)
    kv_tiles = np.stack([lhs_tiles(a["w_ck"][0]), lhs_tiles(a["w_cv"][0])], axis=1).reshape(2 * KT, P, KT, P)
    plain = np.concatenate([lhs_tiles(w_in), kv_tiles, lhs_tiles(w_out), lhs_tiles(a["w_cq"][0]),
                            lhs_tiles(a["w_co"][0])])
    plain = plain.reshape(PAIRS, 2, P, KT, P).transpose(1, 0, 2, 3, 4)

    def ffn_weights(n):
        return np.stack([lhs_tiles(a[f"w{n}_gate"][0]), lhs_tiles(a[f"w{n}_up"][0]),
                         a[f"w{n}_down"][0].reshape(FT, P, KT, P)], axis=1)

    tokens = np.concatenate([a["x_sample"].reshape(TS, D), a["x_prompt"][0]])

    def feature_major(v):
        return v.T.reshape(-1, P, v.shape[0]).transpose(1, 0, 2)

    bd = np.zeros((P, LT, 2, P), np.float32)
    nb = LRU // 8
    for g in range(8):
        r = slice((g % 2) * nb, (g % 2 + 1) * nb)
        bd[r, g // 2, 0, r] = a["w_a"][0, g]
        bd[r, g // 2, 1, r] = a["w_i"][0, g]
    sink = a["sink"][0]
    sink_s = np.tile(np.repeat(sink.reshape(KVH, GRP).T, LS, axis=0), (4, 2))
    parts = {
        **{g: per_tile(a[g][0]) for g in ("g_ffn1", "g_mix", "g_xattn", "g_ffn2", "g_mem", "g_lru_out", "conv_b",
                                          "b_a", "b_i", "lam")},
        "g_attn_out": per_tile(a["g_attn_out"][0][perm]),
        "g_final": per_tile(a["g_final"]),
        "conv_w": np.concatenate([per_tile(a["conv_w"][0, j]) for j in range(4)], axis=1),
        "sink": np.tile(sink, (P, 1)),
        "sink_s": sink_s,
        "h0": a["state_lru_h"][0].T.reshape(LT, P, NS).transpose(1, 0, 2).reshape(P, LT * NS),
        "hist": a["state_conv"][0].transpose(2, 0, 1).reshape(LT, P, NS, 3).transpose(1, 0, 2, 3)
        .reshape(P, LT * NS * 3),
    }
    host = {
        "x": feature_major(tokens),
        "cst": np.concatenate([parts[k] for k in COLS], axis=1),
        "w_ffn1": ffn_weights(1), "w_ffn2": ffn_weights(2), "w_plain": plain, "bd": bd,
        "mem": feature_major(a["mem_prompt"][0]),
        "kc": a["cache_swa_k"][0].transpose(2, 3, 0, 1).reshape(P, NS, WIN),
        "vc": a["cache_swa_v"][0].transpose(1, 0, 2, 3).reshape(WIN, NS, KVH * HD),
        "ck": a["cache_mem_k"][0].reshape(NS, NM, KT, P).transpose(0, 3, 2, 1),
        "cv": a["cache_mem_v"][0].reshape(NS, 2, P, D).transpose(0, 2, 1, 3),
        **tables(),
    }
    host = {k: np.ascontiguousarray(v) for k, v in host.items()}
    nc = bacc.Bacc("TRN2", target_bir_lowering=False, num_devices=1)
    t_in = {k: nc.dram_tensor(f"in_{k}", v.shape, F32, kind="ExternalInput").ap() for k, v in host.items()}
    t_out = {k: nc.dram_tensor(f"out_{k}", s, F32, kind="ExternalOutput").ap() for k, s in _OUTS.items()}
    build(nc, t_in, t_out)
    r = run_bass_kernel_spmd(nc, [{f"in_{k}": v for k, v in host.items()}], core_ids=[0]).results[0]
    o = {k: r[f"out_{k}"] for k in _OUTS}

    y = o["y"].transpose(2, 1, 0).reshape(T, D)
    small = o["small"]
    conv_p = small[:, SM_CP:SM_CS].reshape(P, LT, 3).transpose(2, 1, 0).reshape(1, 1, 3, LRU)
    conv_s = small[:, SM_CS:SM_HP].reshape(P, LT, NS, 3).transpose(2, 3, 1, 0).reshape(1, NS, 3, LRU)
    h_p = small[:, SM_HP:SM_HS].T.reshape(1, 1, LRU)
    h_s = small[:, SM_HS:].reshape(P, LT, NS).transpose(2, 1, 0).reshape(1, NS, LRU)
    return (
        y[TS:].reshape(1, SEQ, D), y[:TS].reshape(NS, LS, D),
        o["mem_k"].transpose(2, 1, 0).reshape(1, 1, NM, XH, XD),
        o["mem_v"].transpose(1, 0, 2).reshape(1, 1, NM, XH, XD),
        o["k_prompt"].T.reshape(1, 1, WIN, KVH, HD), o["v_prompt"].reshape(1, 1, WIN, KVH, HD),
        conv_p, h_p,
        o["k_sample"].transpose(1, 2, 0).reshape(1, NS, WIN, KVH, HD),
        o["v_sample"].transpose(1, 0, 2).reshape(1, NS, WIN, KVH, HD),
        conv_s, h_s,
    )
```

```python
from contextlib import ExitStack

import numpy as np
import concourse.bass as bass
from concourse import mybir

F32 = mybir.dt.float32
F32R = mybir.dt.float32r
ALU = mybir.AluOpType
ACT = mybir.ActivationFunctionType
AX_X = mybir.AxisListType.X

P = 128
D = 1024
KT = D // P
SEQ = 1024
NS, LS = 8, 8
TS = NS * LS
T = TS + SEQ
FF = 2816
FT = FF // P
FI = FT // 2
LRU = 512
LT = LRU // P
HD = 64
NH = 8
WIN = 128
NB = SEQ // WIN
KVH = 2
GRP = NH // KVH
NM = 256
XH = 4
XD = D // XH
EPS = 1e-6
IN_T = (2 * LRU + NH * HD + 2 * KVH * HD) // P
NEG = -1.0e30
CH = [(0, 364), (364, 362), (726, 362)]
NC = len(CH)
HALVES = [(0, T // 2), (T // 2, T // 2)]
M_U, M_G, M_Q, M_K, M_V = 0, 4, 8, 12, 13

DOWN_BANKS = (6, 7, 0, 3, 1, 4, 2, 5)

COLS = {}
_n = 0
for _name, _w in [("g_ffn1", KT), ("g_mix", KT), ("g_xattn", KT), ("g_ffn2", KT), ("g_mem", KT), ("g_final", KT),
                  ("g_cat", KT), ("conv_w", 4 * LT), ("conv_b", LT), ("b_a", LT),
                  ("b_i", LT), ("lam", LT), ("sink", NH), ("sink_s", 4), ("h0", LT * NS), ("hist", LT * NS * 3)]:
    COLS[_name] = (_n, _w)
    _n += _w
NCST = _n
SM_CP, SM_CS, SM_HP, SM_HS = 0, LT * 3, LT * 3 + LT * NS * 3, LT * 3 + LT * NS * 3 + LT
NSM = SM_HS + LT * NS
PAIR_IN, PAIR_KV, PAIR_OUT, PAIR_CQ, PAIR_CO, PAIRS = 0, 7, 15, 19, 23, 27
GROUPS = [(PAIR_IN, PAIR_KV, 0, NC), (PAIR_KV, PAIR_OUT, 7 * NC, 0), (PAIR_OUT, PAIRS, 7 * NC, NC)]
NORMS = ("ffn1", "mix", "lru", "mem", "attn", "xattn", "ffn2", "final")
_SQUARES = {"lru": 2 * LT, "mem": 1, "attn": 2 * LT}
SQ0 = {k: sum(_SQUARES.get(j, 2 * KT) for j in NORMS[:n]) for n, k in enumerate(NORMS)}
SUM0 = {k: sum(1 if j == "mem" else NC for j in NORMS[:n]) for n, k in enumerate(NORMS)}
SPLIT0 = {k: n * NC * KT for n, k in enumerate(("ffn1", "mix", "cat", "xattn", "co", "ffn2"))}


def groups_before(pair):
    return max(base + (min(pair, b) - a) * each for a, b, base, each in GROUPS if pair > a) if pair else 0


class Steps:

    def __init__(self, eng, sem, base=0):
        self.eng, self.sem, self.base, self.n = eng, sem, base, 0

    def mark(self, ins):
        self.n += 1
        ins.then_inc(self.sem, 1)
        return self.base + self.n

    def done(self, ins):
        self.eng.wait_ge(self.sem, self.mark(ins))


def build(nc, t_in, t_out):
    ctx = ExitStack()
    with ctx:
        def sem(name):
            return ctx.enter_context(nc.semaphore(name))

        START = 16512
        LIMIT = 229344

        def at(name, shape, off, dt=F32):
            size = 4 * int(np.prod(shape[1:]))
            assert off % 32 == 0 and off + size <= LIMIT, (name, off, size)
            return nc.alloc_sbuf_tensor_at(name, shape, dt, offset=off)

        ROW = 4 * T
        X0 = START
        A0 = X0 + KT * ROW
        RS0 = A0 + 2 * KT * ROW
        W0 = RS0 + ROW
        C0 = W0 + 6 * 4096
        P0 = C0 + 928 + 512 + 576
        x = at("x", [P, KT, T], X0)
        act_hi = at("act_hi", [P, KT, T], A0, F32R)
        act_lo = at("act_lo", [P, KT, T], A0 + KT * ROW, F32R)
        rstd = at("rstd", [P, T], RS0)
        w_raw = [at(f"w_raw{s}", [P, KT, P], W0 + s * 4096) for s in range(2)]
        w_hi2 = at("w_hi2", [P, 2, KT, P], W0 + 8192, F32R)
        w_lo2 = at("w_lo2", [P, 2, KT, P], W0 + 16384, F32R)
        w_hi = [w_hi2[:, s, :, :] for s in range(2)]
        w_lo = [w_lo2[:, s, :, :] for s in range(2)]
        assert NCST * 4 <= 928 and NSM * 4 <= 576
        cst = at("cst", [P, NCST], C0)
        ones = at("ones", [P, P], C0 + 928)
        small = at("small", [P, NSM], C0 + 1440)
        ACC0 = P0 + 68608
        lrup = at("lrup", [P, 8, LT], ACC0 + 2 * ROW)
        acc = at("acc", [P, T], ACC0)
        sq = at("sq", [P, T], ACC0 + ROW)
        ff_raw_up = at("ff_raw_up", [P, KT, P], P0)
        ff_raw_down = at("ff_raw_down", [P, KT, P], P0 + 4096)
        up_hi = [at(f"up_hi{s}", [P, KT, P], P0 + 8192 + s * 4096, F32R) for s in range(2)]
        up_lo = [at(f"up_lo{s}", [P, KT, P], P0 + 16384 + s * 4096, F32R) for s in range(2)]
        dn_hi = [at(f"dn_hi{s}", [P, KT, P], P0 + 24576 + s * 4096, F32R) for s in range(2)]
        dn_lo = [at(f"dn_lo{s}", [P, KT, P], P0 + 32768 + s * 4096, F32R) for s in range(2)]
        hid_hi = [at(f"hid_hi{s}", [P, T], P0 + 40960 + s * ROW, F32R) for s in range(2)]
        hid_lo = [at(f"hid_lo{s}", [P, T], P0 + 40960 + (2 + s) * ROW, F32R) for s in range(2)]
        gate_t = at("gate_t", [P, T], P0 + 40960 + 4 * ROW)
        hid_t = at("hid_t", [P, T], P0 + 40960 + 5 * ROW)
        mix = at("mix", [P, IN_T, T], P0)
        t_conv = at("t_conv", [P, T], P0 + IN_T * ROW)
        t_a = at("t_a", [P, T], P0 + (IN_T + 1) * ROW)
        t_b = at("t_b", [P, T], P0 + (IN_T + 2) * ROW)
        bd = at("bd", [P, LT, 2, P], P0 + M_V * ROW)
        mem_kT = at("mem_kT", [P, KT, NM], P0 + M_G * ROW)
        mem_v = at("mem_v", [P, 2, D], P0 + M_G * ROW + 8192)
        mem_raw = at("mem_raw", [P, KT, NM], P0 + M_G * ROW + 8192)

        lru_rstd = at("lru_rstd", [P, T], P0 + IN_T * ROW)
        mem_sq = at("mem_sq", [P, KT, NM], P0 + M_G * ROW)

        cur = [A0]

        def here(name, shape, dt=F32):
            tns = at(name, shape, cur[0], dt)
            cur[0] += -(-4 * int(np.prod(shape[1:])) // 32) * 32
            assert cur[0] <= RS0, name
            return tns

        rope_cos = here("rope_cos", [P, T])
        rope_sin = here("rope_sin", [P, T])
        masks = here("masks", [P, 2, 2 * WIN])
        ident = here("ident", [P, P])
        rotm = here("rotm", [P, P])
        s_m = [here(f"s_m{s}", [P, NH, 2 * WIN]) for s in range(2)]
        p_T = here("p_T", [P, 2, NH, WIN])
        q_r = here("q_r", [P, GRP, WIN])
        k_r = [here(f"k_r{s}", [P, WIN]) for s in range(2)]
        v_b = here("v_b", [P, WIN])
        v_n = [here(f"v_n{s}", [P, KVH * HD]) for s in range(2)]
        rot_q = here("rot_q", [P, GRP, WIN])
        rot_k = here("rot_k", [P, WIN])
        st8 = here("st8", [P, 8, NH])
        memn_hi = here("memn_hi", [P, KT, NM], F32R)
        memn_lo = here("memn_lo", [P, KT, NM], F32R)
        SA0 = P0 + IN_T * ROW
        kc_T = at("kc_T", [P, NS, WIN], SA0)
        v_c = at("v_c", [P, NS, KVH * HD], SA0 + 4096)
        qs_r = at("qs_r", [P, NS, GRP, LS], SA0 + 8192)
        ks_r = at("ks_r", [P, TS], SA0 + 9216)
        mask_s = at("mask_s", [P, WIN + LS], SA0 + 9472)
        SM0 = A0 + 2 * ROW + 2048 + 1024
        ss_m = at("ss_m", [P, 4, WIN + LS], SM0)
        pcs_T = at("pcs_T", [P, 4, P], SM0 + 2208)
        pns_T = at("pns_T", [LS, 4, P], SM0 + 2208 + 2048)
        vs_n = at("vs_n", [LS, NS, KVH * HD], SA0 + 10240)

        xq = at("xq", [P, KT, T], P0 + 33792)
        cur[0] = A0
        x_id = here("x_id", [P, P])
        xq_b = here("xq_b", [P, KT, P])
        xs_m = [here(f"xs_m{s}", [P, XH, NM]) for s in range(2)]
        xp_T = here("xp_T", [P, 2, XH, P])
        xst = here("xst", [P, 2, 4, XH])
        qs_b = here("qs_b", [P, KT, 32])
        ys_m = [here(f"ys_m{s}", [P, NM]) for s in range(2)]
        yp_T = here("yp_T", [P, 2, P])
        yst = here("yst", [P, 8])
        y_s = here("y_s", [P, NM])
        ck_T = [here(f"ck_T{s}", [P, KT, NM]) for s in range(2)]
        cv_n = [here(f"cv_n{s}", [P, 2, D]) for s in range(2)]

        y = at("y", [P, KT, T], P0)
        ps = ctx.enter_context(nc.psum_tensor("ps", [P, 8, 512], F32))

        def c_(name, j=0, n=1):
            o, w = COLS[name]
            return cst[:, o + j:o + j + n]

        def cd(name, j):
            return cst[:, bass.ds(j + COLS[name][0], 1)]

        cst_in = sem("cst_in")
        bd_in = sem("bd_in")
        x_in = [sem(f"x_in{c}") for c in range(NC)]
        ones_set = sem("ones_set")
        dve_own = sem("dve_own")
        act_own = sem("act_own")
        act_hi_done, act_lo_done = sem("act_hi_done"), sem("act_lo_done")
        memn_hi_done, memn_lo_done = sem("memn_hi_done"), sem("memn_lo_done")
        sq_done, sq_used = sem("sq_done"), sem("sq_used")
        ssq_mm, ssq_ev = sem("ssq_mm"), sem("ssq_ev")
        rms_done, rstd_done = sem("rms_done"), sem("rstd_done")

        def ffn_sems(tag):
            names = ("gu_in", "dn_in", "gu_split", "dn_split", "pool_own", "pool_dn", "gate_mm", "up_mm",
                     "gate_ev", "up_ev", "silu", "hid_f", "hid_hi", "hid_lo", "dn_mm", "dn_ev")
            return {n: sem(f"{tag}_{n}") for n in names}

        ffn = {"ffn1": ffn_sems("ffn1"), "ffn2": ffn_sems("ffn2")}
        w_in = [sem(f"w_in{s}") for s in range(2)]
        w_split = [sem(f"w_split{s}") for s in range(2)]
        w_mm = [sem(f"w_mm{s}") for s in range(2)]
        w_pool = sem("w_pool")
        STAGES = ("in", "out", "cq", "co")
        g_ev = {k: sem(f"{k}_ev") for k in STAGES}
        conv_done = sem("conv_done")
        conv_back = sem("conv_back")
        gate_gelu = sem("gate_gelu")
        lru_sp = sem("lru_sp")
        lru_mm = sem("lru_mm")
        lru_ev = sem("lru_ev")
        lru_r = sem("lru_r")
        lru_th = sem("lru_th")
        lru_a = sem("lru_a")
        lru_q = sem("lru_q")
        lru_s = sem("lru_s")
        lru_y = sem("lru_y")
        lru_normed, mem_normed, attn_normed = sem("lru_normed"), sem("mem_normed"), sem("attn_normed")
        swa_tab = sem("swa_tab")
        rope_tab = sem("rope_tab")
        rot_mm, rope_done = sem("rot_mm"), sem("rope_done")
        sc_mm, sc_taken, nmax_done, exp_done, p_done = (
            sem("sc_mm"), sem("sc_taken"), sem("nmax_done"), sem("exp_done"), sem("p_done"))
        pt_mm, pt_ev = sem("pt_mm"), sem("pt_ev")
        vt_mm, vt_ev = sem("vt_mm"), sem("vt_ev")
        pv_mm, o_ev = sem("pv_mm"), sem("o_ev")
        kv_ev = sem("kv_ev")
        rot_ev, v_st, mem_mm = sem("rot_ev"), sem("v_st"), sem("mem_mm")
        swa_own = sem("swa_own")
        mem_in = sem("mem_in")
        kvc_in = sem("kvc_in")
        s_rot_mm, s_rope, s_sc_mm, s_nmax, s_exp, s_p = (
            sem("s_rot_mm"), sem("s_rope"), sem("s_sc_mm"), sem("s_nmax"), sem("s_exp"), sem("s_p"))
        s_pt_mm, s_pt_ev, s_pv_mm, s_o_ev = sem("s_pt_mm"), sem("s_pt_ev"), sem("s_pv_mm"), sem("s_o_ev")
        x_tab = sem("x_tab")
        ck_in = [sem(f"ck_in{s}") for s in range(2)]
        cv_in = [sem(f"cv_in{s}") for s in range(2)]
        x_turned, y_mm, y_ev = sem("x_turned"), sem("y_mm"), sem("y_ev")
        xq_st, x_sc_mm, x_nmax, x_exp, x_p = sem("xq_st"), sem("x_sc_mm"), sem("x_nmax"), sem("x_exp"), sem("x_p")
        x_pt_mm, x_pt_ev, x_pv_mm, x_o_ev, x_own = (
            sem("x_pt_mm"), sem("x_pt_ev"), sem("x_pv_mm"), sem("x_o_ev"), sem("x_own"))
        y_done = sem("y_done")
        stored = sem("stored")

        block = ctx.enter_context(nc.Block())

        def pair_src(s, p):
            return t_in["w_plain"][s, p, :, :, :]


        @block.sync
        def _(sp):
            def load_gu(f, w, t, first=False):
                if not first:
                    sp.wait_ge(f["gu_split"], t)
                sp.dma_start(w_raw[0][:, :, :], w[t, 0, :, :, :]).then_inc(f["gu_in"], 16)
                sp.dma_start(ff_raw_up[:, :, :], w[t, 1, :, :, :]).then_inc(f["gu_in"], 16)

            def load_down(f, w, j, first=False):
                if not first:
                    sp.wait_ge(f["dn_split"], j)
                sp.dma_start(w_raw[1][:, :, :], w[j * 2, 2, :, :, :]).then_inc(f["dn_in"], 16)
                sp.dma_start(ff_raw_down[:, :, :], w[j * 2 + 1, 2, :, :, :]).then_inc(f["dn_in"], 16)

            def load_ffn(f, w):
                load_gu(f, w, 1)
                load_down(f, w, 0, first=True)
                load_gu(f, w, 2)
                load_gu(f, w, 3)
                with sp.Fori(1, FI - 1) as i:
                    load_gu(f, w, i * 2 + 2)
                    load_down(f, w, i)
                    load_gu(f, w, i * 2 + 3)
                load_down(f, w, FI - 1)

            def load_pairs(a, b):
                with sp.Fori(a, b) as p:
                    for s in range(2):
                        sp.wait_ge(w_split[s], p)
                        sp.dma_start(w_raw[s][:, :, :], pair_src(s, p)).then_inc(w_in[s], 16)

            f = ffn["ffn1"]
            sp.dma_start(cst[:, :], t_in["cst"]).then_inc(cst_in, 16)
            for c, (o, n) in enumerate(CH):
                if c == 0:
                    load_gu(f, t_in["w_ffn1"], 0, first=True)
                sp.dma_start(x[:, :, o:o + n], t_in["x"][:, :, o:o + n]).then_inc(x_in[c], 16)
            load_ffn(f, t_in["w_ffn1"])

            sp.wait_ge(f["gu_split"], FT)
            sp.dma_start(w_raw[0][:, :, :], pair_src(0, 0)).then_inc(w_in[0], 16)
            sp.wait_ge(f["dn_split"], FI)
            sp.dma_start(w_raw[1][:, :, :], pair_src(1, 0)).then_inc(w_in[1], 16)
            sp.wait_ge(g_ev["in"], 6 + 3)
            sp.dma_start(bd[:, :, :, :], t_in["bd"]).then_inc(bd_in, 16)
            load_pairs(1, PAIR_KV)
            sp.wait_ge(lru_y, LT)
            sp.dma_start(mem_raw[:, :, :], t_in["mem"]).then_inc(mem_in, 16)
            load_pairs(PAIR_KV, PAIR_KV + 1)
            sp.wait_ge(w_mm[1], groups_before(PAIR_KV))
            for dst, src in ((rotm, "rotm"), (rope_cos, "cos"), (rope_sin, "sin"), (ident, "ident")):
                sp.dma_start(dst[:, :], t_in[src]).then_inc(rope_tab, 16)
            sp.dma_start(masks[:, :, :], t_in["masks"]).then_inc(swa_tab, 16)
            sp.wait_ge(lru_normed, LT)
            sp.wait_ge(mem_normed, 1)
            sp.dma_start(kc_T[:, :, :], t_in["kc"]).then_inc(kvc_in, 16)
            sp.dma_start(v_c[:, :, :], t_in["vc"]).then_inc(kvc_in, 16)
            sp.dma_start(mask_s[:, :], t_in["mask_s"]).then_inc(kvc_in, 16)
            load_pairs(PAIR_KV + 1, PAIR_CO)
            sp.wait_ge(w_mm[1], groups_before(PAIR_CO))
            sp.dma_start(x_id[:, :], t_in["ident"]).then_inc(x_tab, 16)

            def load_keys(b, s):
                sp.dma_start(ck_T[s][:, :, :], t_in["ck"][b, :, :, :]).then_inc(ck_in[s], 16)

            def load_values(b, s):
                sp.dma_start(cv_n[s][:, :, :], t_in["cv"][b, :, :, :]).then_inc(cv_in[s], 16)

            for s in range(2):
                load_keys(s, s)
                load_values(s, s)
            load_pairs(PAIR_CO, PAIR_CO + 1)
            with sp.Fori(1, NS // 2) as i:
                for s in range(2):
                    sp.wait_ge(x_sc_mm, i * 2 + (s - 1))
                    load_keys(i * 2 + s, s)
                    sp.wait_ge(y_mm, i * 2 + (s - 1))
                    load_values(i * 2 + s, s)
            load_pairs(PAIR_CO + 1, PAIRS)

            f = ffn["ffn2"]
            sp.wait_ge(act_lo_done, SPLIT0["co"] + NC * KT)
            sp.wait_ge(w_split[0], PAIRS)
            sp.wait_ge(w_split[1], PAIRS)
            load_gu(f, t_in["w_ffn2"], 0, first=True)
            load_ffn(f, t_in["w_ffn2"])

        @block.gpsimd
        def _(pool):
            def split(raw, hi, lo, steps, last=None):
                one = ones[:, :].unsqueeze(1).to_broadcast([P, KT, P])
                steps.done(pool.tensor_tensor(hi[:, :, :], raw[:, :, :], one, ALU.mult))
                ins = pool.tensor_tensor(lo[:, :, :], raw[:, :, :], hi[:, :, :].bitcast(F32), ALU.subtract)
                steps.done(ins) if last is None else ins.then_inc(last, 1)

            def split_gu(f, t, s):
                pool.wait_ge(f["gu_in"], (t + 1) * 32)
                steps = Steps(pool, f["pool_own"], t * 3)
                split(w_raw[0], w_hi[s], w_lo[s], steps)
                split(ff_raw_up, up_hi[s], up_lo[s], steps, f["gu_split"])

            def split_down(f, j):
                pool.wait_ge(f["dn_in"], (j + 1) * 32)
                steps = Steps(pool, f["pool_dn"], j * 3)
                split(w_raw[1], dn_hi[0], dn_lo[0], steps)
                split(ff_raw_down, dn_hi[1], dn_lo[1], steps, f["dn_split"])

            def split_ffn(f):
                split_gu(f, 1, 1)
                split_down(f, 0)
                for t in (2, 3):
                    pool.wait_ge(f["up_mm"], (t - 1) * NC)
                    split_gu(f, t, t % 2)
                with pool.Fori(1, FI - 1) as i:
                    pool.wait_ge(f["up_mm"], i * (2 * NC) + NC)
                    split_gu(f, i * 2 + 2, 0)
                    pool.wait_ge(f["dn_mm"], i * (NC * KT))
                    split_down(f, i)
                    pool.wait_ge(f["up_mm"], i * (2 * NC) + 2 * NC)
                    split_gu(f, i * 2 + 3, 1)
                pool.wait_ge(f["dn_mm"], (FI - 1) * (NC * KT))
                split_down(f, FI - 1)

            def split_plain(s, p):
                pool.wait_ge(w_in[s], (p + 1) * 16)
                split(w_raw[s], w_hi[s], w_lo[s], Steps(pool, w_pool, p * 2 + s), w_split[s])

            f = ffn["ffn1"]
            pool.wait_ge(ones_set, 1)
            split_gu(f, 0, 0)
            split_ffn(f)
            for s in range(2):
                pool.wait_ge(f["up_mm"], (FT - 1 + s) * NC)
                split_plain(s, 0)
            def split_pairs(first, last, pair0, base):
                with pool.Fori(first, last) as p:
                    for s in range(2):
                        pool.wait_ge(w_mm[s], p * NC + (base - pair0 * NC))
                        split_plain(s, p)

            split_pairs(1, PAIR_KV + 1, PAIR_IN, 0)
            pool.wait_ge(rstd_done, SUM0["lru"] + NC)
            for ct in range(LT):
                pool.tensor_tensor(mix[:, M_U + ct, :], mix[:, M_U + ct, :], lru_rstd[:, :], ALU.mult)\
                    .then_inc(lru_normed, 1)
            for s in range(2):
                pool.wait_ge(mem_mm, 1 + s)
                split_plain(s, PAIR_KV + 1)
            with pool.Fori(1, NB // 2) as i:
                for s in range(2):
                    pool.wait_ge(mem_mm, i * 4)
                    split_plain(s, i * 2 + PAIR_KV)
                for s in range(2):
                    pool.wait_ge(mem_mm, i * 4 + (1 + s))
                    split_plain(s, i * 2 + (PAIR_KV + 1))
            for s in range(2):
                pool.wait_ge(mem_mm, 2 * NB)
                split_plain(s, PAIR_OUT)
            split_pairs(PAIR_OUT + 1, PAIRS, PAIR_OUT, 7 * NC)
            f = ffn["ffn2"]
            pool.wait_ge(w_mm[0], groups_before(PAIRS))
            pool.wait_ge(stored, 16 * 9)
            split_gu(f, 0, 0)
            pool.wait_ge(w_mm[1], groups_before(PAIRS))
            split_ffn(f)

        @block.tensor
        def _(pe):
            def three(out, pairs, first, last):
                ins = None
                for n, (wh, wl, ah, al) in enumerate(pairs):
                    end = last and n == len(pairs) - 1
                    pe.matmul(out, wh, ah, start=(first and n == 0), stop=False)
                    pe.matmul(out, wh, al, start=False, stop=False)
                    ins = pe.matmul(out, wl, ah, start=False, stop=end)
                return ins

            def product(out, wh, wl, c, feed):
                o, n = CH[c]
                for k in range(KT):
                    if feed:
                        pe.wait_ge(act_lo_done, SPLIT0[feed] + c * KT + k + 1)
                    ins = three(out, [(wh[:, k, :], wl[:, k, :], act_hi[:, k, o:o + n], act_lo[:, k, o:o + n])],
                                k == 0, k == KT - 1)
                return ins

            def sum_squares(key, chunks, adds, src=acc):
                pe.wait_ge(sq_used, SQ0[key] + adds)
                for c, (o, n) in enumerate(chunks):
                    if c >= 2:
                        pe.wait_ge(ssq_ev, SUM0[key] + c - 1)
                    pe.matmul(ps[:, 6 + c % 2, 0:n], ones[:, :], src[:, o:o + n], start=True, stop=True)\
                      .then_inc(ssq_mm, 1)

            def gu(f, t, s, feed=None, taken=None, norm=None):
                if feed:
                    pe.wait_ge(f["pool_own"], 2)
                else:
                    pe.wait_ge(f["gu_split"], t + 1)
                for c, (o, n) in enumerate(CH):
                    if taken:
                        taken(c)
                    product(ps[:, c, 0:n], w_hi[s], w_lo[s], c, feed).then_inc(f["gate_mm"], 1)
                    if feed and c == 0:
                        pe.wait_ge(f["gu_split"], t + 1)
                    product(ps[:, 3 + c, 0:n], up_hi[s], up_lo[s], c, None).then_inc(f["up_mm"], 1)
                    if norm and c == 0:
                        sum_squares(norm, CH, 2 * KT)

            def down(f, j, t_before, by_chunk=False):
                pe.wait_ge(f["dn_split"], j + 1)
                for n_ in range(KT * NC):
                    m, c = (n_ % KT, n_ // KT) if by_chunk else divmod(n_, NC)
                    bank = DOWN_BANKS[n_ % 8]
                    o, n = CH[c]
                    if m == 0:
                        pe.wait_ge(f["hid_lo"], j * (2 * NC) + NC + c + 1)
                    pe.wait_ge(f["dn_ev"], j * (NC * KT) + n_ + 1)
                    if n_ < 8 and bank < 6:
                        pe.wait_ge(f["gate_ev" if bank < 3 else "up_ev"], t_before * NC + bank % 3 + 1)
                    three(ps[:, bank, 0:n], [(dn_hi[s][:, m, :], dn_lo[s][:, m, :], hid_hi[s][:, o:o + n],
                                              hid_lo[s][:, o:o + n]) for s in range(2)], True, True)\
                        .then_inc(f["dn_mm"], 1)

            def ffn_layer(f, key, before, by_chunk=False):
                def after_gu(t):
                    def taken(c):
                        pe.wait_ge(f["gate_ev"], t * NC + c + 1)
                        pe.wait_ge(f["up_ev"], t * NC + c + 1)
                    return taken

                def after_down(j):
                    def taken(c):
                        at_ = max(DOWN_BANKS.index(c), DOWN_BANKS.index(3 + c))
                        pe.wait_ge(f["dn_ev"], j * (NC * KT) + (NC * KT - 8) + at_ + 1 + 8)
                    return taken

                before()
                gu(f, 0, 0, feed=key, norm=key)
                gu(f, 1, 1, taken=after_gu(0))
                with pe.Fori(1, FI) as i:
                    gu(f, i * 2, 0, taken=after_gu(i * 2 - 1))
                    down(f, i - 1, i * 2)
                    gu(f, i * 2 + 1, 1, taken=after_down(i - 1))
                down(f, FI - 1, FT - 1, by_chunk)

            def tile(stage, p, s, n0, feed=None, norm=None):
                pe.wait_ge(w_split[s], p + 1)
                for c, (o, n) in enumerate(CH):
                    pe.wait_ge(g_ev[stage], n0 + c + 1)
                    ins = product(ps[:, 3 * s + c, 0:n], w_hi[s], w_lo[s], c, feed)
                    ins.then_inc(w_mm[s], 1)
                    if norm and c == 1:
                        sum_squares(norm, CH, 2 * KT)

            def plain(stage, pair0, pairs, feed, norm=None):
                tile(stage, pair0, 0, 0, feed=feed, norm=norm)
                tile(stage, pair0, 1, NC)
                with pe.Fori(1, pairs) as i:
                    for s in range(2):
                        tile(stage, i + pair0, s, i * (2 * NC) + s * NC)

            pe.wait_ge(ones_set, 1)
            ffn_layer(ffn["ffn1"], "ffn1", lambda: None, by_chunk=True)

            def lru_gates(ct):
                pe.wait_ge(conv_back, ct + 1)
                if ct == 0:
                    pe.wait_ge(bd_in, 16)
                    pe.wait_ge(ssq_ev, SUM0["mix"] + NC)
                for j in range(2 * NC):
                    n_ = ct * 2 * NC + j
                    o, n = CH[j % NC]
                    if n_ >= 2:
                        pe.wait_ge(lru_ev, n_ - 1)
                    pe.matmul(ps[:, 6 + n_ % 2, 0:n], bd[:, ct, j // NC, :], mix[:, M_U + ct, o:o + n],
                              start=True, stop=True).then_inc(lru_mm, 1)

            plain("in", PAIR_IN, 4, "mix", norm="mix")
            for m in range(8, IN_T):
                if m < 8 + LT:
                    lru_gates(m - 8)
                tile("in", m // 2, m % 2, m * NC)
                if m == IN_T - 2:
                    sum_squares("lru", CH, 2 * LT)
                    pe.wait_ge(ssq_ev, SUM0["lru"] + NC)
            sum_squares("mem", [(0, NM)], 1, sq)

            pe.wait_ge(ssq_ev, SUM0["mem"] + 1)
            pe.wait_ge(g_ev["in"], 6 + 3 * IN_T)
            pe.wait_ge(rope_tab, 64)

            def blk(b):
                return bass.ds(b * WIN + TS, WIN)

            def rotate(b):
                if not (isinstance(b, int) and b == 0):
                    pe.wait_ge(rot_ev, b)
                if not isinstance(b, int) or b > 1:
                    pe.wait_ge(o_ev, b - 1)
                    pe.wait_ge(vt_ev, b - 1)
                    pe.wait_ge(kv_ev, b * 2 - 3)
                pe.matmul(ps[:, 6, :], rotm[:, :], mix[:, M_Q:M_Q + GRP, blk(b)], start=True, stop=True)
                pe.matmul(ps[:, 7, 0:WIN], rotm[:, :], mix[:, M_K, blk(b)], start=True, stop=True)\
                  .then_inc(rot_mm, 1)

            def scores(b, s):
                pe.wait_ge(rope_done, b + 1)
                pe.wait_ge(sc_taken, b + 1)
                for j in range(NH):
                    g, kv = divmod(j, KVH)
                    h = kv * GRP + g
                    r = slice(kv * HD, kv * HD + HD)
                    for half in range(2):
                        k = k_r[1 - s] if half == 0 else k_r[s]
                        ins = pe.matmul(ps[:, h // 2, (h % 2) * 256 + half * WIN:(h % 2) * 256 + half * WIN + WIN],
                                        q_r[r, g, :], k[r, :], start=True, stop=True)
                ins.then_inc(sc_mm, 1)

            def turn_v(b):
                pe.wait_ge(v_st, b + 1)
                pe.wait_ge(kv_ev, b * 2 + 1)
                pe.transpose(ps[:, 7, WIN:2 * WIN], v_b[:, :], ident[:, :]).then_inc(vt_mm, 1)

            def turn_p(b, s, kv):
                pe.wait_ge(pt_ev, b * 2 + kv + 1)
                for g in range(GRP):
                    for half in range(2):
                        ins = pe.transpose(ps[:, 4 + half, g * WIN:(g + 1) * WIN],
                                           s_m[s][:, kv * GRP + g, half * WIN:(half + 1) * WIN], ident[:, :])
                ins.then_inc(pt_mm, 1)

            def weigh(b, s, kv):
                pe.wait_ge(pt_ev, b * 2 + kv + 2)
                for half in range(2):
                    v = v_n[1 - s] if half == 0 else v_n[s]
                    ins = pe.matmul(ps[kv * HD:(kv + 1) * HD, 6, :], v[:, kv * HD:(kv + 1) * HD],
                                    p_T[:, half, kv * GRP:(kv + 1) * GRP, :], start=(half == 0), stop=(half == 1))
                return ins

            def memory_tile(b, s, j):
                for slot in ((j,) if s == 0 else (0, 1)):
                    pe.wait_ge(w_split[slot], b + (PAIR_KV + 1))
                pe.wait_ge(kv_ev, b * 2 + j + 1)
                out = ps[:, 7, 256:512]
                for k in range(KT):
                    if s == 0:
                        ins = three(out, [(w_hi[j][:, k, :], w_lo[j][:, k, :], memn_hi[:, k, :],
                                           memn_lo[:, k, :])], k == 0, k == KT - 1)
                    else:
                        r = slice(j * P, (j + 1) * P)
                        ins = three(out, [(memn_hi[:, k, r], memn_lo[:, k, r], w_hi2[:, :, k, :],
                                           w_lo2[:, :, k, :])], k == 0, k == KT - 1)
                ins.then_inc(mem_mm, 1)

            def block_step(b, s, more=True, rot=True):
                if more:
                    scores(b + 1, 1 - s)
                pe.wait_ge(p_done, b + 1)
                turn_p(b, s, 0)
                if rot:
                    rotate(b + 2)
                turn_p(b, s, 1)
                pe.wait_ge(vt_ev, b + 1)
                if rot:
                    pe.wait_ge(rot_ev, b + 3)
                else:
                    pe.wait_ge(o_ev, b + 1)
                memory_tile(b, s, 0)
                if not more:
                    sample_scores()
                weigh(b, s, 0)
                memory_tile(b, s, 1)
                weigh(b, s, 1).then_inc(pv_mm, 1)
                if more:
                    turn_v(b + 1)

            def sample_rotate():
                pe.wait_ge(o_ev, NB)
                pe.matmul(ps[:, 6, 0:GRP * TS], rotm[:, :], mix[:, M_Q:M_Q + GRP, 0:TS], start=True, stop=True)
                pe.matmul(ps[:, 6, 256:256 + TS], rotm[:, :], mix[:, M_K, 0:TS], start=True, stop=True)\
                  .then_inc(s_rot_mm, 1)
                pe.wait_ge(pt_ev, NB * 2 - 1)
                for b in range(NS):
                    pe.transpose(ps[0:LS, 4 + b // 4, (b % 4) * P:(b % 4 + 1) * P],
                                 mix[:, M_V, b * LS:(b + 1) * LS], ident[:, :]).then_inc(s_rot_mm, 1)
                pe.wait_ge(s_pt_ev, 1)

            def sample_scores():
                pe.wait_ge(kvc_in, 48)
                pe.wait_ge(s_rope, 1)
                pe.wait_ge(sc_taken, NB + 1)
                for b in range(NS):
                    for kv in range(KVH):
                        r = slice(kv * HD, kv * HD + HD)
                        q = qs_r[r, b, :, :]
                        out = ps[32 * (b % 4):32 * (b % 4) + 32, (b // 4) * 2 + kv, 0:WIN + LS]
                        pe.matmul(out[:, 0:WIN], q, kc_T[r, b, :], start=True, stop=True)
                        ins = pe.matmul(out[:, WIN:WIN + LS], q, ks_r[r, b * LS:(b + 1) * LS], start=True, stop=True)
                ins.then_inc(s_sc_mm, 1)

            rotate(0)
            scores(0, 0)
            rotate(1)
            pe.wait_ge(rot_ev, 2)
            turn_v(0)
            pe.wait_ge(memn_lo_done, 1)
            with pe.Fori(0, NB // 2 - 1) as i:
                block_step(i * 2, 0)
                block_step(i * 2 + 1, 1)
            block_step(NB - 2, 0, rot=False)
            sample_rotate()
            block_step(NB - 1, 1, more=False, rot=False)

            pe.wait_ge(s_p, 1)
            for t in range(4):
                pe.transpose(ps[:, 2, t * P:(t + 1) * P], ss_m[:, t, 0:WIN], ident[:, :])
                ins = pe.transpose(ps[0:LS, 3, t * P:(t + 1) * P], ss_m[:, t, WIN:WIN + LS], ident[:, :])
            ins.then_inc(s_pt_mm, 1)
            pe.wait_ge(s_pt_ev, 3)
            pe.wait_ge(o_ev, NB + 1)
            for b in range(NS):
                for kv in range(KVH):
                    t, j = (b // 4) * 2 + kv, b % 4
                    r = slice(kv * HD, kv * HD + HD)
                    out = ps[r, 6, b * 32:(b + 1) * 32]
                    pe.matmul(out, v_c[:, b, r], pcs_T[:, t, 32 * j:32 * j + 32], start=True, stop=False)
                    ins = pe.matmul(out, vs_n[:, b, r], pns_T[:, t, 32 * j:32 * j + 32], start=False, stop=True)
            ins.then_inc(s_pv_mm, 1)
            sum_squares("attn", CH, 2 * LT)

            plain("out", PAIR_OUT, 4, "cat")
            plain("cq", PAIR_CQ, 4, "xattn", norm="xattn")

            pe.wait_ge(x_tab, 16)
            pe.wait_ge(g_ev["cq"], 6 + NC * KT)

            def x_scores(b, half, s):
                pe.wait_ge(xq_st, b + 1)
                pe.wait_ge(x_exp, b + 1)
                for h in range(XH):
                    for d in range(2):
                        pe.matmul(ps[:, h // 2, (h % 2) * NM:(h % 2 + 1) * NM], xq_b[:, 2 * h + d, :],
                                  mem_kT[:, 2 * h + d, :], start=(d == 0), stop=(d == 1))
                pe.wait_ge(ck_in[s], half * 16 + 16)
                for h in range(XH):
                    for d in range(2):
                        ins = pe.matmul(ps[32 * h:32 * h + 32, 2, 0:NM], qs_b[:, 2 * h + d, :],
                                        ck_T[s][:, 2 * h + d, :], start=(d == 0), stop=(d == 1))
                ins.then_inc(x_sc_mm, 1)

            def back():
                for d in range(2):
                    ins = pe.transpose(ps[:, 5, NM + d * P:NM + (d + 1) * P], y_s[:, d * P:(d + 1) * P], x_id[:, :])
                return ins

            def x_turn(b, s, after=True):
                pe.wait_ge(x_p, b + 1)
                pe.wait_ge(x_pt_ev, b + 1)
                for h in range(XH):
                    for mt in range(2):
                        ins = pe.transpose(ps[:, 3 + mt, h * P:(h + 1) * P], xs_m[s][:, h, mt * P:(mt + 1) * P],
                                           x_id[:, :])
                ins.then_inc(x_turned, 1)
                if after:
                    pe.wait_ge(y_ev, b)
                    back()
                for mt in range(2):
                    ins = pe.transpose(ps[:, 5, mt * P:(mt + 1) * P], ys_m[s][:, mt * P:(mt + 1) * P], x_id[:, :])
                ins.then_inc(x_pt_mm, 1)

            def x_weigh(b, half, s):
                pe.wait_ge(x_pt_ev, b + 2)
                pe.wait_ge(cv_in[s], half * 16 + 16)
                for mt in range(2):
                    for h in range(XH):
                        ins = pe.matmul(ps[32 * h:32 * h + 32, 5, NM:2 * NM], yp_T[:, mt, 32 * h:32 * h + 32],
                                        cv_n[s][:, mt, h * XD:(h + 1) * XD], start=(mt == 0), stop=(mt == 1))
                ins.then_inc(y_mm, 1)
                pe.wait_ge(x_o_ev, b + 1)
                for kt in range(KT):
                    for mt in range(2):
                        ins = pe.matmul(ps[:, 6 + kt // 4, (kt % 4) * P:(kt % 4 + 1) * P],
                                        mem_v[:, mt, kt * P:(kt + 1) * P], xp_T[:, mt, kt // 2, :],
                                        start=(mt == 0), stop=(mt == 1))
                ins.then_inc(x_pv_mm, 1)

            def x_step(b, half, s, more=True, after=True):
                if more:
                    x_scores(b + 1, half + s, 1 - s)
                x_turn(b, s, after)
                x_weigh(b, half, s)

            x_scores(0, 0, 0)
            x_step(0, 0, 0, after=False)
            x_step(1, 0, 1)
            with pe.Fori(1, NB // 2 - 1) as i:
                x_step(i * 2, i, 0)
                x_step(i * 2 + 1, i, 1)
            x_step(NB - 2, NB // 2 - 1, 0)
            x_step(NB - 1, NB // 2 - 1, 1, more=False)
            pe.wait_ge(y_ev, NB)
            back().then_inc(x_pt_mm, 1)

            plain("co", PAIR_CO, 4, "co")
            ffn_layer(ffn["ffn2"], "ffn2", lambda: pe.wait_ge(g_ev["co"], 6 + NC * KT))
            sum_squares("final", CH, 2 * KT)

        @block.scalar
        def _(act):
            def squares(key, tiles, src, ready):
                for m in range(tiles):
                    square(key, m, src(m), ready)

            def square(key, m, src, ready):
                ready(m)
                for h, (o, n) in enumerate(HALVES):
                    if not (isinstance(m, int) and m == 0):
                        act.wait_ge(sq_used, m * 2 + (SQ0[key] + h - 1))
                    act.activation(sq[:, o:o + n], src[:, o:o + n], ACT.Square).then_inc(sq_done, 1)

            def rms(key, chunks=CH, of=rstd):
                for c, (o, n) in enumerate(chunks):
                    act.wait_ge(ssq_ev, SUM0[key] + c + 1)
                    act.activation(of[:, o:o + n], of[:, o:o + n], ACT.Sqrt).then_inc(rms_done, 1)

            def hi_parts(key, src, gain=None, ready=None):
                for c, (o, n) in enumerate(CH):
                    if ready:
                        ready(c)
                    for k in range(KT):
                        act.activation(act_hi[:, k, o:o + n], src(k)[:, o:o + n], ACT.Copy,
                                       scale=c_(gain, k) if gain else 1.0).then_inc(act_hi_done, 1)

            def ffn_tile(f, t, s, down_done):
                for c, (o, n) in enumerate(CH):
                    act.wait_ge(f["gate_ev"], t * NC + c + 1)
                    act.activation(gate_t[:, o:o + n], gate_t[:, o:o + n], ACT.Silu).then_inc(f["silu"], 1)
                if down_done is not None:
                    act.wait_ge(f["dn_mm"], down_done)
                for c, (o, n) in enumerate(CH):
                    act.wait_ge(f["hid_f"], t * NC + c + 1)
                    act.activation(hid_hi[s][:, o:o + n], hid_t[:, o:o + n], ACT.Copy).then_inc(f["hid_hi"], 1)

            def lru_parameters():
                act.wait_ge(lru_sp, 1)
                act.activation(lrup[:, 2, :], lrup[:, 2, :], ACT.Exp, scale=-1.0).then_inc(lru_sp, 1)

            def ffn_layer(f, between=lambda: None):
                ffn_tile(f, 0, 0, None)
                ffn_tile(f, 1, 1, None)
                between()
                with act.Fori(1, FI) as i:
                    ffn_tile(f, i * 2, 0, i * (NC * KT))
                    ffn_tile(f, i * 2 + 1, 1, i * (NC * KT))

            def x_tile(k):
                return x[:, k, :]

            act.wait_ge(cst_in, 16)
            hi_parts("ffn1", x_tile, "g_ffn1", ready=lambda c: act.wait_ge(x_in[c], 16))
            squares("ffn1", KT, x_tile, lambda m: None)
            rms("ffn1")
            ffn_layer(ffn["ffn1"], lru_parameters)
            hi_parts("mix", x_tile, "g_mix",
                     ready=lambda c: act.wait_ge(ffn["ffn1"]["dn_ev"], 8 + (FI - 1) * NC * KT + KT * (c + 1)))
            squares("mix", KT, x_tile, lambda m: None)
            rms("mix")

            for ct in range(LT):
                act.wait_ge(conv_done, ct + 1)
                act.activation(mix[:, M_U + ct, :], t_conv[:, :], ACT.Copy).then_inc(conv_back, 1)
            act.wait_ge(g_ev["in"], 6 + 8 * NC)
            act.activation(mix[:, M_G:M_G + LT, :], mix[:, M_G:M_G + LT, :], ACT.Gelu_apprx_tanh)\
               .then_inc(gate_gelu, 1)
            for ct in range(LT):
                if ct:
                    act.wait_ge(lru_y, ct)
                for j in range(2 * NC):
                    n_ = ct * 2 * NC + j
                    o, n = CH[j % NC]
                    act.wait_ge(lru_mm, n_ + 1)
                    gate, bias = (t_a, "b_a") if j < NC else (t_b, "b_i")
                    act.activation(gate[:, o:o + n], ps[:, 6 + n_ % 2, 0:n], ACT.Sigmoid, bias=c_(bias, ct))\
                       .then_inc(lru_ev, 1)
                act.wait_ge(lru_ev, ct * 2 * NC + NC)
                act.activation(t_conv[:, :], t_a[:, :], ACT.Tanh, scale=lrup[:, 6, ct:ct + 1]).then_inc(lru_th, 1)
                act.activation(t_a[:, :], t_a[:, :], ACT.Exp, scale=lrup[:, 7, ct:ct + 1]).then_inc(lru_a, 1)
                act.wait_ge(lru_q, ct + 1)
                act.activation(t_conv[:, :], t_conv[:, :], ACT.Sqrt).then_inc(lru_s, 1)
            act.wait_ge(lru_y, LT)
            act.dma_start(t_out["small"], small[:, :]).then_inc(stored, 16)
            squares("lru", LT, lambda m: mix[:, M_U + m, :], lambda m: None)
            act.wait_ge(mem_in, 16)
            act.activation(mem_sq[:, :, :], mem_raw[:, :, :], ACT.Square).then_inc(sq_done, 1)
            rms("lru", of=lru_rstd)
            rms("mem", [(0, NM)], of=acc)
            act.wait_ge(mem_normed, 1)
            act.wait_ge(w_mm[1], groups_before(PAIR_KV))
            act.activation(memn_hi[:, :, :], mem_raw[:, :, :], ACT.Copy).then_inc(memn_hi_done, 1)

            def exps(b, s):
                act.wait_ge(nmax_done, b + 1)
                for h in range(NH):
                    act.activation(s_m[s][:, h, :], s_m[s][:, h, :], ACT.Exp, bias=st8[:, 1, h:h + 1],
                                   scale=HD ** -0.5, accum_out=st8[:, 4, h:h + 1])
                act.activation(st8[:, 3, :], st8[:, 2, :], ACT.Exp).then_inc(exp_done, 1)

            def take_v(b, s):
                act.wait_ge(vt_mm, b + 1)
                act.activation(v_n[s][:, :], ps[:, 7, WIN:2 * WIN], ACT.Copy).then_inc(vt_ev, 1)

            def block_step(b, s, more=True):
                for kv in range(KVH):
                    act.wait_ge(pt_mm, b * 2 + kv + 1)
                    act.activation(p_T[:, :, kv * GRP:(kv + 1) * GRP, :], ps[:, 4:6, :], ACT.Copy)\
                       .then_inc(pt_ev, 1)
                if more:
                    exps(b + 1, 1 - s)
                    take_v(b + 1, 1 - s)

            act.sem_inc(pt_ev, 1)
            exps(0, 0)
            take_v(0, 0)
            with act.Fori(0, NB // 2 - 1) as i:
                block_step(i * 2, 0)
                block_step(i * 2 + 1, 1)
            block_step(NB - 2, 0)
            act.wait_ge(rope_done, NB)
            act.wait_ge(vt_ev, NB)
            act.dma_start(t_out["k_prompt"], k_r[1][:, :]).then_inc(stored, 16)
            act.dma_start(t_out["v_prompt"], v_n[1][:, :]).then_inc(stored, 16)
            act.wait_ge(s_rot_mm, 1 + NS)
            act.activation(vs_n[:, :, :], ps[0:LS, 4:6, :], ACT.Copy).then_inc(s_pt_ev, 1)
            block_step(NB - 1, 1, more=False)
            act.wait_ge(s_rope, 1)
            act.dma_start(t_out["k_sample"][:, :, 0:WIN - LS], kc_T[:, :, LS:WIN]).then_inc(stored, 16)
            act.dma_start(t_out["k_sample"][:, :, WIN - LS:WIN], ks_r[:, :].rearrange("p (b t) -> p b t", b=NS))\
               .then_inc(stored, 16)
            act.dma_start(t_out["v_sample"][0:WIN - LS, :, :], v_c[LS:WIN, :, :]).then_inc(stored, 16)
            act.wait_ge(s_pt_ev, 1)
            act.dma_start(t_out["v_sample"][WIN - LS:WIN, :, :], vs_n[:, :, :]).then_inc(stored, 16)
            act.wait_ge(s_nmax, 1)
            for t in range(4):
                act.activation(ss_m[:, t, :], ss_m[:, t, :], ACT.Exp, bias=st8[:, 1, t:t + 1], scale=HD ** -0.5,
                               accum_out=st8[:, 4, t:t + 1])
            act.activation(st8[:, 3, 0:4], st8[:, 2, 0:4], ACT.Exp).then_inc(s_exp, 1)
            act.wait_ge(s_pt_mm, 1)
            act.activation(pcs_T[:, :, :], ps[:, 2, :], ACT.Copy).then_inc(s_pt_ev, 1)
            act.activation(pns_T[:, :, :], ps[0:LS, 3, :], ACT.Copy).then_inc(s_pt_ev, 1)

            def cat_tile(k):
                return mix[:, M_U + k, :] if k < LT else mix[:, M_Q + k - LT, :]

            act.wait_ge(s_o_ev, 1)
            act.wait_ge(stored, 16 * 7)
            squares("attn", LT, lambda m: mix[:, M_Q + m, :], lambda m: None)
            rms("attn")
            act.wait_ge(lru_normed, LT)
            hi_parts("cat", cat_tile, "g_cat", ready=lambda c: act.wait_ge(attn_normed, c + 1))
            act.dma_start(t_out["mem_k"], mem_kT[:, :, :]).then_inc(stored, 16)
            act.dma_start(t_out["mem_v"], mem_v[:, :, :]).then_inc(stored, 16)

            def plain_squares(stage, key):
                def ready(m):
                    act.wait_ge(g_ev[stage], m * NC + (6 + NC))
                for m in range(2):
                    square(key, m, x[:, m, :], ready)
                with act.Fori(2, KT) as m:
                    square(key, m, x[:, m, :], ready)

            plain_squares("out", "xattn")
            act.wait_ge(w_mm[1], groups_before(PAIR_CQ))
            hi_parts("xattn", x_tile, "g_xattn")
            rms("xattn")

            def x_exps(b, s):
                act.wait_ge(x_nmax, b + 1)
                for h in range(XH):
                    act.activation(xs_m[s][:, h, :], ps[:, h // 2, (h % 2) * NM:(h % 2 + 1) * NM], ACT.Exp,
                                   bias=xst[:, s, 1, h:h + 1], scale=XD ** -0.5, accum_out=xst[:, s, 2, h:h + 1])
                act.activation(ys_m[s][:, :], ps[:, 2, 0:NM], ACT.Exp, bias=yst[:, s * 4 + 1:s * 4 + 2],
                               scale=XD ** -0.5, accum_out=yst[:, s * 4 + 2:s * 4 + 3]).then_inc(x_exp, 1)

            def y_back(b):
                return act.activation(
                    xq[:, :, bass.ds(b * LS, LS)],
                    ps[:, 5, NM:2 * NM].rearrange("p (d w) -> p d w", d=2)[:, :, 0:P]
                    .rearrange("p d (h w) -> p h d w", h=XH)[:, :, :, 0:LS], ACT.Copy)

            def x_step(b, s, more=True, after=True):
                act.wait_ge(x_turned, b + 1)
                act.activation(xp_T[:, :, :, :], ps[:, 3:5, :], ACT.Copy)
                act.wait_ge(x_pt_mm, b + 1)
                if after:
                    y_back(b - 1)
                act.activation(yp_T[:, :, :], ps[:, 5, 0:2 * P], ACT.Copy).then_inc(x_pt_ev, 1)
                if more:
                    x_exps(b + 1, 1 - s)
                act.wait_ge(y_mm, b + 1)
                act.activation(y_s[:, :], ps[:, 5, NM:2 * NM], ACT.Copy).then_inc(y_ev, 1)

            act.sem_inc(x_exp, 1)
            act.sem_inc(x_pt_ev, 1)
            x_exps(0, 0)
            x_step(0, 0, after=False)
            x_step(1, 1)
            with act.Fori(1, NB // 2 - 1) as i:
                x_step(i * 2, 0)
                x_step(i * 2 + 1, 1)
            x_step(NB - 2, 0)
            x_step(NB - 1, 1, more=False)
            act.wait_ge(x_pt_mm, NB + 1)
            y_back(NB - 1).then_inc(y_ev, 1)
            act.wait_ge(y_ev, NB + 1)

            act.wait_ge(x_pv_mm, NB)
            act.wait_ge(x_o_ev, 1 + NB)
            hi_parts("co", lambda k: xq[:, k, :])
            plain_squares("co", "ffn2")
            act.wait_ge(w_mm[1], groups_before(PAIRS))
            hi_parts("ffn2", x_tile, "g_ffn2")
            rms("ffn2")
            act.wait_ge(stored, 16 * 9)
            ffn_layer(ffn["ffn2"])
            squares("final", KT, x_tile,
                    lambda m: act.wait_ge(ffn["ffn2"]["dn_ev"], 8 + (FI - 1) * NC * KT + NC * (m + 1)))
            rms("final")
            for c, (o, n) in enumerate(CH):
                act.wait_ge(y_done, c + 1)
                act.dma_start(t_out["y"][:, :, o:o + n], y[:, :, o:o + n]).then_inc(stored, 16)
            act.wait_ge(stored, 16 * (9 + NC))

        @block.vector
        def _(dve):
            own = Steps(dve, dve_own)

            def take_out(out, src):
                return dve.tensor_scalar(out, src, 1.0, None, ALU.mult)

            def add_square(key, m):
                for h, (o, n) in enumerate(HALVES):
                    dve.wait_ge(sq_done, m * 2 + (SQ0[key] + h + 1))
                    if isinstance(m, int) and m == 0:
                        dve.tensor_copy(acc[:, o:o + n], sq[:, o:o + n]).then_inc(sq_used, 1)
                    else:
                        dve.wait_ge(sq_used, m * 2 + (SQ0[key] + h - 1))
                        dve.tensor_tensor(acc[:, o:o + n], acc[:, o:o + n], sq[:, o:o + n], ALU.add)\
                           .then_inc(sq_used, 1)

            def inverse_rms(key, width, chunks=CH, then=None, to=rstd):
                for c, (o, n) in enumerate(chunks):
                    dve.wait_ge(ssq_mm, SUM0[key] + c + 1)
                    dve.tensor_scalar(to[:, o:o + n], ps[:, 6 + c % 2, 0:n], 1.0 / width, EPS, ALU.mult, ALU.add)\
                       .then_inc(ssq_ev, 1)
                for c, (o, n) in enumerate(chunks):
                    dve.wait_ge(rms_done, SUM0[key] + c + 1)
                    dve.reciprocal(to[:, o:o + n], to[:, o:o + n]).then_inc(rstd_done, 1)
                    if then or c == len(chunks) - 1:
                        dve.wait_ge(rstd_done, SUM0[key] + c + 1)
                    if then:
                        then(c)

            def lo_parts(key, src, gain=None, chunks=range(NC)):
                for c in chunks:
                    o, n = CH[c]
                    for k in range(KT):
                        dve.wait_ge(act_hi_done, SPLIT0[key] + c * KT + k + 1)
                        hi = act_hi[:, k, o:o + n].bitcast(F32)
                        if gain:
                            ins = dve.scalar_tensor_tensor(out=act_lo[:, k, o:o + n], in0=src(k)[:, o:o + n],
                                                           scalar=c_(gain, k), in1=hi, op0=ALU.mult,
                                                           op1=ALU.subtract)
                        else:
                            ins = dve.tensor_tensor(act_lo[:, k, o:o + n], src(k)[:, o:o + n], hi, ALU.subtract)
                        ins.then_inc(act_lo_done, 1)

            def ffn_hidden(f, t):
                def gate(c):
                    o, n = CH[c]
                    dve.wait_ge(f["gate_mm"], t * NC + c + 1)
                    dve.tensor_tensor(gate_t[:, o:o + n], ps[:, c, 0:n], rstd[:, o:o + n], ALU.mult)\
                       .then_inc(f["gate_ev"], 1)

                def up(c):
                    o, n = CH[c]
                    dve.wait_ge(f["up_mm"], t * NC + c + 1)
                    dve.wait_ge(f["silu"], t * NC + c + 1)
                    dve.tensor_tensor(hid_t[:, o:o + n], ps[:, 3 + c, 0:n], gate_t[:, o:o + n], ALU.mult)\
                       .then_inc(f["up_ev"], 1)
                    dve.wait_ge(f["up_ev"], t * NC + c + 1)
                    dve.tensor_tensor(hid_t[:, o:o + n], hid_t[:, o:o + n], rstd[:, o:o + n], ALU.mult)\
                       .then_inc(f["hid_f"], 1)

                gate(0)
                gate(1)
                up(0)
                gate(2)
                up(1)
                up(2)

            def ffn_lo(f, t, s):
                for c, (o, n) in enumerate(CH):
                    dve.wait_ge(f["hid_hi"], t * NC + c + 1)
                    dve.tensor_tensor(hid_lo[s][:, o:o + n], hid_t[:, o:o + n],
                                      hid_hi[s][:, o:o + n].bitcast(F32), ALU.subtract).then_inc(f["hid_lo"], 1)

            def ffn_take(f, j, m, c, n_):
                o, n = CH[c]
                dve.wait_ge(f["dn_mm"], j * (NC * KT) + (n_ + 1))
                dve.scalar_tensor_tensor(out=x[:, m, o:o + n], in0=ps[:, DOWN_BANKS[n_ % 8], 0:n], scalar=0.5,
                                         in1=x[:, m, o:o + n], op0=ALU.mult, op1=ALU.add).then_inc(f["dn_ev"], 1)

            def ffn_layer(f, key, between=lambda: None):
                inverse_rms(key, D)
                dve.sem_inc(f["dn_ev"], 8)
                for t in range(2):
                    ffn_hidden(f, t)
                    ffn_lo(f, t, t)
                between()
                with dve.Fori(1, FI) as i:
                    ffn_hidden(f, i * 2)
                    dve.wait_ge(f["dn_ev"], i * (NC * KT) + (8 - NC * KT))
                    for n_ in range(NC * KT):
                        ffn_take(f, i - 1, n_ // NC, n_ % NC, n_)
                    ffn_lo(f, i * 2, 0)
                    ffn_hidden(f, i * 2 + 1)
                    ffn_lo(f, i * 2 + 1, 1)
                dve.wait_ge(f["dn_ev"], (FI - 1) * NC * KT + 8)

            def x_tile(k):
                return x[:, k, :]

            def scaled_take(stage, s, p, dst):
                for c, (o, n) in enumerate(CH):
                    dve.wait_ge(w_mm[s], slot_groups(stage, p, c))
                    dve.tensor_tensor(dst[:, o:o + n], ps[:, 3 * s + c, 0:n], rstd[:, o:o + n], ALU.mult)\
                       .then_inc(g_ev[stage], 1)

            def slot_groups(stage, p, c):
                a, _, base, each = GROUPS[0] if stage == "in" else GROUPS[2]
                return p * each + (base - a * each + c + 1)

            dve.memset(ones[:, :], 1.0).then_inc(ones_set, 1)
            dve.wait_ge(cst_in, 16)
            lo_parts("ffn1", x_tile, "g_ffn1")
            for m in range(KT):
                add_square("ffn1", m)

            def lru_parameters():
                lam, neg, e, den, z, z2, ser = (c_("lam", 0, LT), lrup[:, 1, :], lrup[:, 2, :], lrup[:, 3, :],
                                                lrup[:, 0, :], lrup[:, 4, :], lrup[:, 5, :])
                own.done(dve.tensor_scalar(neg, lam, -1.0, None, ALU.mult))
                dve.tensor_tensor(e, lam, neg, ALU.max).then_inc(lru_sp, 1)
                dve.wait_ge(lru_sp, 2)
                own.done(dve.tensor_scalar(den, e, 2.0, None, ALU.add))
                own.done(dve.reciprocal(den, den))
                own.done(dve.tensor_tensor(z, e, den, ALU.mult))
                own.done(dve.tensor_tensor(z2, z, z, ALU.mult))
                own.done(dve.tensor_scalar(ser, z2, 1.0 / 17, 1.0 / 15, ALU.mult, ALU.add))
                for k in (13, 11, 9, 7, 5, 3, 1):
                    own.done(dve.tensor_tensor(ser, ser, z2, ALU.mult))
                    own.done(dve.tensor_scalar(ser, ser, 1.0 / k, None, ALU.add))
                own.done(dve.tensor_tensor(ser, ser, z, ALU.mult))
                own.done(dve.tensor_scalar(ser, ser, 16.0, None, ALU.mult))
                own.done(dve.tensor_scalar(neg, neg, 0.0, 8.0, ALU.max, ALU.mult))
                own.done(dve.tensor_tensor(lrup[:, 6, :], ser, neg, ALU.add))
                own.done(dve.tensor_scalar(lrup[:, 7, :], lrup[:, 6, :], -1.0, None, ALU.mult))

            ffn_layer(ffn["ffn1"], "ffn1", lru_parameters)
            for c in range(NC):
                for m in range(KT):
                    ffn_take(ffn["ffn1"], FI - 1, m, c, c * KT + m)
                dve.wait_ge(ffn["ffn1"]["dn_ev"], (FI - 1) * NC * KT + 8 + (c + 1) * KT)
                if c == NC - 1:
                    dve.sem_inc(g_ev["in"], 6)
                lo_parts("mix", x_tile, "g_mix", [c])
            for m in range(KT):
                add_square("mix", m)
            inverse_rms("mix", D)

            def take_in(a, b):
                with dve.Fori(a, b) as p:
                    for s in range(2):
                        scaled_take("in", s, p, mix[:, bass.ds(p * 2 + s, 1), :].squeeze(1))

            take_in(0, 2)

            own.base, own.n = own.base + own.n, 0
            dve.wait_ge(g_ev["in"], 6 + 4 * NC)
            for ct in range(LT):
                u = mix[:, M_U + ct, :]
                us = u[:, 0:TS].rearrange("p (b t) -> p b t", b=NS)
                cs = t_conv[:, 0:TS].rearrange("p (b t) -> p b t", b=NS)
                o, _ = COLS["hist"]
                hist = cst[:, o + ct * NS * 3:o + (ct + 1) * NS * 3].rearrange("p (b t) -> p b t", b=NS)
                if ct:
                    dve.wait_ge(conv_back, ct)
                dve.tensor_copy(small[:, SM_CP + ct * 3:SM_CP + ct * 3 + 3], u[:, T - 3:T])
                dve.tensor_copy(small[:, SM_CS + ct * NS * 3:SM_CS + (ct + 1) * NS * 3]
                                .rearrange("p (b t) -> p b t", b=NS), us[:, :, LS - 3:LS])
                own.done(dve.tensor_scalar(t_conv[:, :], u, c_("conv_w", 3 * LT + ct), c_("conv_b", ct), ALU.mult,
                                           ALU.add))
                for d in (1, 2, 3):
                    w = c_("conv_w", (3 - d) * LT + ct)
                    parts = [(t_conv[:, TS + d:T], u[:, TS:T - d]), (cs[:, :, d:LS], us[:, :, 0:LS - d]),
                             (cs[:, :, 0:d], hist[:, :, 3 - d:3])]
                    for n_, (to, src) in enumerate(parts):
                        ins = dve.scalar_tensor_tensor(out=to, in0=src, scalar=w, in1=to, op0=ALU.mult, op1=ALU.add)
                        if d == 3 and n_ == 2:
                            ins.then_inc(conv_done, 1)
                        else:
                            own.done(ins)
            take_in(2, 4)

            def lru_gated(ct):
                u = mix[:, M_U + ct, :]
                dve.wait_ge(lru_ev, (ct + 1) * 2 * NC)
                own.done(dve.tensor_tensor(t_b[:, :], t_b[:, :], u, ALU.mult))
                dve.wait_ge(lru_a, ct + 1)
                own.done(dve.tensor_tensor(u, t_a[:, :], t_a[:, :], ALU.mult))
                dve.wait_ge(lru_th, ct + 1)
                dve.scalar_tensor_tensor(out=t_conv[:, :], in0=u, scalar=1.0, in1=t_conv[:, :], op0=ALU.add,
                                         op1=ALU.mult).then_inc(lru_q, 1)

            def lru_scan(ct):
                u, g = mix[:, M_U + ct, :], mix[:, M_G + ct, :]
                tmp = small[:, SM_HS + ct * NS:SM_HS + (ct + 1) * NS]
                own.done(dve.tensor_tensor(tmp, t_a[:, 0:TS:LS], c_("h0", ct * NS, NS), ALU.mult))
                own.done(dve.memset(t_a[:, 0:TS + 1:LS], 0.0))
                dve.wait_ge(lru_s, ct + 1)
                own.done(dve.tensor_tensor(t_b[:, :], t_conv[:, :], t_b[:, :], ALU.mult))
                own.done(dve.tensor_tensor(t_b[:, 0:TS:LS], t_b[:, 0:TS:LS], tmp, ALU.add))
                own.done(dve.tensor_tensor_scan(u, t_a[:, :], t_b[:, :], 0.0, ALU.mult, ALU.add))
                own.done(dve.tensor_copy(tmp, u[:, LS - 1:TS:LS]))
                own.done(dve.tensor_copy(small[:, SM_HP + ct:SM_HP + ct + 1], u[:, T - 1:T]))
                if ct == 0:
                    dve.wait_ge(gate_gelu, 1)
                dve.tensor_tensor(u, u, g, ALU.mult).then_inc(lru_y, 1)

            for ct in range(LT):
                lru_gated(ct)
                if ct:
                    scaled_take("in", (ct - 1) % 2, (7 + ct) // 2, mix[:, 7 + ct, :])
                lru_scan(ct)
            scaled_take("in", 1, 5, mix[:, 11, :])
            for ct in range(LT):
                add_square("lru", ct)
            scaled_take("in", 0, 6, mix[:, 12, :])
            inverse_rms("lru", LRU, to=lru_rstd)

            dve.wait_ge(sq_done, SQ0["mem"] + 1)
            dve.tensor_reduce(sq[:, 0:NM], mem_sq[:, :, :].rearrange("p k t -> p t k"), AX_X, ALU.add)\
               .then_inc(sq_used, 1)
            inverse_rms("mem", D, [(0, NM)], to=acc)
            for k in range(KT):
                ins = dve.scalar_tensor_tensor(out=mem_raw[:, k, :], in0=mem_raw[:, k, :], scalar=c_("g_mem", k),
                                               in1=acc[:, 0:NM], op0=ALU.mult, op1=ALU.mult)
            ins.then_inc(mem_normed, 1)
            scaled_take("in", 1, 6, mix[:, 13, :])
            dve.wait_ge(memn_hi_done, 1)
            dve.tensor_tensor(memn_lo[:, :, :], mem_raw[:, :, :], memn_hi[:, :, :].bitcast(F32), ALU.subtract)\
               .then_inc(memn_lo_done, 1)

            dve.memset(k_r[1][:, :], 0.0)
            own.done(dve.memset(v_n[1][:, :], 0.0))
            own.done(dve.tensor_scalar(st8[:, 7, :], c_("sink", 0, NH), HD ** 0.5, None, ALU.mult))
            dve.sem_inc(sc_taken, 1)
            dve.sem_inc(o_ev, 1)
            dve.sem_inc(kv_ev, 1)
            dve.wait_ge(rope_tab, 64)

            def blk(b):
                return bass.ds(b * WIN + TS, WIN)

            def over(ap, n, w):
                return ap.unsqueeze(1).to_broadcast([P, n, w])

            def rope_read(b):
                sin = rope_sin[:, blk(b)]
                dve.wait_ge(rot_mm, b + 1)
                dve.tensor_tensor(rot_q[:, :, :], ps[:, 6, :].rearrange("p (g w) -> p g w", g=GRP),
                                  over(sin, GRP, WIN), ALU.mult)
                dve.tensor_tensor(rot_k[:, :], ps[:, 7, 0:WIN], sin, ALU.mult).then_inc(rot_ev, 1)

            def rope(b, s, steps):
                cos = rope_cos[:, blk(b)]
                dve.tensor_tensor(q_r[:, :, :], mix[:, M_Q:M_Q + GRP, blk(b)], over(cos, GRP, WIN), ALU.mult)
                steps.done(dve.tensor_tensor(k_r[s][:, :], mix[:, M_K, blk(b)], cos, ALU.mult))
                dve.wait_ge(rot_ev, b + 1)
                dve.tensor_tensor(q_r[:, :, :], q_r[:, :, :], rot_q[:, :, :], ALU.add)
                dve.tensor_tensor(k_r[s][:, :], k_r[s][:, :], rot_k[:, :], ALU.add).then_inc(rope_done, 1)

            def add_mask(b, s, mask):
                dve.wait_ge(sc_mm, b + 1)
                dve.tensor_tensor(s_m[s][:, :, :], ps[:, 0:4, :].rearrange("p a (h w) -> p (a h) w", w=2 * WIN),
                                  over(mask, NH, 2 * WIN), ALU.add).then_inc(sc_taken, 1)

            def maxima(b, s, steps):
                dve.wait_ge(sc_taken, b + 2)
                steps.done(dve.tensor_reduce(st8[:, 0, :], s_m[s][:, :, :], AX_X, ALU.max))
                steps.done(dve.tensor_tensor(st8[:, 0, :], st8[:, 0, :], st8[:, 7, :], ALU.max))
                steps.done(dve.tensor_scalar(st8[:, 1, :], st8[:, 0, :], -(HD ** -0.5), None, ALU.mult))
                dve.tensor_tensor(st8[:, 2, :], st8[:, 1, :], c_("sink", 0, NH), ALU.add).then_inc(nmax_done, 1)

            def probabilities(b, s, steps):
                dve.wait_ge(exp_done, b + 1)
                steps.done(dve.tensor_tensor(st8[:, 5, :], st8[:, 3, :], st8[:, 4, :], ALU.add))
                steps.done(dve.reciprocal(st8[:, 6, :], st8[:, 5, :]))
                dve.tensor_tensor(s_m[s][:, :, :], s_m[s][:, :, :],
                                  st8[:, 6, :].unsqueeze(2).to_broadcast([P, NH, 2 * WIN]), ALU.mult)\
                   .then_inc(p_done, 1)

            def stage_v(b):
                if not (isinstance(b, int) and b == 0):
                    dve.wait_ge(vt_mm, b)
                take_out(v_b[:, :], mix[:, M_V, blk(b)]).then_inc(v_st, 1)

            ROPE_STEPS, SWA_STEPS = 1, 5

            def take_memory(b, s, j):
                dve.wait_ge(mem_mm, b * 2 + j + 1)
                if s == 0:
                    to = mem_kT[:, bass.ds(b + j, 1), :].squeeze(1)
                else:
                    to = mem_v[:, j, bass.ds(b * P - P, 2 * P)]
                take_out(to, ps[:, 7, 256:512]).then_inc(kv_ev, 1)

            def take_result(b):
                dve.wait_ge(pv_mm, b + 1)
                take_out(mix[:, M_Q:M_Q + GRP, blk(b)], ps[:, 6, :].rearrange("p (g w) -> p g w", g=GRP))\
                    .then_inc(o_ev, 1)

            def block_step(b, s, rot=True):
                steps = Steps(dve, swa_own, b * (ROPE_STEPS + SWA_STEPS) + (2 * ROPE_STEPS + SWA_STEPS))
                add_mask(b + 1, 1 - s, masks[:, 1, :])
                if rot:
                    rope_read(b + 2)
                maxima(b + 1, 1 - s, steps)
                if rot:
                    rope(b + 2, s, steps)
                stage_v(b + 1)
                for j in range(2):
                    take_memory(b, s, j)
                probabilities(b + 1, 1 - s, steps)
                assert steps.n == SWA_STEPS + (ROPE_STEPS if rot else 0)
                take_result(b)

            first = Steps(dve, swa_own, 0)
            rope_read(0)
            rope(0, 0, first)
            stage_v(0)
            dve.wait_ge(swa_tab, 16)
            add_mask(0, 0, masks[:, 0, :])
            maxima(0, 0, first)
            rope_read(1)
            rope(1, 1, first)
            probabilities(0, 0, first)
            with dve.Fori(0, NB // 2 - 1) as i:
                block_step(i * 2, 0)
                block_step(i * 2 + 1, 1)
            block_step(NB - 2, 0, rot=False)
            own.base, own.n = own.base + own.n, 0
            dve.wait_ge(s_rot_mm, 1)
            cos, sin = rope_cos[:, 0:TS], rope_sin[:, 0:TS]
            dve.tensor_tensor(rot_q[:, :, 0:TS], ps[:, 6, 0:256].rearrange("p (g w) -> p g w", g=GRP),
                              over(sin, GRP, TS), ALU.mult)
            dve.tensor_tensor(rot_k[:, 0:TS], ps[:, 6, 256:256 + TS], sin, ALU.mult)
            dve.tensor_tensor(q_r[:, :, 0:TS], mix[:, M_Q:M_Q + GRP, 0:TS], over(cos, GRP, TS), ALU.mult)
            own.done(dve.tensor_tensor(ks_r[:, :], mix[:, M_K, 0:TS], cos, ALU.mult))
            dve.tensor_tensor(qs_r[:, :, :, :].rearrange("p b g t -> p g b t"),
                              q_r[:, :, 0:TS].rearrange("p g (b t) -> p g b t", b=NS),
                              rot_q[:, :, 0:TS].rearrange("p g (b t) -> p g b t", b=NS), ALU.add)
            dve.tensor_tensor(ks_r[:, :], ks_r[:, :], rot_k[:, 0:TS], ALU.add).then_inc(s_rope, 1)
            take_memory(NB - 1, 1, 0)
            own.done(dve.tensor_scalar(st8[:, 7, 0:4], c_("sink_s", 0, 4), HD ** 0.5, None, ALU.mult))
            dve.wait_ge(kvc_in, 48)
            dve.wait_ge(s_sc_mm, 1)
            own.done(dve.tensor_tensor(ss_m[:, :, :], ps[:, 0:4, 0:WIN + LS], over(mask_s[:, :], 4, WIN + LS),
                                       ALU.add))
            own.done(dve.tensor_reduce(st8[:, 0, 0:4], ss_m[:, :, :], AX_X, ALU.max))
            own.done(dve.tensor_tensor(st8[:, 0, 0:4], st8[:, 0, 0:4], st8[:, 7, 0:4], ALU.max))
            own.done(dve.tensor_scalar(st8[:, 1, 0:4], st8[:, 0, 0:4], -(HD ** -0.5), None, ALU.mult))
            dve.tensor_tensor(st8[:, 2, 0:4], st8[:, 1, 0:4], c_("sink_s", 0, 4), ALU.add).then_inc(s_nmax, 1)
            take_memory(NB - 1, 1, 1)
            dve.wait_ge(s_exp, 1)
            own.done(dve.tensor_tensor(st8[:, 5, 0:4], st8[:, 3, 0:4], st8[:, 4, 0:4], ALU.add))
            own.done(dve.reciprocal(st8[:, 6, 0:4], st8[:, 5, 0:4]))
            dve.tensor_tensor(ss_m[:, :, :], ss_m[:, :, :],
                              st8[:, 6, 0:4].unsqueeze(2).to_broadcast([P, 4, WIN + LS]), ALU.mult).then_inc(s_p, 1)
            take_result(NB - 1)
            dve.wait_ge(s_pv_mm, 1)
            dve.tensor_copy(mix[:, M_Q:M_Q + GRP, 0:TS].rearrange("p g (b t) -> p g b t", b=NS),
                            ps[:, 6, 0:256].rearrange("p (b g t) -> p g b t", b=NS, g=GRP)).then_inc(s_o_ev, 1)

            dve.wait_ge(stored, 16 * 7)
            for ct in range(LT):
                add_square("attn", ct)
            dve.sem_inc(g_ev["out"], 6)

            def cat_tile(k):
                return mix[:, M_U + k, :] if k < LT else mix[:, M_Q + k - LT, :]

            def attn_norm(c):
                o, n = CH[c]
                for ct in range(LT):
                    ins = dve.tensor_tensor(mix[:, M_Q + ct, o:o + n], mix[:, M_Q + ct, o:o + n], rstd[:, o:o + n],
                                            ALU.mult)
                ins.then_inc(attn_normed, 1)
                if c:
                    lo_parts("cat", cat_tile, "g_cat", [c - 1])

            inverse_rms("attn", LRU, then=attn_norm)
            dve.wait_ge(attn_normed, NC)
            lo_parts("cat", cat_tile, "g_cat", [NC - 1])

            def plain_residual(stage, pair0, key):
                def take(m, p, s):
                    to = x[:, m, :] if isinstance(m, int) else x[:, bass.ds(m, 1), :].squeeze(1)
                    for c, (o, n) in enumerate(CH):
                        dve.wait_ge(w_mm[s], slot_groups(stage, p, c))
                        dve.tensor_tensor(to[:, o:o + n], ps[:, 3 * s + c, 0:n], to[:, o:o + n], ALU.add)\
                           .then_inc(g_ev[stage], 1)
                    add_square(key, m)

                for s in range(2):
                    take(s, pair0, s)
                with dve.Fori(1, KT // 2) as i:
                    for s in range(2):
                        take(i * 2 + s, i + pair0, s)
                dve.wait_ge(g_ev[stage], 6 + NC * KT)

            plain_residual("out", PAIR_OUT, "xattn")
            dve.sem_inc(g_ev["cq"], 6)
            lo_parts("xattn", x_tile, "g_xattn")
            inverse_rms("xattn", D)
            with dve.Fori(0, KT // 2) as i:
                for s in range(2):
                    scaled_take("cq", s, i + PAIR_CQ, xq[:, bass.ds(i * 2 + s, 1), :].squeeze(1))
            dve.wait_ge(g_ev["cq"], 6 + NC * KT)

            def xcol(b):
                return bass.ds(b * P + TS, P)

            def x_stage(b):
                dve.tensor_copy(qs_b[:, :, :], xq[:, :, bass.ds(b * LS, 32)])
                dve.tensor_copy(xq_b[:, :, :], xq[:, :, xcol(b)]).then_inc(xq_st, 1)

            def x_soft(b, s, steps):
                dve.wait_ge(x_sc_mm, b + 1)
                steps.mark(dve.tensor_reduce(xst[:, s, 0, :], ps[:, 0:2, :].rearrange("p a (h w) -> p (a h) w", w=NM),
                                             AX_X, ALU.max))
                steps.done(dve.tensor_reduce(yst[:, 4 * s:4 * s + 1], ps[:, 2, 0:NM], AX_X, ALU.max))
                dve.tensor_scalar(xst[:, s, 1, :], xst[:, s, 0, :], -(XD ** -0.5), None, ALU.mult)
                dve.tensor_scalar(yst[:, 4 * s + 1:4 * s + 2], yst[:, 4 * s:4 * s + 1], -(XD ** -0.5), None,
                                  ALU.mult).then_inc(x_nmax, 1)

            def x_norm(b, s, steps):
                dve.wait_ge(x_exp, b + 2)
                steps.mark(dve.reciprocal(xst[:, s, 3, :], xst[:, s, 2, :]))
                steps.done(dve.reciprocal(yst[:, 4 * s + 3:4 * s + 4], yst[:, 4 * s + 2:4 * s + 3]))
                dve.tensor_tensor(xs_m[s][:, :, :], xs_m[s][:, :, :],
                                  xst[:, s, 3, :].unsqueeze(2).to_broadcast([P, XH, NM]), ALU.mult)
                dve.tensor_scalar(ys_m[s][:, :], ys_m[s][:, :], yst[:, 4 * s + 3:4 * s + 4], None, ALU.mult)\
                   .then_inc(x_p, 1)

            X_STEPS = 4

            def x_take(b):
                dve.wait_ge(x_pv_mm, b + 1)
                take_out(xq[:, :, xcol(b)], ps[:, 6:8, :].rearrange("p a (k w) -> p (a k) w", w=P))\
                    .then_inc(x_o_ev, 1)

            def x_step(b, s, more=True, stage=True):
                if more:
                    steps = Steps(dve, x_own, (b + 1) * X_STEPS)
                    x_soft(b + 1, 1 - s, steps)
                    if stage:
                        x_stage(b + 2)
                    x_norm(b + 1, 1 - s, steps)
                x_take(b)

            dve.sem_inc(x_o_ev, 1)
            x_stage(0)
            first = Steps(dve, x_own, 0)
            x_soft(0, 0, first)
            x_stage(1)
            x_norm(0, 0, first)
            with dve.Fori(0, NB // 2 - 1) as i:
                x_step(i * 2, 0)
                x_step(i * 2 + 1, 1)
            x_step(NB - 2, 0, stage=False)
            x_step(NB - 1, 1, more=False)
            dve.wait_ge(x_o_ev, 1 + NB)

            dve.wait_ge(y_ev, NB + 1)
            dve.sem_inc(g_ev["co"], 6)
            lo_parts("co", lambda k: xq[:, k, :])
            plain_residual("co", PAIR_CO, "ffn2")
            lo_parts("ffn2", x_tile, "g_ffn2")
            ffn_layer(ffn["ffn2"], "ffn2")
            for m in range(KT):
                for c in range(NC):
                    ffn_take(ffn["ffn2"], FI - 1, m, c, m * NC + c)
                if m:
                    add_square("final", m - 1)
            add_square("final", KT - 1)
            dve.wait_ge(ffn["ffn2"]["dn_ev"], FI * NC * KT + 8)

            def result(c):
                o, n = CH[c]
                for m in range(KT):
                    ins = dve.scalar_tensor_tensor(out=y[:, m, o:o + n], in0=x[:, m, o:o + n],
                                                   scalar=c_("g_final", m), in1=rstd[:, o:o + n], op0=ALU.mult,
                                                   op1=ALU.mult)
                ins.then_inc(y_done, 1)

            inverse_rms("final", D, then=result)


_OUTS = {
    "y": (P, KT, T), "mem_k": (P, KT, NM), "mem_v": (P, 2, D), "k_prompt": (P, WIN), "v_prompt": (P, KVH * HD),
    "k_sample": (P, NS, WIN), "v_sample": (WIN, NS, KVH * HD), "small": (P, NSM),
}


def tables():
    half = HD // 2
    inv = (10000.0 ** (-np.arange(half) / half)).astype(np.float32)
    pos = np.concatenate([np.tile(1024 + np.arange(LS), NS), np.arange(SEQ)]).astype(np.float32)
    ang = np.tile(inv, P // half)[:, None] * pos[None, :]
    rot = np.zeros((P, P), np.float32)
    for m in range(P):
        if m % HD < half:
            rot[m + half, m] = -1.0
        else:
            rot[m - half, m] = 1.0
    i, j = np.arange(WIN)[:, None], np.arange(2 * WIN)[None, :]
    band = np.where((j > i) & (j <= i + WIN), 0.0, NEG).astype(np.float32)
    start = np.where(j >= WIN, band, np.float32(NEG))
    masks = np.stack([start, band], axis=1)
    tok, key = (np.arange(P) % LS)[:, None], np.arange(WIN + LS)[None, :]
    mask_s = np.where((key > tok) & (key <= tok + WIN), 0.0, NEG).astype(np.float32)
    return {"cos": np.cos(ang).astype(np.float32), "sin": np.sin(ang).astype(np.float32), "rotm": rot,
            "ident": np.eye(P, dtype=np.float32), "masks": np.ascontiguousarray(masks), "mask_s": mask_s}


def kernel(**inputs):
    import concourse.bacc as bacc
    from concourse.bass_utils import run_bass_kernel_spmd

    a = {k: np.asarray(v) for k, v in inputs.items()}

    def per_tile(v):
        return v.reshape(-1, P).T

    def lhs_tiles(w):
        k, m = w.shape
        return w.reshape(k // P, P, m // P, P).transpose(2, 1, 0, 3)

    heads = [kv * GRP + g for g in range(GRP) for kv in range(KVH)]
    perm = np.concatenate([np.arange(h * HD, (h + 1) * HD) for h in heads])
    w_in = a["w_in"][0]
    q0 = 2 * LRU
    w_in = np.concatenate([w_in[:, :q0], w_in[:, q0:q0 + NH * HD][:, perm], w_in[:, q0 + NH * HD:]], axis=1)
    w_out = np.concatenate([a["w_out"][0][:LRU], a["w_out"][0][LRU:][perm]], axis=0)
    kv_tiles = np.stack([lhs_tiles(a[w][0]).reshape(KT // 2, 2, P, KT, P) for w in ("w_ck", "w_cv")], axis=1)
    kv_tiles = kv_tiles.reshape(2 * KT, P, KT, P)
    plain = np.concatenate([lhs_tiles(w_in), kv_tiles, lhs_tiles(w_out), lhs_tiles(a["w_cq"][0]),
                            lhs_tiles(a["w_co"][0])])
    plain = plain.reshape(PAIRS, 2, P, KT, P).transpose(1, 0, 2, 3, 4)

    def ffn_weights(n):
        return np.stack([lhs_tiles(a[f"w{n}_gate"][0]), lhs_tiles(a[f"w{n}_up"][0]),
                         a[f"w{n}_down"][0].reshape(FT, P, KT, P)], axis=1)

    tokens = np.concatenate([a["x_sample"].reshape(TS, D), a["x_prompt"][0]])

    def feature_major(v):
        return v.T.reshape(-1, P, v.shape[0]).transpose(1, 0, 2)

    bd = np.zeros((P, LT, 2, P), np.float32)
    nb = LRU // 8
    for g in range(8):
        r = slice((g % 2) * nb, (g % 2 + 1) * nb)
        bd[r, g // 2, 0, r] = a["w_a"][0, g]
        bd[r, g // 2, 1, r] = a["w_i"][0, g]
    sink = a["sink"][0]
    sink_s = np.tile(np.repeat(sink.reshape(KVH, GRP).T, LS, axis=0), (4, 2))
    parts = {
        **{g: per_tile(a[g][0]) for g in ("g_ffn1", "g_mix", "g_xattn", "g_ffn2", "g_mem", "conv_b",
                                          "b_a", "b_i", "lam")},
        "g_cat": per_tile(np.concatenate([a["g_lru_out"][0], a["g_attn_out"][0][perm]])),
        "g_final": per_tile(a["g_final"]),
        "conv_w": np.concatenate([per_tile(a["conv_w"][0, j]) for j in range(4)], axis=1),
        "sink": np.tile(sink, (P, 1)),
        "sink_s": sink_s,
        "h0": a["state_lru_h"][0].T.reshape(LT, P, NS).transpose(1, 0, 2).reshape(P, LT * NS),
        "hist": a["state_conv"][0].transpose(2, 0, 1).reshape(LT, P, NS, 3).transpose(1, 0, 2, 3)
        .reshape(P, LT * NS * 3),
    }
    host = {
        "x": feature_major(tokens),
        "cst": np.concatenate([parts[k] for k in COLS], axis=1),
        "w_ffn1": ffn_weights(1), "w_ffn2": ffn_weights(2), "w_plain": plain, "bd": bd,
        "mem": feature_major(a["mem_prompt"][0]),
        "kc": a["cache_swa_k"][0].transpose(2, 3, 0, 1).reshape(P, NS, WIN),
        "vc": a["cache_swa_v"][0].transpose(1, 0, 2, 3).reshape(WIN, NS, KVH * HD),
        "ck": a["cache_mem_k"][0].reshape(NS, NM, KT, P).transpose(0, 3, 2, 1),
        "cv": a["cache_mem_v"][0].reshape(NS, 2, P, D).transpose(0, 2, 1, 3),
        **tables(),
    }
    host = {k: np.ascontiguousarray(v) for k, v in host.items()}
    nc = bacc.Bacc("TRN2", target_bir_lowering=False, num_devices=1)
    t_in = {k: nc.dram_tensor(f"in_{k}", v.shape, F32, kind="ExternalInput").ap() for k, v in host.items()}
    t_out = {k: nc.dram_tensor(f"out_{k}", s, F32, kind="ExternalOutput").ap() for k, s in _OUTS.items()}
    build(nc, t_in, t_out)
    r = run_bass_kernel_spmd(nc, [{f"in_{k}": v for k, v in host.items()}], core_ids=[0]).results[0]
    o = {k: r[f"out_{k}"] for k in _OUTS}

    y = o["y"].transpose(2, 1, 0).reshape(T, D)
    small = o["small"]
    conv_p = small[:, SM_CP:SM_CS].reshape(P, LT, 3).transpose(2, 1, 0).reshape(1, 1, 3, LRU)
    conv_s = small[:, SM_CS:SM_HP].reshape(P, LT, NS, 3).transpose(2, 3, 1, 0).reshape(1, NS, 3, LRU)
    h_p = small[:, SM_HP:SM_HS].T.reshape(1, 1, LRU)
    h_s = small[:, SM_HS:].reshape(P, LT, NS).transpose(2, 1, 0).reshape(1, NS, LRU)
    return (
        y[TS:].reshape(1, SEQ, D), y[:TS].reshape(NS, LS, D),
        o["mem_k"].transpose(2, 1, 0).reshape(1, 1, NM, XH, XD),
        o["mem_v"].transpose(1, 0, 2).reshape(1, 1, NM, XH, XD),
        o["k_prompt"].T.reshape(1, 1, WIN, KVH, HD), o["v_prompt"].reshape(1, 1, WIN, KVH, HD),
        conv_p, h_p,
        o["k_sample"].transpose(1, 2, 0).reshape(1, NS, WIN, KVH, HD),
        o["v_sample"].transpose(1, 0, 2).reshape(1, NS, WIN, KVH, HD),
        conv_s, h_s,
    )
```

```python
from contextlib import ExitStack

import numpy as np
import concourse.bass as bass
from concourse import mybir

F32 = mybir.dt.float32
F32R = mybir.dt.float32r
ALU = mybir.AluOpType
ACT = mybir.ActivationFunctionType
AX_X = mybir.AxisListType.X

P = 128
D = 1024
KT = D // P
SEQ = 1024
NS, LS = 8, 8
TS = NS * LS
T = TS + SEQ
FF = 2816
FT = FF // P
FI = FT // 2
LRU = 512
LT = LRU // P
HD = 64
NH = 8
WIN = 128
NB = SEQ // WIN
KVH = 2
GRP = NH // KVH
NM = 256
XH = 4
XD = D // XH
EPS = 1e-6
YT = 6
IN_T = (2 * LRU + NH * HD + 2 * KVH * HD) // P
NEG = -1.0e30
CH = [(0, 364), (364, 362), (726, 362)]
NC = len(CH)
HALVES = [(0, T // 2), (T // 2, T // 2)]
M_U, M_G, M_Q, M_K, M_V = 0, 4, 8, 12, 13

DOWN_BANKS = (6, 7, 0, 3, 1, 4, 2, 5)

COLS = {}
_n = 0
for _name, _w in [("g_ffn1", KT), ("g_mix", KT), ("g_xattn", KT), ("g_ffn2", KT), ("g_mem", KT), ("g_final", KT),
                  ("g_cat", KT), ("conv_w", 4 * LT), ("conv_b", LT), ("b_a", LT),
                  ("b_i", LT), ("lam", LT), ("sink", NH), ("sink_s", 4), ("h0", LT * NS), ("hist", LT * NS * 3)]:
    COLS[_name] = (_n, _w)
    _n += _w
NCST = _n
SM_CP, SM_CS, SM_HP, SM_HS = 0, LT * 3, LT * 3 + LT * NS * 3, LT * 3 + LT * NS * 3 + LT
NSM = SM_HS + LT * NS
PAIR_IN, PAIR_KV, PAIR_OUT, PAIR_CQ, PAIR_CO, PAIRS = 0, 7, 15, 19, 23, 27
GROUPS = [(PAIR_IN, PAIR_KV, 0, NC), (PAIR_KV, PAIR_OUT, 7 * NC, 0), (PAIR_OUT, PAIRS, 7 * NC, NC)]
NORMS = ("ffn1", "mix", "lru", "mem", "attn", "xattn", "ffn2", "final")
_SQUARES = {"ffn1": NC * KT, "lru": 2 * LT, "mem": 1, "attn": 2 * LT}
SQ0 = {k: sum(_SQUARES.get(j, 2 * KT) for j in NORMS[:n]) for n, k in enumerate(NORMS)}
SUM0 = {k: sum(1 if j == "mem" else NC for j in NORMS[:n]) for n, k in enumerate(NORMS)}
SPLIT0 = {k: n * NC * KT for n, k in enumerate(("ffn1", "mix", "cat", "xattn", "co", "ffn2"))}


def groups_before(pair):
    return max(base + (min(pair, b) - a) * each for a, b, base, each in GROUPS if pair > a) if pair else 0


class Steps:

    def __init__(self, eng, sem, base=0):
        self.eng, self.sem, self.base, self.n = eng, sem, base, 0

    def mark(self, ins):
        self.n += 1
        ins.then_inc(self.sem, 1)
        return self.base + self.n

    def done(self, ins):
        self.eng.wait_ge(self.sem, self.mark(ins))


def build(nc, t_in, t_out):
    ctx = ExitStack()
    with ctx:
        def sem(name):
            return ctx.enter_context(nc.semaphore(name))

        START = 16512
        LIMIT = 229344

        def at(name, shape, off, dt=F32):
            size = 4 * int(np.prod(shape[1:]))
            assert off % 32 == 0 and off + size <= LIMIT, (name, off, size)
            return nc.alloc_sbuf_tensor_at(name, shape, dt, offset=off)

        ROW = 4 * T
        X0 = START
        A0 = X0 + KT * ROW
        RS0 = A0 + 2 * KT * ROW
        W0 = RS0 + ROW
        C0 = W0 + 6 * 4096
        P0 = C0 + 928 + 512 + 576
        x = at("x", [P, KT, T], X0)
        act_hi = at("act_hi", [P, KT, T], A0, F32R)
        act_lo = at("act_lo", [P, KT, T], A0 + KT * ROW, F32R)
        rstd = at("rstd", [P, T], RS0)
        w_raw = [at(f"w_raw{s}", [P, KT, P], W0 + s * 4096) for s in range(2)]
        w_hi2 = at("w_hi2", [P, 2, KT, P], W0 + 8192, F32R)
        w_lo2 = at("w_lo2", [P, 2, KT, P], W0 + 16384, F32R)
        w_hi = [w_hi2[:, s, :, :] for s in range(2)]
        w_lo = [w_lo2[:, s, :, :] for s in range(2)]
        assert NCST * 4 <= 928 and NSM * 4 <= 576
        cst = at("cst", [P, NCST], C0)
        ones = at("ones", [P, P], C0 + 928)
        small = at("small", [P, NSM], C0 + 1440)
        ACC0 = P0 + 68608
        lrup = at("lrup", [P, 8, LT], ACC0 + 2 * ROW)
        acc = at("acc", [P, T], ACC0)
        sq = at("sq", [P, T], ACC0 + ROW)
        ff_raw_up = at("ff_raw_up", [P, KT, P], P0)
        ff_raw_down = at("ff_raw_down", [P, KT, P], P0 + 4096)
        up_hi = [at(f"up_hi{s}", [P, KT, P], P0 + 8192 + s * 4096, F32R) for s in range(2)]
        up_lo = [at(f"up_lo{s}", [P, KT, P], P0 + 16384 + s * 4096, F32R) for s in range(2)]
        dn_hi = [at(f"dn_hi{s}", [P, KT, P], P0 + 24576 + s * 4096, F32R) for s in range(2)]
        dn_lo = [at(f"dn_lo{s}", [P, KT, P], P0 + 32768 + s * 4096, F32R) for s in range(2)]
        hid_hi = [at(f"hid_hi{s}", [P, T], P0 + 40960 + s * ROW, F32R) for s in range(2)]
        hid_lo = [at(f"hid_lo{s}", [P, T], P0 + 40960 + (2 + s) * ROW, F32R) for s in range(2)]
        gate_t = at("gate_t", [P, T], P0 + 40960 + 4 * ROW)
        hid_t = at("hid_t", [P, T], P0 + 40960 + 5 * ROW)
        mix = at("mix", [P, IN_T, T], P0)
        t_conv = at("t_conv", [P, T], P0 + IN_T * ROW)
        t_a = at("t_a", [P, T], P0 + (IN_T + 1) * ROW)
        t_b = at("t_b", [P, T], P0 + (IN_T + 2) * ROW)
        bd = at("bd", [P, LT, 2, P], P0 + M_V * ROW)
        mem_kT = at("mem_kT", [P, KT, NM], P0 + M_G * ROW)
        mem_v = at("mem_v", [P, 2, D], P0 + M_G * ROW + 8192)
        mem_raw = at("mem_raw", [P, KT, NM], P0 + M_G * ROW + 8192)

        lru_rstd = at("lru_rstd", [P, T], P0 + IN_T * ROW)
        mem_sq = at("mem_sq", [P, KT, NM], P0 + M_G * ROW)

        cur = [A0]

        def here(name, shape, dt=F32):
            tns = at(name, shape, cur[0], dt)
            cur[0] += -(-4 * int(np.prod(shape[1:])) // 32) * 32
            assert cur[0] <= RS0, name
            return tns

        rope_cos = here("rope_cos", [P, T])
        rope_sin = here("rope_sin", [P, T])
        masks = here("masks", [P, 3, 2 * WIN])
        ident = here("ident", [P, P])
        rotm = here("rotm", [P, P])
        s_m = [here(f"s_m{s}", [P, NH, 2 * WIN]) for s in range(2)]
        p_T = here("p_T", [P, 2, NH, WIN])
        q_r = here("q_r", [P, GRP, WIN])
        k_r = here("k_r", [P, 2, WIN])
        v_b = here("v_b", [P, WIN])
        v_n = [here(f"v_n{s}", [P, KVH * HD]) for s in range(2)]
        rot_q = here("rot_q", [P, GRP, WIN])
        rot_k = here("rot_k", [P, WIN])
        st8 = here("st8", [P, 8, NH])
        memn_hi = here("memn_hi", [P, KT, NM], F32R)
        memn_lo = here("memn_lo", [P, KT, NM], F32R)
        SA0 = P0 + IN_T * ROW
        kc_T = at("kc_T", [P, NS, WIN], SA0)
        v_c = at("v_c", [P, NS, KVH * HD], SA0 + 4096)
        qs_r = at("qs_r", [P, NS, GRP, LS], SA0 + 8192)
        ks_r = at("ks_r", [P, TS], SA0 + 9216)
        mask_s = at("mask_s", [P, WIN + LS], SA0 + 9472)
        SM0 = A0 + 2 * ROW + 3072 + 1024
        ss_m = at("ss_m", [P, 4, WIN + LS], SM0)
        pcs_T = at("pcs_T", [P, 4, P], SM0 + 2208)
        pns_T = at("pns_T", [LS, 4, P], SM0 + 2208 + 2048)
        vs_n = at("vs_n", [LS, NS, KVH * HD], SA0 + 10240)

        xq = at("xq", [P, KT, T], P0 + 33792)
        cur[0] = A0
        x_id = here("x_id", [P, P])
        xq_b = here("xq_b", [P, KT, P])
        xs_m = [here(f"xs_m{s}", [P, XH, NM]) for s in range(2)]
        xp_T = here("xp_T", [P, 2, XH, P])
        xst = here("xst", [P, 2, 4, XH])
        qs_b = here("qs_b", [P, KT, 32])
        ys_m = [here(f"ys_m{s}", [P, NM]) for s in range(2)]
        yp_T = here("yp_T", [P, 2, P])
        yst = here("yst", [P, 8])
        y_s = here("y_s", [P, NM])
        ck_T = [here(f"ck_T{s}", [P, KT, NM]) for s in range(2)]
        cv_n = [here(f"cv_n{s}", [P, 2, D]) for s in range(2)]

        y = at("y", [P, KT, T], P0)
        ps = ctx.enter_context(nc.psum_tensor("ps", [P, 8, 512], F32))

        def c_(name, j=0, n=1):
            o, w = COLS[name]
            return cst[:, o + j:o + j + n]

        cst_in = sem("cst_in")
        bd_in = sem("bd_in")
        x_in = [sem(f"x_in{c}") for c in range(NC)]
        ones_set = sem("ones_set")
        dve_own = sem("dve_own")
        act_hi_done, act_lo_done = sem("act_hi_done"), sem("act_lo_done")
        memn_hi_done, memn_lo_done = sem("memn_hi_done"), sem("memn_lo_done")
        sq_done, sq_used = sem("sq_done"), sem("sq_used")
        ssq_mm, ssq_ev = sem("ssq_mm"), sem("ssq_ev")
        rms_done, rstd_done = sem("rms_done"), sem("rstd_done")

        def ffn_sems(tag):
            names = ("gu_in", "dn_in", "gu_split", "dn_split", "pool_own", "pool_dn", "gate_mm", "up_mm",
                     "gate_ev", "up_ev", "silu", "hid_f", "hid_hi", "hid_lo", "dn_mm", "dn_ev")
            return {n: sem(f"{tag}_{n}") for n in names}

        ffn = {"ffn1": ffn_sems("ffn1"), "ffn2": ffn_sems("ffn2")}
        w_in = [sem(f"w_in{s}") for s in range(2)]
        w_split = [sem(f"w_split{s}") for s in range(2)]
        w_mm = [sem(f"w_mm{s}") for s in range(2)]
        w_pool = sem("w_pool")
        STAGES = ("in", "out", "cq", "co")
        g_ev = {k: sem(f"{k}_ev") for k in STAGES}
        conv_done = sem("conv_done")
        conv_back = sem("conv_back")
        gate_gelu = sem("gate_gelu")
        lru_sp = sem("lru_sp")
        lru_mm = sem("lru_mm")
        lru_ev = sem("lru_ev")
        lru_th = sem("lru_th")
        lru_a = sem("lru_a")
        lru_q = sem("lru_q")
        lru_s = sem("lru_s")
        lru_y = sem("lru_y")
        lru_normed, mem_normed, attn_normed = sem("lru_normed"), sem("mem_normed"), sem("attn_normed")
        swa_tab = sem("swa_tab")
        rope_tab = sem("rope_tab")
        rot_mm, rot_ev = sem("rot_mm"), sem("rot_ev")
        rope_done = sem("rope_done")
        sc_mm, sc_taken = sem("sc_mm"), sem("sc_taken")
        nmax_done, exp_done, p_done = sem("nmax_done"), sem("exp_done"), sem("p_done")
        pt_mm, pt_ev = sem("pt_mm"), sem("pt_ev")
        v_st, vt_mm, vt_ev = sem("v_st"), sem("vt_mm"), sem("vt_ev")
        pv_mm, o_ev = sem("pv_mm"), sem("o_ev")
        mem_mm, kv_ev = sem("mem_mm"), sem("kv_ev")
        swa_own = sem("swa_own")
        mem_in = sem("mem_in")
        kvc_in = sem("kvc_in")
        s_rot_mm, s_rope, s_sc_mm, s_nmax, s_exp, s_p = (
            sem("s_rot_mm"), sem("s_rope"), sem("s_sc_mm"), sem("s_nmax"), sem("s_exp"), sem("s_p"))
        s_pt_mm, s_pt_ev, s_pv_mm, s_o_ev = sem("s_pt_mm"), sem("s_pt_ev"), sem("s_pv_mm"), sem("s_o_ev")
        x_tab = sem("x_tab")
        ck_in = [sem(f"ck_in{s}") for s in range(2)]
        cv_in = [sem(f"cv_in{s}") for s in range(2)]
        xq_st = sem("xq_st")
        x_sc_mm, x_nmax, x_exp, x_p = sem("x_sc_mm"), sem("x_nmax"), sem("x_exp"), sem("x_p")
        x_turned = sem("x_turned")
        x_pt_mm, x_pt_ev = sem("x_pt_mm"), sem("x_pt_ev")
        y_mm, y_ev = sem("y_mm"), sem("y_ev")
        x_pv_mm, x_o_ev, x_own = sem("x_pv_mm"), sem("x_o_ev"), sem("x_own")
        y_done, y_gain, y_pool = sem("y_done"), sem("y_gain"), sem("y_pool")
        stored = sem("stored")

        block = ctx.enter_context(nc.Block())

        def pair_src(s, p):
            return t_in["w_plain"][s, p, :, :, :]


        @block.sync
        def _(sp):
            def load_gu(f, w, t, first=False):
                if not first:
                    sp.wait_ge(f["gu_split"], t)
                sp.dma_start(w_raw[0][:, :, :], w[t, 0, :, :, :]).then_inc(f["gu_in"], 16)
                sp.dma_start(ff_raw_up[:, :, :], w[t, 1, :, :, :]).then_inc(f["gu_in"], 16)

            def load_down(f, w, j, first=False):
                if not first:
                    sp.wait_ge(f["dn_split"], j)
                sp.dma_start(w_raw[1][:, :, :], w[j * 2, 2, :, :, :]).then_inc(f["dn_in"], 16)
                sp.dma_start(ff_raw_down[:, :, :], w[j * 2 + 1, 2, :, :, :]).then_inc(f["dn_in"], 16)

            def load_ffn(f, w):
                load_gu(f, w, 1)
                load_down(f, w, 0, first=True)
                load_gu(f, w, 2)
                load_gu(f, w, 3)
                with sp.Fori(1, FI - 1) as i:
                    load_gu(f, w, i * 2 + 2)
                    load_down(f, w, i)
                    load_gu(f, w, i * 2 + 3)
                load_down(f, w, FI - 1)

            def load_pairs(a, b):
                with sp.Fori(a, b) as p:
                    for s in range(2):
                        sp.wait_ge(w_split[s], p)
                        sp.dma_start(w_raw[s][:, :, :], pair_src(s, p)).then_inc(w_in[s], 16)

            f = ffn["ffn1"]
            sp.dma_start(cst[:, :], t_in["cst"]).then_inc(cst_in, 16)
            for c, (o, n) in enumerate(CH):
                if c == 0:
                    load_gu(f, t_in["w_ffn1"], 0, first=True)
                sp.dma_start(x[:, :, o:o + n], t_in["x"][:, :, o:o + n]).then_inc(x_in[c], 16)
            load_ffn(f, t_in["w_ffn1"])

            sp.wait_ge(f["gu_split"], FT)
            sp.dma_start(w_raw[0][:, :, :], pair_src(0, 0)).then_inc(w_in[0], 16)
            sp.wait_ge(f["dn_split"], FI)
            sp.dma_start(w_raw[1][:, :, :], pair_src(1, 0)).then_inc(w_in[1], 16)
            load_pairs(1, 3)
            sp.wait_ge(g_ev["in"], 6 + 3)
            sp.dma_start(bd[:, :, :, :], t_in["bd"]).then_inc(bd_in, 16)
            load_pairs(3, PAIR_KV)
            sp.wait_ge(lru_y, LT)
            sp.dma_start(mem_raw[:, :, :], t_in["mem"]).then_inc(mem_in, 16)
            load_pairs(PAIR_KV, PAIR_KV + 1)
            sp.wait_ge(w_mm[1], groups_before(PAIR_KV))
            for dst, src in ((rotm, "rotm"), (rope_cos, "cos"), (rope_sin, "sin"), (ident, "ident")):
                sp.dma_start(dst[:, :], t_in[src]).then_inc(rope_tab, 16)
            sp.dma_start(masks[:, :, :], t_in["masks"]).then_inc(swa_tab, 16)
            sp.wait_ge(lru_normed, LT)
            sp.wait_ge(mem_normed, 1)
            sp.dma_start(kc_T[:, :, :], t_in["kc"]).then_inc(kvc_in, 16)
            sp.dma_start(v_c[:, :, :], t_in["vc"]).then_inc(kvc_in, 16)
            sp.dma_start(mask_s[:, :], t_in["mask_s"]).then_inc(kvc_in, 16)
            load_pairs(PAIR_KV + 1, PAIR_CO)
            sp.wait_ge(w_mm[1], groups_before(PAIR_CO))
            sp.dma_start(x_id[:, :], t_in["ident"]).then_inc(x_tab, 16)

            def load_keys(b, s):
                sp.dma_start(ck_T[s][:, :, :], t_in["ck"][b, :, :, :]).then_inc(ck_in[s], 16)

            def load_values(b, s):
                sp.dma_start(cv_n[s][:, :, :], t_in["cv"][b, :, :, :]).then_inc(cv_in[s], 16)

            for s in range(2):
                load_keys(s, s)
                load_values(s, s)
            load_pairs(PAIR_CO, PAIR_CO + 1)
            with sp.Fori(1, NS // 2) as i:
                for s in range(2):
                    sp.wait_ge(x_sc_mm, i * 2 + (s - 1))
                    load_keys(i * 2 + s, s)
                    sp.wait_ge(y_mm, i * 2 + (s - 1))
                    load_values(i * 2 + s, s)
            load_pairs(PAIR_CO + 1, PAIRS)

            f = ffn["ffn2"]
            sp.wait_ge(act_lo_done, SPLIT0["co"] + NC * KT)
            sp.wait_ge(w_split[0], PAIRS)
            sp.wait_ge(w_split[1], PAIRS)
            load_gu(f, t_in["w_ffn2"], 0, first=True)
            load_ffn(f, t_in["w_ffn2"])

        @block.gpsimd
        def _(pool):
            def split(raw, hi, lo, steps, last=None):
                one = ones[:, :].unsqueeze(1).to_broadcast([P, KT, P])
                steps.done(pool.tensor_tensor(hi[:, :, :], raw[:, :, :], one, ALU.mult))
                ins = pool.tensor_tensor(lo[:, :, :], raw[:, :, :], hi[:, :, :].bitcast(F32), ALU.subtract)
                steps.done(ins) if last is None else ins.then_inc(last, 1)

            def split_gu(f, t, s):
                pool.wait_ge(f["gu_in"], (t + 1) * 32)
                steps = Steps(pool, f["pool_own"], t * 3)
                split(w_raw[0], w_hi[s], w_lo[s], steps)
                split(ff_raw_up, up_hi[s], up_lo[s], steps, f["gu_split"])

            def split_down(f, j):
                pool.wait_ge(f["dn_in"], (j + 1) * 32)
                steps = Steps(pool, f["pool_dn"], j * 3)
                split(w_raw[1], dn_hi[0], dn_lo[0], steps)
                split(ff_raw_down, dn_hi[1], dn_lo[1], steps, f["dn_split"])

            def split_ffn(f):
                split_gu(f, 1, 1)
                split_down(f, 0)
                for t in (2, 3):
                    pool.wait_ge(f["up_mm"], (t - 1) * NC)
                    split_gu(f, t, t % 2)
                with pool.Fori(1, FI - 1) as i:
                    pool.wait_ge(f["up_mm"], i * (2 * NC) + NC)
                    split_gu(f, i * 2 + 2, 0)
                    pool.wait_ge(f["dn_mm"], i * (NC * KT))
                    split_down(f, i)
                    pool.wait_ge(f["up_mm"], i * (2 * NC) + 2 * NC)
                    split_gu(f, i * 2 + 3, 1)
                pool.wait_ge(f["dn_mm"], (FI - 1) * (NC * KT))
                split_down(f, FI - 1)

            def split_plain(s, p):
                pool.wait_ge(w_in[s], (p + 1) * 16)
                split(w_raw[s], w_hi[s], w_lo[s], Steps(pool, w_pool, p * 2 + s), w_split[s])

            f = ffn["ffn1"]
            pool.wait_ge(ones_set, 1)
            split_gu(f, 0, 0)
            split_ffn(f)
            for s in range(2):
                pool.wait_ge(f["up_mm"], (FT - 1 + s) * NC)
                split_plain(s, 0)
            def split_pairs(first, last, pair0, base):
                with pool.Fori(first, last) as p:
                    for s in range(2):
                        pool.wait_ge(w_mm[s], p * NC + (base - pair0 * NC))
                        split_plain(s, p)

            split_pairs(1, PAIR_KV + 1, PAIR_IN, 0)
            pool.wait_ge(rstd_done, SUM0["lru"] + NC)
            for ct in range(LT):
                pool.tensor_tensor(mix[:, M_U + ct, :], mix[:, M_U + ct, :], lru_rstd[:, :], ALU.mult)\
                    .then_inc(lru_normed, 1)
            for s in range(2):
                pool.wait_ge(mem_mm, 1 + s)
                split_plain(s, PAIR_KV + 1)
            with pool.Fori(1, NB // 2) as i:
                for s in range(2):
                    pool.wait_ge(mem_mm, i * 4)
                    split_plain(s, i * 2 + PAIR_KV)
                for s in range(2):
                    pool.wait_ge(mem_mm, i * 4 + (1 + s))
                    split_plain(s, i * 2 + (PAIR_KV + 1))
            for s in range(2):
                pool.wait_ge(mem_mm, 2 * NB)
                split_plain(s, PAIR_OUT)
            split_pairs(PAIR_OUT + 1, PAIRS, PAIR_OUT, 7 * NC)
            f = ffn["ffn2"]
            pool.wait_ge(w_mm[0], groups_before(PAIRS))
            pool.wait_ge(stored, 16 * 9)
            split_gu(f, 0, 0)
            pool.wait_ge(w_mm[1], groups_before(PAIRS))
            split_ffn(f)
            pool.wait_ge(y_gain, KT - YT)
            for c, (o, n) in enumerate(CH):
                pool.wait_ge(rstd_done, SUM0["final"] + c + 1)
                for m in range(YT, KT):
                    ins = pool.tensor_tensor(y[:, m, o:o + n], y[:, m, o:o + n], rstd[:, o:o + n], ALU.mult)
                ins.then_inc(y_pool, 1)


        @block.tensor
        def _(pe):
            def three(out, pairs, first, last):
                ins = None
                for n, (wh, wl, ah, al) in enumerate(pairs):
                    end = last and n == len(pairs) - 1
                    pe.matmul(out, wh, ah, start=(first and n == 0), stop=False)
                    pe.matmul(out, wh, al, start=False, stop=False)
                    ins = pe.matmul(out, wl, ah, start=False, stop=end)
                return ins

            def product(out, wh, wl, c, feed):
                o, n = CH[c]
                for k in range(KT):
                    if feed:
                        pe.wait_ge(act_lo_done, SPLIT0[feed] + c * KT + k + 1)
                    ins = three(out, [(wh[:, k, :], wl[:, k, :], act_hi[:, k, o:o + n], act_lo[:, k, o:o + n])],
                                k == 0, k == KT - 1)
                return ins

            def sum_squares(key, chunks, adds, src=acc):
                for c in range(len(chunks)):
                    sum_chunk(key, chunks, c, adds, src)

            def sum_chunk(key, chunks, c, adds, src=acc):
                o, n = chunks[c]
                pe.wait_ge(sq_used, SQ0[key] + adds)
                if c >= 2:
                    pe.wait_ge(ssq_ev, SUM0[key] + c - 1)
                pe.matmul(ps[:, 6 + c % 2, 0:n], ones[:, :], src[:, o:o + n], start=True, stop=True)\
                  .then_inc(ssq_mm, 1)

            def gu(f, t, s, feed=None, taken=None, after=lambda c: None):
                if feed:
                    pe.wait_ge(f["pool_own"], 2)
                else:
                    pe.wait_ge(f["gu_split"], t + 1)
                for c, (o, n) in enumerate(CH):
                    if taken:
                        taken(c)
                    product(ps[:, c, 0:n], w_hi[s], w_lo[s], c, feed).then_inc(f["gate_mm"], 1)
                    if feed and c == 0:
                        pe.wait_ge(f["gu_split"], t + 1)
                    product(ps[:, 3 + c, 0:n], up_hi[s], up_lo[s], c, None).then_inc(f["up_mm"], 1)
                    after(c)

            def down(f, j, t_before, by_chunk=False):
                pe.wait_ge(f["dn_split"], j + 1)
                for n_ in range(KT * NC):
                    m, c = (n_ % KT, n_ // KT) if by_chunk else divmod(n_, NC)
                    bank = DOWN_BANKS[n_ % 8]
                    o, n = CH[c]
                    if m == 0:
                        pe.wait_ge(f["hid_lo"], j * (2 * NC) + NC + c + 1)
                    pe.wait_ge(f["dn_ev"], j * (NC * KT) + n_ + 1)
                    if n_ < 8 and bank < 6:
                        pe.wait_ge(f["gate_ev" if bank < 3 else "up_ev"], t_before * NC + bank % 3 + 1)
                    three(ps[:, bank, 0:n], [(dn_hi[s][:, m, :], dn_lo[s][:, m, :], hid_hi[s][:, o:o + n],
                                              hid_lo[s][:, o:o + n]) for s in range(2)], True, True)\
                        .then_inc(f["dn_mm"], 1)

            def ffn_layer(f, key, before, after, by_chunk=False):
                def after_gu(t):
                    def taken(c):
                        pe.wait_ge(f["gate_ev"], t * NC + c + 1)
                        pe.wait_ge(f["up_ev"], t * NC + c + 1)
                    return taken

                def after_down(j):
                    def taken(c):
                        at_ = max(DOWN_BANKS.index(c), DOWN_BANKS.index(3 + c))
                        pe.wait_ge(f["dn_ev"], j * (NC * KT) + (NC * KT - 8) + at_ + 1 + 8)
                    return taken

                before()
                gu(f, 0, 0, feed=key, after=lambda c: after(0, c))
                gu(f, 1, 1, taken=after_gu(0), after=lambda c: after(1, c))
                with pe.Fori(1, FI) as i:
                    gu(f, i * 2, 0, taken=after_gu(i * 2 - 1))
                    down(f, i - 1, i * 2)
                    gu(f, i * 2 + 1, 1, taken=after_down(i - 1))
                down(f, FI - 1, FT - 1, by_chunk)

            def tile(stage, p, s, n0, feed=None):
                pe.wait_ge(w_split[s], p + 1)
                for c, (o, n) in enumerate(CH):
                    pe.wait_ge(g_ev[stage], n0 + c + 1)
                    ins = product(ps[:, 3 * s + c, 0:n], w_hi[s], w_lo[s], c, feed)
                    ins.then_inc(w_mm[s], 1)

            def plain(stage, pair0, pairs, feed, norm=None):
                tile(stage, pair0, 0, 0, feed=feed)
                if norm:
                    sum_squares(norm, CH, 2 * KT)
                tile(stage, pair0, 1, NC)
                with pe.Fori(1, pairs) as i:
                    for s in range(2):
                        tile(stage, i + pair0, s, i * (2 * NC) + s * NC)

            pe.wait_ge(ones_set, 1)

            def sum_ffn1(t, c):
                if (t, c) in ((0, 0), (0, 1), (1, 0)):
                    sum_chunk("ffn1", CH, c + 2 * t, (c + 2 * t + 1) * KT)

            def sum_ffn2(t, c):
                if (t, c) == (0, 1):
                    sum_squares("ffn2", CH, 2 * KT)

            ffn_layer(ffn["ffn1"], "ffn1", lambda: None, sum_ffn1, by_chunk=True)

            def lru_gates(ct):
                pe.wait_ge(conv_back, ct + 1)
                if ct == 0:
                    pe.wait_ge(bd_in, 16)
                    pe.wait_ge(ssq_ev, SUM0["mix"] + NC)
                for j in range(2 * NC):
                    n_ = ct * 2 * NC + j
                    o, n = CH[j % NC]
                    if n_ >= 2:
                        pe.wait_ge(lru_ev, n_ - 1)
                    pe.matmul(ps[:, 6 + n_ % 2, 0:n], bd[:, ct, j // NC, :], mix[:, M_U + ct, o:o + n],
                              start=True, stop=True).then_inc(lru_mm, 1)

            plain("in", PAIR_IN, 4, "mix", norm="mix")
            for m in range(8, IN_T):
                if m < 8 + LT:
                    lru_gates(m - 8)
                tile("in", m // 2, m % 2, m * NC)
                if m == IN_T - 2:
                    sum_squares("lru", CH, 2 * LT)
                    pe.wait_ge(ssq_ev, SUM0["lru"] + NC)
            sum_squares("mem", [(0, NM)], 1, sq)

            pe.wait_ge(ssq_ev, SUM0["mem"] + 1)
            pe.wait_ge(g_ev["in"], 6 + 3 * IN_T)
            pe.wait_ge(rope_tab, 64)

            def blk(b):
                return bass.ds(b * WIN + TS, WIN)

            def rotate(b):
                if not (isinstance(b, int) and b == 0):
                    pe.wait_ge(rot_ev, b)
                if not isinstance(b, int) or b > 1:
                    pe.wait_ge(o_ev, b - 1)
                    pe.wait_ge(vt_ev, b - 1)
                    pe.wait_ge(kv_ev, b * 2 - 3)
                pe.matmul(ps[:, 6, :], rotm[:, :], mix[:, M_Q:M_Q + GRP, blk(b)], start=True, stop=True)
                pe.matmul(ps[:, 7, 0:WIN], rotm[:, :], mix[:, M_K, blk(b)], start=True, stop=True)\
                  .then_inc(rot_mm, 1)

            def scores(b):
                pe.wait_ge(rope_done, b + 1)
                pe.wait_ge(sc_taken, b + 1)
                for j in range(NH):
                    g, kv = divmod(j, KVH)
                    h = kv * GRP + g
                    r = slice(kv * HD, kv * HD + HD)
                    ins = pe.matmul(ps[:, h // 2, (h % 2) * 256:(h % 2) * 256 + 256], q_r[r, g, :], k_r[r, :, :],
                                    start=True, stop=True)
                ins.then_inc(sc_mm, 1)

            def turn_v(b):
                pe.wait_ge(v_st, b + 1)
                pe.wait_ge(kv_ev, b * 2 + 1)
                pe.transpose(ps[:, 7, WIN:2 * WIN], v_b[:, :], ident[:, :]).then_inc(vt_mm, 1)

            def turn_p(b, s, kv):
                pe.wait_ge(pt_ev, b * 2 + kv + 1)
                for g in range(GRP):
                    for half in range(2):
                        ins = pe.transpose(ps[:, 4 + half, g * WIN:(g + 1) * WIN],
                                           s_m[s][:, kv * GRP + g, half * WIN:(half + 1) * WIN], ident[:, :])
                ins.then_inc(pt_mm, 1)

            def weigh(b, kv):
                pe.wait_ge(pt_ev, b * 2 + kv + 2)
                for half in range(2):
                    ins = pe.matmul(ps[kv * HD:(kv + 1) * HD, 6, :], v_n[half][:, kv * HD:(kv + 1) * HD],
                                    p_T[:, half, kv * GRP:(kv + 1) * GRP, :], start=(half == 0), stop=(half == 1))
                return ins

            def memory_tile(b, s, j):
                for slot in ((j,) if s == 0 else (0, 1)):
                    pe.wait_ge(w_split[slot], b + (PAIR_KV + 1))
                pe.wait_ge(kv_ev, b * 2 + j + 1)
                out = ps[:, 7, 256:512]
                for k in range(KT):
                    if s == 0:
                        ins = three(out, [(w_hi[j][:, k, :], w_lo[j][:, k, :], memn_hi[:, k, :],
                                           memn_lo[:, k, :])], k == 0, k == KT - 1)
                    else:
                        r = slice(j * P, (j + 1) * P)
                        ins = three(out, [(memn_hi[:, k, r], memn_lo[:, k, r], w_hi2[:, :, k, :],
                                           w_lo2[:, :, k, :])], k == 0, k == KT - 1)
                ins.then_inc(mem_mm, 1)

            def block_step(b, s, more=True, rot=True):
                if more:
                    scores(b + 1)
                pe.wait_ge(p_done, b + 1)
                turn_p(b, s, 0)
                if rot:
                    rotate(b + 2)
                turn_p(b, s, 1)
                pe.wait_ge(vt_ev, b + 1)
                if rot:
                    pe.wait_ge(rot_ev, b + 3)
                else:
                    pe.wait_ge(o_ev, b + 1)
                memory_tile(b, s, 0)
                if not more:
                    sample_scores()
                weigh(b, 0)
                memory_tile(b, s, 1)
                weigh(b, 1).then_inc(pv_mm, 1)
                if more:
                    turn_v(b + 1)

            def sample_rotate():
                pe.wait_ge(o_ev, NB)
                pe.matmul(ps[:, 6, 0:GRP * TS], rotm[:, :], mix[:, M_Q:M_Q + GRP, 0:TS], start=True, stop=True)
                pe.matmul(ps[:, 6, 256:256 + TS], rotm[:, :], mix[:, M_K, 0:TS], start=True, stop=True)\
                  .then_inc(s_rot_mm, 1)
                pe.wait_ge(pt_ev, NB * 2 - 1)
                for b in range(NS):
                    pe.transpose(ps[0:LS, 4 + b // 4, (b % 4) * P:(b % 4 + 1) * P],
                                 mix[:, M_V, b * LS:(b + 1) * LS], ident[:, :]).then_inc(s_rot_mm, 1)
                pe.wait_ge(s_pt_ev, 1)

            def sample_scores():
                pe.wait_ge(kvc_in, 48)
                pe.wait_ge(s_rope, 1)
                pe.wait_ge(sc_taken, NB + 1)
                for b in range(NS):
                    for kv in range(KVH):
                        r = slice(kv * HD, kv * HD + HD)
                        q = qs_r[r, b, :, :]
                        out = ps[32 * (b % 4):32 * (b % 4) + 32, (b // 4) * 2 + kv, 0:WIN + LS]
                        pe.matmul(out[:, 0:WIN], q, kc_T[r, b, :], start=True, stop=True)
                        ins = pe.matmul(out[:, WIN:WIN + LS], q, ks_r[r, b * LS:(b + 1) * LS], start=True, stop=True)
                ins.then_inc(s_sc_mm, 1)

            rotate(0)
            scores(0)
            rotate(1)
            pe.wait_ge(rot_ev, 2)
            turn_v(0)
            pe.wait_ge(memn_lo_done, 1)
            with pe.Fori(0, NB // 2 - 1) as i:
                block_step(i * 2, 0)
                block_step(i * 2 + 1, 1)
            block_step(NB - 2, 0, rot=False)
            sample_rotate()
            block_step(NB - 1, 1, more=False, rot=False)

            pe.wait_ge(s_p, 1)
            for t in range(4):
                pe.transpose(ps[:, 2, t * P:(t + 1) * P], ss_m[:, t, 0:WIN], ident[:, :])
                ins = pe.transpose(ps[0:LS, 3, t * P:(t + 1) * P], ss_m[:, t, WIN:WIN + LS], ident[:, :])
            ins.then_inc(s_pt_mm, 1)
            pe.wait_ge(s_pt_ev, 3)
            pe.wait_ge(o_ev, NB + 1)
            for b in range(NS):
                for kv in range(KVH):
                    t, j = (b // 4) * 2 + kv, b % 4
                    r = slice(kv * HD, kv * HD + HD)
                    out = ps[r, 6, b * 32:(b + 1) * 32]
                    pe.matmul(out, v_c[:, b, r], pcs_T[:, t, 32 * j:32 * j + 32], start=True, stop=False)
                    ins = pe.matmul(out, vs_n[:, b, r], pns_T[:, t, 32 * j:32 * j + 32], start=False, stop=True)
            ins.then_inc(s_pv_mm, 1)
            sum_squares("attn", CH, 2 * LT)

            plain("out", PAIR_OUT, 4, "cat")
            plain("cq", PAIR_CQ, 4, "xattn", norm="xattn")

            pe.wait_ge(x_tab, 16)
            pe.wait_ge(g_ev["cq"], 6 + NC * KT)

            def x_scores(b):
                pe.wait_ge(xq_st, b + 1)
                pe.wait_ge(x_exp, b + 1)
                for h in range(XH):
                    for d in range(2):
                        pe.matmul(ps[:, h // 2, (h % 2) * NM:(h % 2 + 1) * NM], xq_b[:, 2 * h + d, :],
                                  mem_kT[:, 2 * h + d, :], start=(d == 0), stop=(d == 1))

            def y_scores(b, half, s):
                pe.wait_ge(ck_in[s], half * 16 + 16)
                for h in range(XH):
                    for d in range(2):
                        ins = pe.matmul(ps[32 * h:32 * h + 32, 2, 0:NM], qs_b[:, 2 * h + d, :],
                                        ck_T[s][:, 2 * h + d, :], start=(d == 0), stop=(d == 1))
                ins.then_inc(x_sc_mm, 1)

            def back():
                for d in range(2):
                    ins = pe.transpose(ps[:, 5, NM + d * P:NM + (d + 1) * P], y_s[:, d * P:(d + 1) * P], x_id[:, :])
                return ins

            def x_turn(b, s):
                pe.wait_ge(x_p, b + 1)
                pe.wait_ge(x_pt_ev, b + 1)
                for h in range(XH):
                    for mt in range(2):
                        ins = pe.transpose(ps[:, 3 + mt, h * P:(h + 1) * P], xs_m[s][:, h, mt * P:(mt + 1) * P],
                                           x_id[:, :])
                ins.then_inc(x_turned, 1)

            def y_turn(b, s, after=True):
                if after:
                    pe.wait_ge(y_ev, b)
                    back()
                for mt in range(2):
                    ins = pe.transpose(ps[:, 5, mt * P:(mt + 1) * P], ys_m[s][:, mt * P:(mt + 1) * P], x_id[:, :])
                ins.then_inc(x_pt_mm, 1)

            def x_weigh(b, half, s):
                pe.wait_ge(x_pt_ev, b + 2)
                pe.wait_ge(cv_in[s], half * 16 + 16)
                for mt in range(2):
                    for h in range(XH):
                        ins = pe.matmul(ps[32 * h:32 * h + 32, 5, NM:2 * NM], yp_T[:, mt, 32 * h:32 * h + 32],
                                        cv_n[s][:, mt, h * XD:(h + 1) * XD], start=(mt == 0), stop=(mt == 1))
                ins.then_inc(y_mm, 1)
                pe.wait_ge(x_o_ev, b + 1)
                for kt in range(KT):
                    for mt in range(2):
                        ins = pe.matmul(ps[:, 6 + kt // 4, (kt % 4) * P:(kt % 4 + 1) * P],
                                        mem_v[:, mt, kt * P:(kt + 1) * P], xp_T[:, mt, kt // 2, :],
                                        start=(mt == 0), stop=(mt == 1))
                ins.then_inc(x_pv_mm, 1)

            def x_step(b, half, s, more=True, after=True):
                if more:
                    x_scores(b + 1)
                x_turn(b, s)
                if more:
                    y_scores(b + 1, half + s, 1 - s)
                y_turn(b, s, after)
                x_weigh(b, half, s)

            x_scores(0)
            y_scores(0, 0, 0)
            x_step(0, 0, 0, after=False)
            x_step(1, 0, 1)
            with pe.Fori(1, NB // 2 - 1) as i:
                x_step(i * 2, i, 0)
                x_step(i * 2 + 1, i, 1)
            x_step(NB - 2, NB // 2 - 1, 0)
            x_step(NB - 1, NB // 2 - 1, 1, more=False)
            pe.wait_ge(y_ev, NB)
            back().then_inc(x_pt_mm, 1)

            plain("co", PAIR_CO, 4, "co")
            ffn_layer(ffn["ffn2"], "ffn2", lambda: pe.wait_ge(g_ev["co"], 6 + NC * KT), sum_ffn2)
            sum_squares("final", CH, 2 * KT)

        @block.scalar
        def _(act):
            def squares(key, tiles, src, ready):
                for m in range(tiles):
                    square(key, m, src(m), ready)

            def square(key, m, src, ready):
                ready(m)
                for h, (o, n) in enumerate(HALVES):
                    if not (isinstance(m, int) and m == 0):
                        act.wait_ge(sq_used, m * 2 + (SQ0[key] + h - 1))
                    act.activation(sq[:, o:o + n], src[:, o:o + n], ACT.Square).then_inc(sq_done, 1)

            def rms(key, chunks=CH, of=rstd, which=range(NC)):
                for c in which[:len(chunks)]:
                    o, n = chunks[c]
                    act.wait_ge(ssq_ev, SUM0[key] + c + 1)
                    act.activation(of[:, o:o + n], of[:, o:o + n], ACT.Sqrt).then_inc(rms_done, 1)

            def hi_parts(key, src, gain=None, ready=None, chunks=range(NC), tiles=range(KT)):
                for c in chunks:
                    o, n = CH[c]
                    if ready:
                        ready(c)
                    for k in tiles:
                        act.activation(act_hi[:, k, o:o + n], src(k)[:, o:o + n], ACT.Copy,
                                       scale=c_(gain, k) if gain else 1.0).then_inc(act_hi_done, 1)

            def chunk_squares(c):
                o, n = CH[c]
                for m in range(KT):
                    i, at_ = c * KT + m, HALVES[m % 2][0]
                    if i >= 2:
                        act.wait_ge(sq_used, SQ0["ffn1"] + i - 1)
                    act.activation(sq[:, at_:at_ + n], x[:, m, o:o + n], ACT.Square).then_inc(sq_done, 1)

            def silu(f, t, c):
                o, n = CH[c]
                act.wait_ge(f["gate_ev"], t * NC + c + 1)
                act.activation(gate_t[:, o:o + n], gate_t[:, o:o + n], ACT.Silu).then_inc(f["silu"], 1)

            def ffn_tile(f, t, s, down_done, silus=range(NC)):
                for c in silus:
                    silu(f, t, c)
                if down_done is not None:
                    act.wait_ge(f["dn_mm"], down_done)
                for c, (o, n) in enumerate(CH):
                    act.wait_ge(f["hid_f"], t * NC + c + 1)
                    act.activation(hid_hi[s][:, o:o + n], hid_t[:, o:o + n], ACT.Copy).then_inc(f["hid_hi"], 1)

            def lru_parameters():
                act.wait_ge(lru_sp, 1)
                act.activation(lrup[:, 2, :], lrup[:, 2, :], ACT.Exp, scale=-1.0).then_inc(lru_sp, 1)

            def ffn_layer(f, between=lambda: None, silus=range(NC)):
                ffn_tile(f, 0, 0, None, silus)
                ffn_tile(f, 1, 1, None)
                between()
                with act.Fori(1, FI) as i:
                    ffn_tile(f, i * 2, 0, i * (NC * KT))
                    ffn_tile(f, i * 2 + 1, 1, i * (NC * KT))

            def x_tile(k):
                return x[:, k, :]

            act.wait_ge(cst_in, 16)
            for c in range(NC):
                act.wait_ge(x_in[c], 16)
                hi_parts("ffn1", x_tile, "g_ffn1", chunks=[c])
                if c < NC - 1:
                    chunk_squares(c)
            rms("ffn1", which=range(NC - 1))
            silu(ffn["ffn1"], 0, 0)
            chunk_squares(NC - 1)
            silu(ffn["ffn1"], 0, 1)
            rms("ffn1", which=range(NC - 1, NC))
            ffn_layer(ffn["ffn1"], lru_parameters, silus=range(NC - 1, NC))
            hi_parts("mix", x_tile, "g_mix",
                     ready=lambda c: act.wait_ge(ffn["ffn1"]["dn_ev"], 8 + (FI - 1) * NC * KT + KT * (c + 1)))
            squares("mix", KT, x_tile, lambda m: None)
            rms("mix")

            for ct in range(LT):
                act.wait_ge(conv_done, ct + 1)
                act.activation(mix[:, M_U + ct, :], t_conv[:, :], ACT.Copy).then_inc(conv_back, 1)
            for ct in range(LT):
                if ct:
                    act.wait_ge(lru_y, ct)
                for j in range(2 * NC):
                    n_ = ct * 2 * NC + j
                    o, n = CH[j % NC]
                    act.wait_ge(lru_mm, n_ + 1)
                    gate, bias = (t_a, "b_a") if j < NC else (t_b, "b_i")
                    act.activation(gate[:, o:o + n], ps[:, 6 + n_ % 2, 0:n], ACT.Sigmoid, bias=c_(bias, ct))\
                       .then_inc(lru_ev, 1)
                act.wait_ge(lru_ev, ct * 2 * NC + NC)
                act.activation(t_conv[:, :], t_a[:, :], ACT.Tanh, scale=lrup[:, 6, ct:ct + 1]).then_inc(lru_th, 1)
                act.activation(t_a[:, :], t_a[:, :], ACT.Exp, scale=lrup[:, 7, ct:ct + 1]).then_inc(lru_a, 1)
                act.wait_ge(lru_q, ct + 1)
                act.activation(t_conv[:, :], t_conv[:, :], ACT.Sqrt).then_inc(lru_s, 1)
                if ct == 0:
                    act.wait_ge(g_ev["in"], 6 + 8 * NC)
                    act.activation(mix[:, M_G:M_G + LT, :], mix[:, M_G:M_G + LT, :], ACT.Gelu_apprx_tanh)\
                       .then_inc(gate_gelu, 1)
            act.wait_ge(lru_y, LT)
            act.dma_start(t_out["small"], small[:, :]).then_inc(stored, 16)
            squares("lru", LT, lambda m: mix[:, M_U + m, :], lambda m: None)
            act.wait_ge(mem_in, 16)
            act.activation(mem_sq[:, :, :], mem_raw[:, :, :], ACT.Square).then_inc(sq_done, 1)
            rms("lru", of=lru_rstd)
            rms("mem", [(0, NM)], of=acc)
            act.wait_ge(mem_normed, 1)
            act.wait_ge(w_mm[1], groups_before(PAIR_KV))
            act.activation(memn_hi[:, :, :], mem_raw[:, :, :], ACT.Copy).then_inc(memn_hi_done, 1)

            def exps(b, s):
                act.wait_ge(nmax_done, b + 1)
                for h in range(NH):
                    act.activation(s_m[s][:, h, :], s_m[s][:, h, :], ACT.Exp, bias=st8[:, 1, h:h + 1],
                                   scale=HD ** -0.5, accum_out=st8[:, 4, h:h + 1])
                act.activation(st8[:, 3, :], st8[:, 2, :], ACT.Exp).then_inc(exp_done, 1)

            def take_v(b, s):
                act.wait_ge(vt_mm, b + 1)
                act.activation(v_n[s][:, :], ps[:, 7, WIN:2 * WIN], ACT.Copy).then_inc(vt_ev, 1)

            def block_step(b, s, more=True):
                for kv in range(KVH):
                    act.wait_ge(pt_mm, b * 2 + kv + 1)
                    act.activation(p_T[:, :, kv * GRP:(kv + 1) * GRP, :], ps[:, 4:6, :], ACT.Copy)\
                       .then_inc(pt_ev, 1)
                if more:
                    exps(b + 1, 1 - s)
                    take_v(b + 1, 1 - s)

            act.sem_inc(pt_ev, 1)
            exps(0, 0)
            take_v(0, 0)
            with act.Fori(0, NB // 2 - 1) as i:
                block_step(i * 2, 0)
                block_step(i * 2 + 1, 1)
            block_step(NB - 2, 0)
            act.wait_ge(rope_done, NB)
            act.wait_ge(vt_ev, NB)
            act.dma_start(t_out["k_prompt"], k_r[:, 1, :]).then_inc(stored, 16)
            act.dma_start(t_out["v_prompt"], v_n[1][:, :]).then_inc(stored, 16)
            act.wait_ge(s_rot_mm, 1 + NS)
            act.activation(vs_n[:, :, :], ps[0:LS, 4:6, :], ACT.Copy).then_inc(s_pt_ev, 1)
            block_step(NB - 1, 1, more=False)
            act.wait_ge(s_rope, 1)
            act.dma_start(t_out["k_sample"][:, :, 0:WIN - LS], kc_T[:, :, LS:WIN]).then_inc(stored, 16)
            act.dma_start(t_out["k_sample"][:, :, WIN - LS:WIN], ks_r[:, :].rearrange("p (b t) -> p b t", b=NS))\
               .then_inc(stored, 16)
            act.dma_start(t_out["v_sample"][0:WIN - LS, :, :], v_c[LS:WIN, :, :]).then_inc(stored, 16)
            act.wait_ge(s_pt_ev, 1)
            act.dma_start(t_out["v_sample"][WIN - LS:WIN, :, :], vs_n[:, :, :]).then_inc(stored, 16)
            act.wait_ge(s_nmax, 1)
            for t in range(4):
                act.activation(ss_m[:, t, :], ss_m[:, t, :], ACT.Exp, bias=st8[:, 1, t:t + 1], scale=HD ** -0.5,
                               accum_out=st8[:, 4, t:t + 1])
            act.activation(st8[:, 3, 0:4], st8[:, 2, 0:4], ACT.Exp).then_inc(s_exp, 1)
            act.wait_ge(s_pt_mm, 1)
            act.activation(pcs_T[:, :, :], ps[:, 2, :], ACT.Copy).then_inc(s_pt_ev, 1)
            act.activation(pns_T[:, :, :], ps[0:LS, 3, :], ACT.Copy).then_inc(s_pt_ev, 1)

            def cat_tile(k):
                return mix[:, M_U + k, :] if k < LT else mix[:, M_Q + k - LT, :]

            act.wait_ge(s_o_ev, 1)
            act.wait_ge(stored, 16 * 7)
            squares("attn", LT, lambda m: mix[:, M_Q + m, :], lambda m: None)
            act.wait_ge(lru_normed, LT)
            act.wait_ge(s_pv_mm, 1)
            hi_parts("cat", cat_tile, "g_cat", chunks=[0], tiles=range(LT))
            rms("attn")
            for c in range(NC):
                hi_parts("cat", cat_tile, "g_cat", lambda c: act.wait_ge(attn_normed, c + 1), [c], range(LT, KT))
                if c < NC - 1:
                    hi_parts("cat", cat_tile, "g_cat", chunks=[c + 1], tiles=range(LT))
            act.dma_start(t_out["mem_k"], mem_kT[:, :, :]).then_inc(stored, 16)
            act.dma_start(t_out["mem_v"], mem_v[:, :, :]).then_inc(stored, 16)

            def plain_squares(stage, key):
                def ready(m):
                    act.wait_ge(g_ev[stage], m * NC + (6 + NC))
                for m in range(2):
                    square(key, m, x[:, m, :], ready)
                with act.Fori(2, KT) as m:
                    square(key, m, x[:, m, :], ready)

            plain_squares("out", "xattn")
            act.wait_ge(w_mm[1], groups_before(PAIR_CQ))
            hi_parts("xattn", x_tile, "g_xattn")
            rms("xattn")

            def x_exps(b, s):
                act.wait_ge(x_nmax, b + 1)
                for h in range(XH):
                    act.activation(xs_m[s][:, h, :], ps[:, h // 2, (h % 2) * NM:(h % 2 + 1) * NM], ACT.Exp,
                                   bias=xst[:, s, 1, h:h + 1], scale=XD ** -0.5, accum_out=xst[:, s, 2, h:h + 1])
                act.activation(ys_m[s][:, :], ps[:, 2, 0:NM], ACT.Exp, bias=yst[:, s * 4 + 1:s * 4 + 2],
                               scale=XD ** -0.5, accum_out=yst[:, s * 4 + 2:s * 4 + 3]).then_inc(x_exp, 1)

            def y_back(b):
                return act.activation(
                    xq[:, :, bass.ds(b * LS, LS)],
                    ps[:, 5, NM:2 * NM].rearrange("p (d w) -> p d w", d=2)[:, :, 0:P]
                    .rearrange("p d (h w) -> p h d w", h=XH)[:, :, :, 0:LS], ACT.Copy)

            def x_step(b, s, more=True, after=True):
                act.wait_ge(x_turned, b + 1)
                act.activation(xp_T[:, :, :, :], ps[:, 3:5, :], ACT.Copy)
                act.wait_ge(x_pt_mm, b + 1)
                if after:
                    y_back(b - 1)
                act.activation(yp_T[:, :, :], ps[:, 5, 0:2 * P], ACT.Copy).then_inc(x_pt_ev, 1)
                if more:
                    x_exps(b + 1, 1 - s)
                act.wait_ge(y_mm, b + 1)
                act.activation(y_s[:, :], ps[:, 5, NM:2 * NM], ACT.Copy).then_inc(y_ev, 1)

            act.sem_inc(x_exp, 1)
            act.sem_inc(x_pt_ev, 1)
            x_exps(0, 0)
            x_step(0, 0, after=False)
            x_step(1, 1)
            with act.Fori(1, NB // 2 - 1) as i:
                x_step(i * 2, 0)
                x_step(i * 2 + 1, 1)
            x_step(NB - 2, 0)
            x_step(NB - 1, 1, more=False)
            act.wait_ge(x_pt_mm, NB + 1)
            y_back(NB - 1).then_inc(y_ev, 1)
            act.wait_ge(y_ev, NB + 1)

            act.wait_ge(x_pv_mm, NB)
            act.wait_ge(x_o_ev, 1 + NB)
            hi_parts("co", lambda k: xq[:, k, :])
            plain_squares("co", "ffn2")
            act.wait_ge(w_mm[1], groups_before(PAIRS))
            hi_parts("ffn2", x_tile, "g_ffn2")
            rms("ffn2")
            act.wait_ge(stored, 16 * 9)
            ffn_layer(ffn["ffn2"])
            squares("final", KT, x_tile,
                    lambda m: act.wait_ge(ffn["ffn2"]["dn_ev"], 8 + (FI - 1) * NC * KT + NC * (m + 1)))
            for m in range(YT, KT):
                act.activation(y[:, m, :], x[:, m, :], ACT.Copy, scale=c_("g_final", m)).then_inc(y_gain, 1)
            rms("final")
            for c, (o, n) in enumerate(CH):
                act.wait_ge(y_done, c + 1)
                act.wait_ge(y_pool, c + 1)
                act.dma_start(t_out["y"][:, :, o:o + n], y[:, :, o:o + n]).then_inc(stored, 16)
            act.wait_ge(stored, 16 * (9 + NC))

        @block.vector
        def _(dve):
            own = Steps(dve, dve_own)

            def take_out(out, src):
                return dve.tensor_scalar(out, src, 1.0, None, ALU.mult)

            def add_square(key, m):
                for h, (o, n) in enumerate(HALVES):
                    dve.wait_ge(sq_done, m * 2 + (SQ0[key] + h + 1))
                    if isinstance(m, int) and m == 0:
                        dve.tensor_copy(acc[:, o:o + n], sq[:, o:o + n]).then_inc(sq_used, 1)
                    else:
                        dve.wait_ge(sq_used, m * 2 + (SQ0[key] + h - 1))
                        dve.tensor_tensor(acc[:, o:o + n], acc[:, o:o + n], sq[:, o:o + n], ALU.add)\
                           .then_inc(sq_used, 1)

            def mean_squares(key, width, chunks=CH, to=rstd, which=range(NC)):
                for c in which[:len(chunks)]:
                    o, n = chunks[c]
                    dve.wait_ge(ssq_mm, SUM0[key] + c + 1)
                    dve.tensor_scalar(to[:, o:o + n], ps[:, 6 + c % 2, 0:n], 1.0 / width, EPS, ALU.mult, ALU.add)\
                       .then_inc(ssq_ev, 1)

            def inverse_rms(key, chunks=CH, then=None, to=rstd, which=range(NC)):
                for c in which[:len(chunks)]:
                    o, n = chunks[c]
                    dve.wait_ge(rms_done, SUM0[key] + c + 1)
                    dve.reciprocal(to[:, o:o + n], to[:, o:o + n]).then_inc(rstd_done, 1)
                    if then or c == which[:len(chunks)][-1]:
                        dve.wait_ge(rstd_done, SUM0[key] + c + 1)
                    if then:
                        then(c)

            def lo_parts(key, src, gain=None, chunks=range(NC), tiles=range(KT)):
                for c in chunks:
                    o, n = CH[c]
                    for k in tiles:
                        dve.wait_ge(act_hi_done, SPLIT0[key] + c * KT + k + 1)
                        hi = act_hi[:, k, o:o + n].bitcast(F32)
                        if gain:
                            ins = dve.scalar_tensor_tensor(out=act_lo[:, k, o:o + n], in0=src(k)[:, o:o + n],
                                                           scalar=c_(gain, k), in1=hi, op0=ALU.mult,
                                                           op1=ALU.subtract)
                        else:
                            ins = dve.tensor_tensor(act_lo[:, k, o:o + n], src(k)[:, o:o + n], hi, ALU.subtract)
                        ins.then_inc(act_lo_done, 1)

            def ffn_gate(f, t, c):
                o, n = CH[c]
                dve.wait_ge(f["gate_mm"], t * NC + c + 1)
                dve.tensor_tensor(gate_t[:, o:o + n], ps[:, c, 0:n], rstd[:, o:o + n], ALU.mult)\
                   .then_inc(f["gate_ev"], 1)

            def ffn_up(f, t, c):
                o, n = CH[c]
                dve.wait_ge(f["up_mm"], t * NC + c + 1)
                dve.wait_ge(f["silu"], t * NC + c + 1)
                dve.tensor_tensor(hid_t[:, o:o + n], ps[:, 3 + c, 0:n], gate_t[:, o:o + n], ALU.mult)\
                   .then_inc(f["up_ev"], 1)
                dve.wait_ge(f["up_ev"], t * NC + c + 1)
                dve.tensor_tensor(hid_t[:, o:o + n], hid_t[:, o:o + n], rstd[:, o:o + n], ALU.mult)\
                   .then_inc(f["hid_f"], 1)

            def ffn_hidden(f, t):
                ffn_gate(f, t, 0)
                ffn_gate(f, t, 1)
                ffn_up(f, t, 0)
                ffn_gate(f, t, 2)
                ffn_up(f, t, 1)
                ffn_up(f, t, 2)

            def ffn_lo(f, t, s):
                for c, (o, n) in enumerate(CH):
                    dve.wait_ge(f["hid_hi"], t * NC + c + 1)
                    dve.tensor_tensor(hid_lo[s][:, o:o + n], hid_t[:, o:o + n],
                                      hid_hi[s][:, o:o + n].bitcast(F32), ALU.subtract).then_inc(f["hid_lo"], 1)

            def ffn_take(f, j, m, c, n_):
                o, n = CH[c]
                dve.wait_ge(f["dn_mm"], j * (NC * KT) + (n_ + 1))
                dve.scalar_tensor_tensor(out=x[:, m, o:o + n], in0=ps[:, DOWN_BANKS[n_ % 8], 0:n], scalar=0.5,
                                         in1=x[:, m, o:o + n], op0=ALU.mult, op1=ALU.add).then_inc(f["dn_ev"], 1)

            def add_chunk_squares(c):
                o, n = CH[c]
                for m in range(KT):
                    i, at_ = c * KT + m, HALVES[m % 2][0]
                    dve.wait_ge(sq_done, SQ0["ffn1"] + i + 1)
                    if m == 0:
                        dve.tensor_copy(acc[:, o:o + n], sq[:, at_:at_ + n]).then_inc(sq_used, 1)
                    else:
                        dve.wait_ge(sq_used, SQ0["ffn1"] + i)
                        dve.tensor_tensor(acc[:, o:o + n], acc[:, o:o + n], sq[:, at_:at_ + n], ALU.add)\
                           .then_inc(sq_used, 1)

            def ffn_layer(f, key, between=lambda: None):
                dve.sem_inc(f["dn_ev"], 8)
                if key == "ffn1":
                    inverse_rms(key, then=lambda c: ffn_gate(f, 0, c), which=[0])
                    inverse_rms(key, which=[1])
                    ffn_up(f, 0, 0)
                    add_chunk_squares(2)
                    ffn_gate(f, 0, 1)
                    ffn_up(f, 0, 1)
                    mean_squares(key, D, which=[2])
                    inverse_rms(key, then=lambda c: ffn_gate(f, 0, c), which=[2])
                    ffn_up(f, 0, 2)
                else:
                    inverse_rms(key, then=lambda c: ffn_gate(f, 0, c))
                    for c in range(NC):
                        ffn_up(f, 0, c)
                ffn_lo(f, 0, 0)
                ffn_hidden(f, 1)
                ffn_lo(f, 1, 1)
                between()
                with dve.Fori(1, FI) as i:
                    ffn_hidden(f, i * 2)
                    dve.wait_ge(f["dn_ev"], i * (NC * KT) + (8 - NC * KT))
                    for n_ in range(NC * KT):
                        ffn_take(f, i - 1, n_ // NC, n_ % NC, n_)
                    ffn_lo(f, i * 2, 0)
                    ffn_hidden(f, i * 2 + 1)
                    ffn_lo(f, i * 2 + 1, 1)
                dve.wait_ge(f["dn_ev"], (FI - 1) * NC * KT + 8)

            def x_tile(k):
                return x[:, k, :]

            def scaled_take(stage, s, p, dst, chunks=range(NC)):
                for c in chunks:
                    o, n = CH[c]
                    dve.wait_ge(w_mm[s], slot_groups(stage, p, c))
                    dve.tensor_tensor(dst[:, o:o + n], ps[:, 3 * s + c, 0:n], rstd[:, o:o + n], ALU.mult)\
                       .then_inc(g_ev[stage], 1)

            def slot_groups(stage, p, c):
                a, _, base, each = GROUPS[0] if stage == "in" else GROUPS[2]
                return p * each + (base - a * each + c + 1)

            dve.memset(ones[:, :], 1.0).then_inc(ones_set, 1)
            dve.wait_ge(cst_in, 16)
            for c in range(2):
                lo_parts("ffn1", x_tile, "g_ffn1", [c])
                add_chunk_squares(c)
            mean_squares("ffn1", D, which=[0])
            lo_parts("ffn1", x_tile, "g_ffn1", [2])
            mean_squares("ffn1", D, which=[1])

            def lru_parameters():
                lam, neg, e, den, z, z2, ser = (c_("lam", 0, LT), lrup[:, 1, :], lrup[:, 2, :], lrup[:, 3, :],
                                                lrup[:, 0, :], lrup[:, 4, :], lrup[:, 5, :])
                own.done(dve.tensor_scalar(neg, lam, -1.0, None, ALU.mult))
                dve.tensor_tensor(e, lam, neg, ALU.max).then_inc(lru_sp, 1)
                dve.wait_ge(lru_sp, 2)
                own.done(dve.tensor_scalar(den, e, 2.0, None, ALU.add))
                own.done(dve.reciprocal(den, den))
                own.done(dve.tensor_tensor(z, e, den, ALU.mult))
                own.done(dve.tensor_tensor(z2, z, z, ALU.mult))
                own.done(dve.tensor_scalar(ser, z2, 1.0 / 17, 1.0 / 15, ALU.mult, ALU.add))
                for k in (13, 11, 9, 7, 5, 3, 1):
                    own.done(dve.tensor_tensor(ser, ser, z2, ALU.mult))
                    own.done(dve.tensor_scalar(ser, ser, 1.0 / k, None, ALU.add))
                own.done(dve.tensor_tensor(ser, ser, z, ALU.mult))
                own.done(dve.tensor_scalar(ser, ser, 16.0, None, ALU.mult))
                own.done(dve.tensor_scalar(neg, neg, 0.0, 8.0, ALU.max, ALU.mult))
                own.done(dve.tensor_tensor(lrup[:, 6, :], ser, neg, ALU.add))
                own.done(dve.tensor_scalar(lrup[:, 7, :], lrup[:, 6, :], -1.0, None, ALU.mult))

            ffn_layer(ffn["ffn1"], "ffn1", lru_parameters)
            for c in range(NC):
                for m in range(KT):
                    ffn_take(ffn["ffn1"], FI - 1, m, c, c * KT + m)
                dve.wait_ge(ffn["ffn1"]["dn_ev"], (FI - 1) * NC * KT + 8 + (c + 1) * KT)
                if c == NC - 1:
                    dve.sem_inc(g_ev["in"], 6)
                lo_parts("mix", x_tile, "g_mix", [c])
            for m in range(KT):
                add_square("mix", m)
            mean_squares("mix", D)
            inverse_rms("mix", then=lambda c: scaled_take("in", 0, 0, mix[:, 0, :], [c]))
            scaled_take("in", 1, 0, mix[:, 1, :])

            for m in (2, 3):
                scaled_take("in", m % 2, 1, mix[:, m, :])

            own.base, own.n = own.base + own.n, 0
            dve.wait_ge(g_ev["in"], 6 + 4 * NC)
            for ct in range(LT):
                u = mix[:, M_U + ct, :]
                us = u[:, 0:TS].rearrange("p (b t) -> p b t", b=NS)
                cs = t_conv[:, 0:TS].rearrange("p (b t) -> p b t", b=NS)
                o, _ = COLS["hist"]
                hist = cst[:, o + ct * NS * 3:o + (ct + 1) * NS * 3].rearrange("p (b t) -> p b t", b=NS)
                if ct:
                    dve.wait_ge(conv_back, ct)
                dve.tensor_copy(small[:, SM_CP + ct * 3:SM_CP + ct * 3 + 3], u[:, T - 3:T])
                dve.tensor_copy(small[:, SM_CS + ct * NS * 3:SM_CS + (ct + 1) * NS * 3]
                                .rearrange("p (b t) -> p b t", b=NS), us[:, :, LS - 3:LS])
                own.done(dve.tensor_scalar(t_conv[:, :], u, c_("conv_w", 3 * LT + ct), c_("conv_b", ct), ALU.mult,
                                           ALU.add))
                for d in (1, 2, 3):
                    w = c_("conv_w", (3 - d) * LT + ct)
                    parts = [(t_conv[:, TS + d:T], u[:, TS:T - d]), (cs[:, :, d:LS], us[:, :, 0:LS - d]),
                             (cs[:, :, 0:d], hist[:, :, 3 - d:3])]
                    for n_, (to, src) in enumerate(parts):
                        ins = dve.scalar_tensor_tensor(out=to, in0=src, scalar=w, in1=to, op0=ALU.mult, op1=ALU.add)
                        if d == 3 and n_ == 2:
                            ins.then_inc(conv_done, 1)
                        else:
                            own.done(ins)
                scaled_take("in", ct % 2, 2 + ct // 2, mix[:, M_G + ct, :])

            def lru_gated(ct):
                u = mix[:, M_U + ct, :]
                dve.wait_ge(lru_ev, (ct + 1) * 2 * NC)
                own.done(dve.tensor_tensor(t_b[:, :], t_b[:, :], u, ALU.mult))
                dve.wait_ge(lru_a, ct + 1)
                own.done(dve.tensor_tensor(u, t_a[:, :], t_a[:, :], ALU.mult))
                dve.wait_ge(lru_th, ct + 1)
                dve.scalar_tensor_tensor(out=t_conv[:, :], in0=u, scalar=1.0, in1=t_conv[:, :], op0=ALU.add,
                                         op1=ALU.mult).then_inc(lru_q, 1)

            def lru_scan(ct):
                u, g = mix[:, M_U + ct, :], mix[:, M_G + ct, :]
                tmp = small[:, SM_HS + ct * NS:SM_HS + (ct + 1) * NS]
                own.done(dve.tensor_tensor(tmp, t_a[:, 0:TS:LS], c_("h0", ct * NS, NS), ALU.mult))
                own.done(dve.memset(t_a[:, 0:TS + 1:LS], 0.0))
                dve.wait_ge(lru_s, ct + 1)
                own.done(dve.tensor_tensor(t_b[:, :], t_conv[:, :], t_b[:, :], ALU.mult))
                own.done(dve.tensor_tensor(t_b[:, 0:TS:LS], t_b[:, 0:TS:LS], tmp, ALU.add))
                own.done(dve.tensor_tensor_scan(u, t_a[:, :], t_b[:, :], 0.0, ALU.mult, ALU.add))
                own.done(dve.tensor_copy(tmp, u[:, LS - 1:TS:LS]))
                own.done(dve.tensor_copy(small[:, SM_HP + ct:SM_HP + ct + 1], u[:, T - 1:T]))
                if ct == 0:
                    dve.wait_ge(gate_gelu, 1)
                dve.tensor_tensor(u, u, g, ALU.mult).then_inc(lru_y, 1)

            for ct in range(LT):
                lru_gated(ct)
                if ct:
                    scaled_take("in", (ct - 1) % 2, (7 + ct) // 2, mix[:, 7 + ct, :])
                lru_scan(ct)
            scaled_take("in", 1, 5, mix[:, 11, :])
            for ct in range(LT):
                add_square("lru", ct)
            scaled_take("in", 0, 6, mix[:, 12, :])
            mean_squares("lru", LRU, to=lru_rstd)
            inverse_rms("lru", to=lru_rstd)

            dve.wait_ge(sq_done, SQ0["mem"] + 1)
            dve.tensor_reduce(sq[:, 0:NM], mem_sq[:, :, :].rearrange("p k t -> p t k"), AX_X, ALU.add)\
               .then_inc(sq_used, 1)
            mean_squares("mem", D, [(0, NM)], to=acc)
            inverse_rms("mem", [(0, NM)], to=acc)
            for k in range(KT):
                ins = dve.scalar_tensor_tensor(out=mem_raw[:, k, :], in0=mem_raw[:, k, :], scalar=c_("g_mem", k),
                                               in1=acc[:, 0:NM], op0=ALU.mult, op1=ALU.mult)
            ins.then_inc(mem_normed, 1)
            scaled_take("in", 1, 6, mix[:, 13, :])
            dve.wait_ge(memn_hi_done, 1)
            dve.tensor_tensor(memn_lo[:, :, :], mem_raw[:, :, :], memn_hi[:, :, :].bitcast(F32), ALU.subtract)\
               .then_inc(memn_lo_done, 1)

            dve.memset(k_r[:, 1, :], 0.0)
            own.done(dve.memset(v_n[1][:, :], 0.0))
            own.done(dve.tensor_scalar(st8[:, 7, :], c_("sink", 0, NH), HD ** 0.5, None, ALU.mult))
            dve.sem_inc(sc_taken, 1)
            dve.sem_inc(o_ev, 1)
            dve.sem_inc(kv_ev, 1)
            dve.wait_ge(rope_tab, 64)

            def blk(b):
                return bass.ds(b * WIN + TS, WIN)

            def over(ap, n, w):
                return ap.unsqueeze(1).to_broadcast([P, n, w])

            def rope_read(b):
                sin = rope_sin[:, blk(b)]
                dve.wait_ge(rot_mm, b + 1)
                dve.tensor_tensor(rot_q[:, :, :], ps[:, 6, :].rearrange("p (g w) -> p g w", g=GRP),
                                  over(sin, GRP, WIN), ALU.mult)
                dve.tensor_tensor(rot_k[:, :], ps[:, 7, 0:WIN], sin, ALU.mult).then_inc(rot_ev, 1)

            def rope(b, s, steps):
                cos = rope_cos[:, blk(b)]
                dve.tensor_tensor(q_r[:, :, :], mix[:, M_Q:M_Q + GRP, blk(b)], over(cos, GRP, WIN), ALU.mult)
                steps.done(dve.tensor_tensor(k_r[:, s, :], mix[:, M_K, blk(b)], cos, ALU.mult))
                dve.wait_ge(rot_ev, b + 1)
                dve.tensor_tensor(q_r[:, :, :], q_r[:, :, :], rot_q[:, :, :], ALU.add)
                dve.tensor_tensor(k_r[:, s, :], k_r[:, s, :], rot_k[:, :], ALU.add).then_inc(rope_done, 1)

            def add_mask(b, s, mask):
                dve.wait_ge(sc_mm, b + 1)
                dve.tensor_tensor(s_m[s][:, :, :], ps[:, 0:4, :].rearrange("p a (h w) -> p (a h) w", w=2 * WIN),
                                  over(mask, NH, 2 * WIN), ALU.add).then_inc(sc_taken, 1)

            def maxima(b, s, steps):
                dve.wait_ge(sc_taken, b + 2)
                steps.done(dve.tensor_reduce(st8[:, 0, :], s_m[s][:, :, :], AX_X, ALU.max))
                steps.done(dve.tensor_tensor(st8[:, 0, :], st8[:, 0, :], st8[:, 7, :], ALU.max))
                steps.done(dve.tensor_scalar(st8[:, 1, :], st8[:, 0, :], -(HD ** -0.5), None, ALU.mult))
                dve.tensor_tensor(st8[:, 2, :], st8[:, 1, :], c_("sink", 0, NH), ALU.add).then_inc(nmax_done, 1)

            def probabilities(b, s, steps):
                dve.wait_ge(exp_done, b + 1)
                steps.done(dve.tensor_tensor(st8[:, 5, :], st8[:, 3, :], st8[:, 4, :], ALU.add))
                steps.done(dve.reciprocal(st8[:, 6, :], st8[:, 5, :]))
                dve.tensor_tensor(s_m[s][:, :, :], s_m[s][:, :, :],
                                  st8[:, 6, :].unsqueeze(2).to_broadcast([P, NH, 2 * WIN]), ALU.mult)\
                   .then_inc(p_done, 1)

            def stage_v(b):
                if not (isinstance(b, int) and b == 0):
                    dve.wait_ge(vt_mm, b)
                take_out(v_b[:, :], mix[:, M_V, blk(b)]).then_inc(v_st, 1)

            ROPE_STEPS, SWA_STEPS = 1, 5

            def take_memory(b, s, j):
                dve.wait_ge(mem_mm, b * 2 + j + 1)
                if s == 0:
                    to = mem_kT[:, bass.ds(b + j, 1), :].squeeze(1)
                else:
                    to = mem_v[:, j, bass.ds(b * P - P, 2 * P)]
                take_out(to, ps[:, 7, 256:512]).then_inc(kv_ev, 1)

            def take_result(b):
                dve.wait_ge(pv_mm, b + 1)
                take_out(mix[:, M_Q:M_Q + GRP, blk(b)], ps[:, 6, :].rearrange("p (g w) -> p g w", g=GRP))\
                    .then_inc(o_ev, 1)

            def block_step(b, s, rot=True):
                steps = Steps(dve, swa_own, b * (ROPE_STEPS + SWA_STEPS) + (2 * ROPE_STEPS + SWA_STEPS))
                add_mask(b + 1, 1 - s, masks[:, 2 - s, :])
                if rot:
                    rope_read(b + 2)
                maxima(b + 1, 1 - s, steps)
                if rot:
                    rope(b + 2, s, steps)
                stage_v(b + 1)
                for j in range(2):
                    take_memory(b, s, j)
                probabilities(b + 1, 1 - s, steps)
                assert steps.n == SWA_STEPS + (ROPE_STEPS if rot else 0)
                take_result(b)

            first = Steps(dve, swa_own, 0)
            rope_read(0)
            rope(0, 0, first)
            stage_v(0)
            dve.wait_ge(swa_tab, 16)
            add_mask(0, 0, masks[:, 0, :])
            maxima(0, 0, first)
            rope_read(1)
            rope(1, 1, first)
            probabilities(0, 0, first)
            with dve.Fori(0, NB // 2 - 1) as i:
                block_step(i * 2, 0)
                block_step(i * 2 + 1, 1)
            block_step(NB - 2, 0, rot=False)
            own.base, own.n = own.base + own.n, 0
            dve.wait_ge(s_rot_mm, 1)
            cos, sin = rope_cos[:, 0:TS], rope_sin[:, 0:TS]
            dve.tensor_tensor(rot_q[:, :, 0:TS], ps[:, 6, 0:256].rearrange("p (g w) -> p g w", g=GRP),
                              over(sin, GRP, TS), ALU.mult)
            dve.tensor_tensor(rot_k[:, 0:TS], ps[:, 6, 256:256 + TS], sin, ALU.mult)
            dve.tensor_tensor(q_r[:, :, 0:TS], mix[:, M_Q:M_Q + GRP, 0:TS], over(cos, GRP, TS), ALU.mult)
            own.done(dve.tensor_tensor(ks_r[:, :], mix[:, M_K, 0:TS], cos, ALU.mult))
            dve.tensor_tensor(qs_r[:, :, :, :].rearrange("p b g t -> p g b t"),
                              q_r[:, :, 0:TS].rearrange("p g (b t) -> p g b t", b=NS),
                              rot_q[:, :, 0:TS].rearrange("p g (b t) -> p g b t", b=NS), ALU.add)
            dve.tensor_tensor(ks_r[:, :], ks_r[:, :], rot_k[:, 0:TS], ALU.add).then_inc(s_rope, 1)
            take_memory(NB - 1, 1, 0)
            own.done(dve.tensor_scalar(st8[:, 7, 0:4], c_("sink_s", 0, 4), HD ** 0.5, None, ALU.mult))
            dve.wait_ge(kvc_in, 48)
            dve.wait_ge(s_sc_mm, 1)
            own.done(dve.tensor_tensor(ss_m[:, :, :], ps[:, 0:4, 0:WIN + LS], over(mask_s[:, :], 4, WIN + LS),
                                       ALU.add))
            own.done(dve.tensor_reduce(st8[:, 0, 0:4], ss_m[:, :, :], AX_X, ALU.max))
            own.done(dve.tensor_tensor(st8[:, 0, 0:4], st8[:, 0, 0:4], st8[:, 7, 0:4], ALU.max))
            own.done(dve.tensor_scalar(st8[:, 1, 0:4], st8[:, 0, 0:4], -(HD ** -0.5), None, ALU.mult))
            dve.tensor_tensor(st8[:, 2, 0:4], st8[:, 1, 0:4], c_("sink_s", 0, 4), ALU.add).then_inc(s_nmax, 1)
            take_memory(NB - 1, 1, 1)
            dve.wait_ge(s_exp, 1)
            own.done(dve.tensor_tensor(st8[:, 5, 0:4], st8[:, 3, 0:4], st8[:, 4, 0:4], ALU.add))
            own.done(dve.reciprocal(st8[:, 6, 0:4], st8[:, 5, 0:4]))
            dve.tensor_tensor(ss_m[:, :, :], ss_m[:, :, :],
                              st8[:, 6, 0:4].unsqueeze(2).to_broadcast([P, 4, WIN + LS]), ALU.mult).then_inc(s_p, 1)
            take_result(NB - 1)
            dve.wait_ge(s_pv_mm, 1)
            dve.tensor_copy(mix[:, M_Q:M_Q + GRP, 0:TS].rearrange("p g (b t) -> p g b t", b=NS),
                            ps[:, 6, 0:256].rearrange("p (b g t) -> p g b t", b=NS, g=GRP)).then_inc(s_o_ev, 1)

            dve.wait_ge(stored, 16 * 7)
            for ct in range(LT):
                add_square("attn", ct)
            dve.sem_inc(g_ev["out"], 6)

            def cat_tile(k):
                return mix[:, M_U + k, :] if k < LT else mix[:, M_Q + k - LT, :]

            def attn_norm(c):
                o, n = CH[c]
                for ct in range(LT):
                    ins = dve.tensor_tensor(mix[:, M_Q + ct, o:o + n], mix[:, M_Q + ct, o:o + n], rstd[:, o:o + n],
                                            ALU.mult)
                ins.then_inc(attn_normed, 1)
                lo_parts("cat", cat_tile, "g_cat", [c], range(LT, KT))
                if c < NC - 1:
                    lo_parts("cat", cat_tile, "g_cat", [c + 1], range(LT))

            mean_squares("attn", LRU)
            lo_parts("cat", cat_tile, "g_cat", [0], range(LT))
            inverse_rms("attn", then=attn_norm)

            def plain_residual(stage, pair0, key):
                def take(m, p, s):
                    to = x[:, m, :] if isinstance(m, int) else x[:, bass.ds(m, 1), :].squeeze(1)
                    for c, (o, n) in enumerate(CH):
                        dve.wait_ge(w_mm[s], slot_groups(stage, p, c))
                        dve.tensor_tensor(to[:, o:o + n], ps[:, 3 * s + c, 0:n], to[:, o:o + n], ALU.add)\
                           .then_inc(g_ev[stage], 1)
                    add_square(key, m)

                for s in range(2):
                    take(s, pair0, s)
                with dve.Fori(1, KT // 2) as i:
                    for s in range(2):
                        take(i * 2 + s, i + pair0, s)
                dve.wait_ge(g_ev[stage], 6 + NC * KT)

            plain_residual("out", PAIR_OUT, "xattn")
            dve.sem_inc(g_ev["cq"], 6)
            lo_parts("xattn", x_tile, "g_xattn")
            mean_squares("xattn", D)
            inverse_rms("xattn", then=lambda c: scaled_take("cq", 0, PAIR_CQ, xq[:, 0, :], [c]))
            scaled_take("cq", 1, PAIR_CQ, xq[:, 1, :])
            with dve.Fori(1, KT // 2) as i:
                for s in range(2):
                    scaled_take("cq", s, i + PAIR_CQ, xq[:, bass.ds(i * 2 + s, 1), :].squeeze(1))
            dve.wait_ge(g_ev["cq"], 6 + NC * KT)

            def xcol(b):
                return bass.ds(b * P + TS, P)

            def x_stage(b):
                dve.tensor_copy(qs_b[:, :, :], xq[:, :, bass.ds(b * LS, 32)])
                dve.tensor_copy(xq_b[:, :, :], xq[:, :, xcol(b)]).then_inc(xq_st, 1)

            def x_soft(b, s, steps):
                dve.wait_ge(x_sc_mm, b + 1)
                steps.mark(dve.tensor_reduce(xst[:, s, 0, :], ps[:, 0:2, :].rearrange("p a (h w) -> p (a h) w", w=NM),
                                             AX_X, ALU.max))
                steps.done(dve.tensor_reduce(yst[:, 4 * s:4 * s + 1], ps[:, 2, 0:NM], AX_X, ALU.max))
                dve.tensor_scalar(xst[:, s, 1, :], xst[:, s, 0, :], -(XD ** -0.5), None, ALU.mult)
                dve.tensor_scalar(yst[:, 4 * s + 1:4 * s + 2], yst[:, 4 * s:4 * s + 1], -(XD ** -0.5), None,
                                  ALU.mult).then_inc(x_nmax, 1)

            def x_norm(b, s, steps):
                dve.wait_ge(x_exp, b + 2)
                steps.mark(dve.reciprocal(xst[:, s, 3, :], xst[:, s, 2, :]))
                steps.done(dve.reciprocal(yst[:, 4 * s + 3:4 * s + 4], yst[:, 4 * s + 2:4 * s + 3]))
                dve.tensor_tensor(xs_m[s][:, :, :], xs_m[s][:, :, :],
                                  xst[:, s, 3, :].unsqueeze(2).to_broadcast([P, XH, NM]), ALU.mult)
                dve.tensor_scalar(ys_m[s][:, :], ys_m[s][:, :], yst[:, 4 * s + 3:4 * s + 4], None, ALU.mult)\
                   .then_inc(x_p, 1)

            X_STEPS = 4

            def x_take(b):
                dve.wait_ge(x_pv_mm, b + 1)
                take_out(xq[:, :, xcol(b)], ps[:, 6:8, :].rearrange("p a (k w) -> p (a k) w", w=P))\
                    .then_inc(x_o_ev, 1)

            def x_step(b, s, more=True, stage=True):
                if more:
                    steps = Steps(dve, x_own, (b + 1) * X_STEPS)
                    x_soft(b + 1, 1 - s, steps)
                    if stage:
                        x_stage(b + 2)
                    x_norm(b + 1, 1 - s, steps)
                x_take(b)

            dve.sem_inc(x_o_ev, 1)
            x_stage(0)
            first = Steps(dve, x_own, 0)
            x_soft(0, 0, first)
            x_stage(1)
            x_norm(0, 0, first)
            with dve.Fori(0, NB // 2 - 1) as i:
                x_step(i * 2, 0)
                x_step(i * 2 + 1, 1)
            x_step(NB - 2, 0, stage=False)
            x_step(NB - 1, 1, more=False)
            dve.wait_ge(x_o_ev, 1 + NB)

            dve.wait_ge(y_ev, NB + 1)
            dve.sem_inc(g_ev["co"], 6)
            lo_parts("co", lambda k: xq[:, k, :])
            plain_residual("co", PAIR_CO, "ffn2")
            lo_parts("ffn2", x_tile, "g_ffn2", [0, 1])
            mean_squares("ffn2", D)
            lo_parts("ffn2", x_tile, "g_ffn2", [2])
            ffn_layer(ffn["ffn2"], "ffn2")
            for m in range(KT):
                for c in range(NC):
                    ffn_take(ffn["ffn2"], FI - 1, m, c, m * NC + c)
                if m:
                    add_square("final", m - 1)
            add_square("final", KT - 1)
            dve.wait_ge(ffn["ffn2"]["dn_ev"], FI * NC * KT + 8)

            def result(c):
                o, n = CH[c]
                for m in range(YT):
                    ins = dve.scalar_tensor_tensor(out=y[:, m, o:o + n], in0=x[:, m, o:o + n],
                                                   scalar=c_("g_final", m), in1=rstd[:, o:o + n], op0=ALU.mult,
                                                   op1=ALU.mult)
                ins.then_inc(y_done, 1)

            mean_squares("final", D)
            inverse_rms("final", then=result)


_OUTS = {
    "y": (P, KT, T), "mem_k": (P, KT, NM), "mem_v": (P, 2, D), "k_prompt": (P, WIN), "v_prompt": (P, KVH * HD),
    "k_sample": (P, NS, WIN), "v_sample": (WIN, NS, KVH * HD), "small": (P, NSM),
}


def tables():
    half = HD // 2
    inv = (10000.0 ** (-np.arange(half) / half)).astype(np.float32)
    pos = np.concatenate([np.tile(1024 + np.arange(LS), NS), np.arange(SEQ)]).astype(np.float32)
    ang = np.tile(inv, P // half)[:, None] * pos[None, :]
    rot = np.zeros((P, P), np.float32)
    for m in range(P):
        if m % HD < half:
            rot[m + half, m] = -1.0
        else:
            rot[m - half, m] = 1.0
    i, j = np.arange(WIN)[:, None], np.arange(2 * WIN)[None, :]
    band = np.where((j > i) & (j <= i + WIN), 0.0, NEG).astype(np.float32)
    even = np.concatenate([band[:, WIN:], band[:, :WIN]], axis=1)
    start = np.where(j < WIN, even, np.float32(NEG))
    masks = np.stack([start, even, band], axis=1)
    tok, key = (np.arange(P) % LS)[:, None], np.arange(WIN + LS)[None, :]
    mask_s = np.where((key > tok) & (key <= tok + WIN), 0.0, NEG).astype(np.float32)
    return {"cos": np.cos(ang).astype(np.float32), "sin": np.sin(ang).astype(np.float32), "rotm": rot,
            "ident": np.eye(P, dtype=np.float32), "masks": np.ascontiguousarray(masks), "mask_s": mask_s}


def kernel(**inputs):
    import concourse.bacc as bacc
    from concourse.bass_utils import run_bass_kernel_spmd

    a = {k: np.asarray(v) for k, v in inputs.items()}

    def per_tile(v):
        return v.reshape(-1, P).T

    def lhs_tiles(w):
        k, m = w.shape
        return w.reshape(k // P, P, m // P, P).transpose(2, 1, 0, 3)

    heads = [kv * GRP + g for g in range(GRP) for kv in range(KVH)]
    perm = np.concatenate([np.arange(h * HD, (h + 1) * HD) for h in heads])
    w_in = a["w_in"][0]
    q0 = 2 * LRU
    w_in = np.concatenate([w_in[:, :q0], w_in[:, q0:q0 + NH * HD][:, perm], w_in[:, q0 + NH * HD:]], axis=1)
    w_out = np.concatenate([a["w_out"][0][:LRU], a["w_out"][0][LRU:][perm]], axis=0)
    kv_tiles = np.stack([lhs_tiles(a[w][0]).reshape(KT // 2, 2, P, KT, P) for w in ("w_ck", "w_cv")], axis=1)
    kv_tiles = kv_tiles.reshape(2 * KT, P, KT, P)
    plain = np.concatenate([lhs_tiles(w_in), kv_tiles, lhs_tiles(w_out), lhs_tiles(a["w_cq"][0]),
                            lhs_tiles(a["w_co"][0])])
    plain = plain.reshape(PAIRS, 2, P, KT, P).transpose(1, 0, 2, 3, 4)

    def ffn_weights(n):
        return np.stack([lhs_tiles(a[f"w{n}_gate"][0]), lhs_tiles(a[f"w{n}_up"][0]),
                         a[f"w{n}_down"][0].reshape(FT, P, KT, P)], axis=1)

    tokens = np.concatenate([a["x_sample"].reshape(TS, D), a["x_prompt"][0]])

    def feature_major(v):
        return v.T.reshape(-1, P, v.shape[0]).transpose(1, 0, 2)

    bd = np.zeros((P, LT, 2, P), np.float32)
    nb = LRU // 8
    for g in range(8):
        r = slice((g % 2) * nb, (g % 2 + 1) * nb)
        bd[r, g // 2, 0, r] = a["w_a"][0, g]
        bd[r, g // 2, 1, r] = a["w_i"][0, g]
    sink = a["sink"][0]
    sink_s = np.tile(np.repeat(sink.reshape(KVH, GRP).T, LS, axis=0), (4, 2))
    parts = {
        **{g: per_tile(a[g][0]) for g in ("g_ffn1", "g_mix", "g_xattn", "g_ffn2", "g_mem", "conv_b",
                                          "b_a", "b_i", "lam")},
        "g_cat": per_tile(np.concatenate([a["g_lru_out"][0], a["g_attn_out"][0][perm]])),
        "g_final": per_tile(a["g_final"]),
        "conv_w": np.concatenate([per_tile(a["conv_w"][0, j]) for j in range(4)], axis=1),
        "sink": np.tile(sink, (P, 1)),
        "sink_s": sink_s,
        "h0": a["state_lru_h"][0].T.reshape(LT, P, NS).transpose(1, 0, 2).reshape(P, LT * NS),
        "hist": a["state_conv"][0].transpose(2, 0, 1).reshape(LT, P, NS, 3).transpose(1, 0, 2, 3)
        .reshape(P, LT * NS * 3),
    }
    host = {
        "x": feature_major(tokens),
        "cst": np.concatenate([parts[k] for k in COLS], axis=1),
        "w_ffn1": ffn_weights(1), "w_ffn2": ffn_weights(2), "w_plain": plain, "bd": bd,
        "mem": feature_major(a["mem_prompt"][0]),
        "kc": a["cache_swa_k"][0].transpose(2, 3, 0, 1).reshape(P, NS, WIN),
        "vc": a["cache_swa_v"][0].transpose(1, 0, 2, 3).reshape(WIN, NS, KVH * HD),
        "ck": a["cache_mem_k"][0].reshape(NS, NM, KT, P).transpose(0, 3, 2, 1),
        "cv": a["cache_mem_v"][0].reshape(NS, 2, P, D).transpose(0, 2, 1, 3),
        **tables(),
    }
    host = {k: np.ascontiguousarray(v) for k, v in host.items()}
    nc = bacc.Bacc("TRN2", target_bir_lowering=False, num_devices=1)
    t_in = {k: nc.dram_tensor(f"in_{k}", v.shape, F32, kind="ExternalInput").ap() for k, v in host.items()}
    t_out = {k: nc.dram_tensor(f"out_{k}", s, F32, kind="ExternalOutput").ap() for k, s in _OUTS.items()}
    build(nc, t_in, t_out)
    r = run_bass_kernel_spmd(nc, [{f"in_{k}": v for k, v in host.items()}], core_ids=[0]).results[0]
    o = {k: r[f"out_{k}"] for k in _OUTS}

    y = o["y"].transpose(2, 1, 0).reshape(T, D)
    small = o["small"]
    conv_p = small[:, SM_CP:SM_CS].reshape(P, LT, 3).transpose(2, 1, 0).reshape(1, 1, 3, LRU)
    conv_s = small[:, SM_CS:SM_HP].reshape(P, LT, NS, 3).transpose(2, 3, 1, 0).reshape(1, NS, 3, LRU)
    h_p = small[:, SM_HP:SM_HS].T.reshape(1, 1, LRU)
    h_s = small[:, SM_HS:].reshape(P, LT, NS).transpose(2, 1, 0).reshape(1, NS, LRU)
    return (
        y[TS:].reshape(1, SEQ, D), y[:TS].reshape(NS, LS, D),
        o["mem_k"].transpose(2, 1, 0).reshape(1, 1, NM, XH, XD),
        o["mem_v"].transpose(1, 0, 2).reshape(1, 1, NM, XH, XD),
        o["k_prompt"].T.reshape(1, 1, WIN, KVH, HD), o["v_prompt"].reshape(1, 1, WIN, KVH, HD),
        conv_p, h_p,
        o["k_sample"].transpose(1, 2, 0).reshape(1, NS, WIN, KVH, HD),
        o["v_sample"].transpose(1, 0, 2).reshape(1, NS, WIN, KVH, HD),
        conv_s, h_s,
    )
```
